# Optimizing a Trainium2 kernel written in Bass

```python
import math
import jax, jax.numpy as jnp
from jax import lax
import numpy as np

D_MODEL = 1024
BATCH = 1
SEQ = 256
DEPTH = 1

HEAD_DIM = 64
HEADS_DIFF = 4
HEADS_MOBA = 8
N_HEADS_TOTAL = HEADS_DIFF + HEADS_MOBA
DIFF_WIDTH = HEADS_DIFF * 2 * HEAD_DIM
MOBA_WIDTH = HEADS_MOBA * HEAD_DIM
MIX_WIDTH = DIFF_WIDTH + MOBA_WIDTH
IN_PROJ_WIDTH = 3 * MIX_WIDTH
DIFF_Q_BLOCK = 128
MOBA_BLOCK = 256
MOBA_TOPK = 3
MOBA_Q_CHUNK = 16
NUM_BUCKETS = 32
MAX_DISTANCE = 2048
N_GROUPS = 4
EXPERTS_PER_GROUP = 8
N_EXPERTS = N_GROUPS * EXPERTS_PER_GROUP
EXPERTS_PER_TOKEN = 2
EXPERT_HIDDEN = 256
DISPATCH_CHUNK = 256
RMS_EPS = 1e-6
NEG_INF = -1e30


def rms_norm(x, g):
    xf = x.astype(jnp.float32)
    y = xf * lax.rsqrt(jnp.mean(xf * xf, axis=-1, keepdims=True) + RMS_EPS)
    return (y * g.astype(jnp.float32)).astype(x.dtype)

def t5_bucket(dist):
    n = jnp.maximum(dist, 0)
    max_exact = NUM_BUCKETS // 2
    nf = jnp.maximum(n, 1).astype(jnp.float32)
    large = max_exact + (jnp.log(nf / max_exact) / math.log(MAX_DISTANCE / max_exact)
                         * (NUM_BUCKETS - max_exact)).astype(jnp.int32)
    large = jnp.minimum(large, NUM_BUCKETS - 1)
    return jnp.where(n < max_exact, n, large)

def diff_attention(q, k, v, q_g, k_g, lq1, lk1, lq2, lk2, sub_g, bias_table, lambda_init):
    B, S, H = q.shape[:3]
    q = rms_norm(q, q_g).transpose(0, 2, 3, 1, 4)
    k = rms_norm(k, k_g).transpose(0, 2, 3, 1, 4)
    v = v.transpose(0, 2, 1, 3)
    f32 = jnp.float32
    lam = (jnp.exp(jnp.sum(lq1.astype(f32) * lk1.astype(f32)))
           - jnp.exp(jnp.sum(lq2.astype(f32) * lk2.astype(f32))) + lambda_init)
    scale = HEAD_DIM ** -0.5
    kpos = jnp.arange(S)

    def block(i):
        s0 = i * DIFF_Q_BLOCK
        qb = lax.dynamic_slice_in_dim(q, s0, DIFF_Q_BLOCK, axis=3)
        logits = jnp.einsum('bhmqd,bhmkd->bhmqk', qb, k, preferred_element_type=f32) * scale
        dist = (s0 + jnp.arange(DIFF_Q_BLOCK))[:, None] - kpos[None, :]
        bias = bias_table[t5_bucket(dist)].astype(f32).transpose(2, 0, 1)
        logits = jnp.where(dist >= 0, logits + bias[None, :, None], NEG_INF)
        p = jax.nn.softmax(logits, axis=-1)
        w = p[:, :, 0] - lam * p[:, :, 1]
        return jnp.einsum('bhqk,bhkc->bhqc', w.astype(v.dtype), v)

    out = lax.map(block, jnp.arange(S // DIFF_Q_BLOCK))
    out = out.transpose(1, 0, 3, 2, 4).reshape(B, S, H, 2 * HEAD_DIM)
    out = rms_norm(out, sub_g) * (1.0 - lambda_init)
    return out.reshape(B, S, H * 2 * HEAD_DIM)

def moba_attention(q, k, v, q_g, k_g, bias_table):
    B, S, H, d = q.shape
    f32 = jnp.float32
    q = rms_norm(q, q_g).transpose(0, 2, 1, 3)
    k = rms_norm(k, k_g).transpose(0, 2, 1, 3)
    v = v.transpose(0, 2, 1, 3)
    n_kb = -(-S // MOBA_BLOCK)
    pad = n_kb * MOBA_BLOCK - S
    k_blocks = jnp.pad(k, ((0, 0), (0, 0), (0, pad), (0, 0))).reshape(B, H, n_kb, MOBA_BLOCK, d)
    v_blocks = jnp.pad(v, ((0, 0), (0, 0), (0, pad), (0, 0))).reshape(B, H, n_kb, MOBA_BLOCK, d)
    k_mean = jnp.mean(k_blocks.astype(f32), axis=3)
    top = min(MOBA_TOPK, n_kb)
    scale = HEAD_DIM ** -0.5
    bi = jnp.arange(B)[:, None, None, None]
    hi = jnp.arange(H)[None, :, None, None]
    blk_off = jnp.arange(MOBA_BLOCK)

    def chunk(i):
        s0 = i * MOBA_Q_CHUNK
        qc = lax.dynamic_slice_in_dim(q, s0, MOBA_Q_CHUNK, axis=2)
        qpos = s0 + jnp.arange(MOBA_Q_CHUNK)
        own = s0 // MOBA_BLOCK
        gate = jnp.einsum('bhqd,bhnd->bhqn', qc.astype(f32), k_mean)
        gate = jnp.where(jnp.arange(n_kb) < own, gate, NEG_INF)
        _, sel = lax.top_k(gate, top)
        sel_valid = jnp.arange(top)[:, None] < own
        k_sel = k_blocks[bi, hi, sel]
        v_sel = v_blocks[bi, hi, sel]
        sel_logits = jnp.einsum('bhqd,bhqtkd->bhqtk', qc, k_sel, preferred_element_type=f32) * scale
        sel_pos = sel[..., None] * MOBA_BLOCK + blk_off
        sel_bias = bias_table[t5_bucket(qpos[:, None, None] - sel_pos), hi[..., None]].astype(f32)
        sel_logits = jnp.where(sel_valid, sel_logits + sel_bias, NEG_INF)
        k_own = lax.dynamic_index_in_dim(k_blocks, own, axis=2, keepdims=False)
        v_own = lax.dynamic_index_in_dim(v_blocks, own, axis=2, keepdims=False)
        dist_own = qpos[:, None] - (own * MOBA_BLOCK + blk_off)[None, :]
        own_bias = bias_table[t5_bucket(dist_own)].astype(f32).transpose(2, 0, 1)[None]
        own_logits = jnp.einsum('bhqd,bhkd->bhqk', qc, k_own, preferred_element_type=f32) * scale
        own_logits = jnp.where(dist_own >= 0, own_logits + own_bias, NEG_INF)
        logits = jnp.concatenate([sel_logits.reshape(B, H, MOBA_Q_CHUNK, top * MOBA_BLOCK), own_logits], axis=-1)
        p = jax.nn.softmax(logits, axis=-1).astype(v.dtype)
        p_sel = p[..., :top * MOBA_BLOCK].reshape(B, H, MOBA_Q_CHUNK, top, MOBA_BLOCK)
        p_own = p[..., top * MOBA_BLOCK:]
        return (jnp.einsum('bhqtk,bhqtkd->bhqd', p_sel, v_sel)
                + jnp.einsum('bhqk,bhkd->bhqd', p_own, v_own))

    out = lax.map(chunk, jnp.arange(S // MOBA_Q_CHUNK))
    return out.transpose(1, 0, 3, 2, 4).reshape(B, S, H * d)

def hier_moe(h, router_group, router_expert, w_gate, w_up, w_down):
    B, S, D = h.shape
    N = B * S
    t = h.reshape(N, D)
    f32 = jnp.float32
    g_logits = (t @ router_group).astype(f32)
    g_prob = jax.nn.softmax(g_logits, axis=-1)
    g = jnp.argmax(g_logits, axis=-1)
    p_group = jnp.take_along_axis(g_prob, g[:, None], axis=-1)
    e_logits_all = jnp.einsum('nd,gde->nge', t, router_expert).astype(f32)
    e_logits = jnp.take_along_axis(e_logits_all, g[:, None, None], axis=1)[:, 0]
    top_v, top_e = lax.top_k(e_logits, EXPERTS_PER_TOKEN)
    weight = p_group * jax.nn.softmax(top_v, axis=-1)
    expert_id = g[:, None] * EXPERTS_PER_GROUP + top_e
    A = N * EXPERTS_PER_TOKEN
    C = DISPATCH_CHUNK
    eid = expert_id.reshape(A)
    tok = jnp.repeat(jnp.arange(N, dtype=jnp.int32), EXPERTS_PER_TOKEN)
    w_flat = weight.reshape(A)
    order = jnp.argsort(eid)
    eid_s, tok_s, w_s = eid[order], tok[order], w_flat[order]
    counts = jax.ops.segment_sum(jnp.ones((A,), jnp.int32), eid, num_segments=N_EXPERTS)
    start = jnp.cumsum(counts) - counts
    pad_counts = ((counts + C - 1) // C) * C
    pad_end = jnp.cumsum(pad_counts)
    pad_start = pad_end - pad_counts
    dest = pad_start[eid_s] + (jnp.arange(A, dtype=jnp.int32) - start[eid_s])
    P = A + N_EXPERTS * C
    n_chunks = P // C
    slot_tok = jnp.zeros((P,), jnp.int32).at[dest].set(tok_s)
    slot_w = jnp.zeros((P,), f32).at[dest].set(w_s)
    chunk_e = jnp.minimum(jnp.searchsorted(pad_end, jnp.arange(n_chunks) * C, side='right'), N_EXPERTS - 1)

    def run(args):
        e, toks = args
        xc = t[toks]
        hid = jax.nn.silu(xc @ w_gate[e]) * (xc @ w_up[e])
        return hid @ w_down[e]

    out = lax.map(run, (chunk_e, slot_tok.reshape(n_chunks, C))).reshape(P, D)
    y = jnp.zeros((N, D), t.dtype).at[slot_tok].add((out * slot_w[:, None]).astype(t.dtype))
    return y.reshape(B, S, D)

def first_inputs(seed: int = 0) -> dict:
    key = jax.random.key(seed)
    ks = jax.random.split(key, 20)
    f32 = jnp.float32

    def nrm(k, shape, scale):
        return jax.random.normal(k, shape, f32) * scale

    def gain(k, shape):
        return 1.0 + 0.05 * jax.random.normal(k, shape, f32)

    return {
        'x': nrm(ks[0], (BATCH, SEQ, D_MODEL), 1.0),
        'norm1_g': gain(ks[1], (DEPTH, D_MODEL)),
        'w_in': nrm(ks[2], (DEPTH, D_MODEL, IN_PROJ_WIDTH), D_MODEL ** -0.5),
        'diff_q_g': gain(ks[3], (DEPTH, HEAD_DIM)),
        'diff_k_g': gain(ks[4], (DEPTH, HEAD_DIM)),
        'lambda_q1': nrm(ks[5], (DEPTH, HEAD_DIM), 0.1),
        'lambda_k1': nrm(ks[6], (DEPTH, HEAD_DIM), 0.1),
        'lambda_q2': nrm(ks[7], (DEPTH, HEAD_DIM), 0.1),
        'lambda_k2': nrm(ks[8], (DEPTH, HEAD_DIM), 0.1),
        'diff_sub_g': gain(ks[9], (DEPTH, 2 * HEAD_DIM)),
        'moba_q_g': gain(ks[10], (DEPTH, HEAD_DIM)),
        'moba_k_g': gain(ks[11], (DEPTH, HEAD_DIM)),
        'rel_bias': nrm(ks[12], (NUM_BUCKETS, N_HEADS_TOTAL), 0.5),
        'w_out': nrm(ks[13], (DEPTH, MIX_WIDTH, D_MODEL), MIX_WIDTH ** -0.5),
        'norm2_g': gain(ks[14], (DEPTH, D_MODEL)),
        'router_group': nrm(ks[15], (DEPTH, D_MODEL, N_GROUPS), D_MODEL ** -0.5),
        'router_expert': nrm(ks[16], (DEPTH, N_GROUPS, D_MODEL, EXPERTS_PER_GROUP), D_MODEL ** -0.5),
        'w_gate': nrm(ks[17], (DEPTH, N_EXPERTS, D_MODEL, EXPERT_HIDDEN), D_MODEL ** -0.5),
        'w_up': nrm(ks[18], (DEPTH, N_EXPERTS, D_MODEL, EXPERT_HIDDEN), D_MODEL ** -0.5),
        'w_down': nrm(ks[19], (DEPTH, N_EXPERTS, EXPERT_HIDDEN, D_MODEL), EXPERT_HIDDEN ** -0.5),
    }

def first_block(x, norm1_g, w_in, diff_q_g, diff_k_g, lambda_q1, lambda_k1, lambda_q2, lambda_k2,
              diff_sub_g, moba_q_g, moba_k_g, rel_bias, w_out, norm2_g, router_group,
              router_expert, w_gate, w_up, w_down):
    B, S, _ = x.shape
    bias_diff = rel_bias[:, :HEADS_DIFF]
    bias_moba = rel_bias[:, HEADS_DIFF:]
    splits = [DIFF_WIDTH, 2 * DIFF_WIDTH, 3 * DIFF_WIDTH,
              3 * DIFF_WIDTH + MOBA_WIDTH, 3 * DIFF_WIDTH + 2 * MOBA_WIDTH]
    for layer in range(DEPTH):
        lambda_init = 0.8 - 0.6 * math.exp(-0.3 * layer)
        h = rms_norm(x, norm1_g[layer])
        proj = h @ w_in[layer]
        q_d, k_d, v_d, q_m, k_m, v_m = jnp.split(proj, splits, axis=-1)
        y_d = diff_attention(q_d.reshape(B, S, HEADS_DIFF, 2, HEAD_DIM),
                             k_d.reshape(B, S, HEADS_DIFF, 2, HEAD_DIM),
                             v_d.reshape(B, S, HEADS_DIFF, 2 * HEAD_DIM),
                             diff_q_g[layer], diff_k_g[layer], lambda_q1[layer], lambda_k1[layer],
                             lambda_q2[layer], lambda_k2[layer], diff_sub_g[layer], bias_diff, lambda_init)
        y_m = moba_attention(q_m.reshape(B, S, HEADS_MOBA, HEAD_DIM),
                             k_m.reshape(B, S, HEADS_MOBA, HEAD_DIM),
                             v_m.reshape(B, S, HEADS_MOBA, HEAD_DIM),
                             moba_q_g[layer], moba_k_g[layer], bias_moba)
        x = x + jnp.concatenate([y_d, y_m], axis=-1) @ w_out[layer]
        x = x + hier_moe(rms_norm(x, norm2_g[layer]), router_group[layer], router_expert[layer],
                         w_gate[layer], w_up[layer], w_down[layer])
    return x


ATTN_HEAD_DIM = 64
ATTN_HEADS = D_MODEL // ATTN_HEAD_DIM
ATTN_KV_HEADS = ATTN_HEADS // 4
ATTN_GROUP = ATTN_HEADS // ATTN_KV_HEADS
WINDOW = 128

MLSTM_HEADS = 8
MLSTM_V_DIM = D_MODEL // MLSTM_HEADS
MLSTM_QK_DIM = MLSTM_V_DIM // 2
MLSTM_CHUNK = 64
CONV_WIDTH = 4
GATE_SOFTCAP = 15.0

D_FF = ((8 * D_MODEL // 3 + 127) // 128) * 128
FFN_RESIDUAL_WEIGHT = 0.5
NORM_EPS = 1e-6

SZ_AQ = ATTN_HEADS * ATTN_HEAD_DIM
SZ_AK = ATTN_KV_HEADS * ATTN_HEAD_DIM
SZ_AV = ATTN_KV_HEADS * ATTN_HEAD_DIM
SZ_MQ = MLSTM_HEADS * MLSTM_QK_DIM
SZ_MK = MLSTM_HEADS * MLSTM_QK_DIM
SZ_MV = MLSTM_HEADS * MLSTM_V_DIM
SZ_MO = MLSTM_HEADS * MLSTM_V_DIM
SZ_MI = MLSTM_HEADS
SZ_MF = MLSTM_HEADS
SZ_GATES = 2 * D_MODEL
SPLIT_POINTS = (
    SZ_AQ,
    SZ_AQ + SZ_AK,
    SZ_AQ + SZ_AK + SZ_AV,
    SZ_AQ + SZ_AK + SZ_AV + SZ_MQ,
    SZ_AQ + SZ_AK + SZ_AV + SZ_MQ + SZ_MK,
    SZ_AQ + SZ_AK + SZ_AV + SZ_MQ + SZ_MK + SZ_MV,
    SZ_AQ + SZ_AK + SZ_AV + SZ_MQ + SZ_MK + SZ_MV + SZ_MO,
    SZ_AQ + SZ_AK + SZ_AV + SZ_MQ + SZ_MK + SZ_MV + SZ_MO + SZ_MI,
    SZ_AQ + SZ_AK + SZ_AV + SZ_MQ + SZ_MK + SZ_MV + SZ_MO + SZ_MI + SZ_MF,
)
F_OFFSET = SPLIT_POINTS[7]
IN_WIDTH = SPLIT_POINTS[8] + SZ_GATES


def rms_norm_2(x, g):
    xf = x.astype(jnp.float32)
    y = xf * lax.rsqrt(jnp.mean(xf * xf, axis=-1, keepdims=True) + NORM_EPS)
    return (y * g.astype(jnp.float32)).astype(x.dtype)

def swiglu(x, w_gate, w_up, w_down):
    return (jax.nn.silu(x @ w_gate) * (x @ w_up)) @ w_down

def causal_depthwise_conv(x, w):
    s = x.shape[1]
    xp = jnp.pad(x, ((0, 0), (CONV_WIDTH - 1, 0), (0, 0)))
    out = xp[:, 0:s] * w[0]
    for j in range(1, CONV_WIDTH):
        out = out + xp[:, j:j + s] * w[j]
    return out

def sliding_window_attention(q, k, v, sinks):
    b, s = q.shape[0], q.shape[1]
    nb = s // WINDOW
    qb = q.reshape(b, nb, WINDOW, ATTN_KV_HEADS, ATTN_GROUP, ATTN_HEAD_DIM)

    def band(t):
        tp = jnp.pad(t, ((0, 0), (WINDOW, 0), (0, 0), (0, 0)))
        tp = tp.reshape(b, nb + 1, WINDOW, ATTN_KV_HEADS, ATTN_HEAD_DIM)
        return jnp.concatenate([tp[:, :-1], tp[:, 1:]], axis=2)

    kb, vb = band(k), band(v)
    scale = ATTN_HEAD_DIM ** -0.5
    scores = jnp.einsum('bnqhgd,bnkhd->bhgnqk', qb, kb).astype(jnp.float32) * scale
    qi = jnp.arange(WINDOW)[:, None]
    kj = jnp.arange(2 * WINDOW)[None, :]
    in_window = (kj > qi) & (kj <= qi + WINDOW)
    is_pad = (jnp.arange(nb)[:, None, None] == 0) & (kj < WINDOW)[None]
    valid = in_window[None] & ~is_pad
    scores = jnp.where(valid, scores, -jnp.inf)
    sink = jnp.broadcast_to(
        sinks.astype(jnp.float32).reshape(ATTN_KV_HEADS, ATTN_GROUP)[None, :, :, None, None, None],
        scores.shape[:-1] + (1,))
    probs = jax.nn.softmax(jnp.concatenate([scores, sink], axis=-1), axis=-1)[..., :-1]
    out = jnp.einsum('bhgnqk,bnkhd->bnqhgd', probs.astype(v.dtype), vb)
    return out.reshape(b, s, ATTN_HEADS * ATTN_HEAD_DIM)

def mlstm_chunkwise(q, k, v, i_pre, f_pre):
    b, s = q.shape[0], q.shape[1]
    nc = s // MLSTM_CHUNK
    f32 = jnp.float32

    def to_chunks(t):
        return t.astype(f32).reshape(b, nc, MLSTM_CHUNK, MLSTM_HEADS, t.shape[-1]).transpose(1, 0, 3, 2, 4)

    def gate_chunks(t):
        return t.astype(f32).reshape(b, nc, MLSTM_CHUNK, MLSTM_HEADS).transpose(1, 0, 3, 2)

    qc, kc, vc = to_chunks(q), to_chunks(k), to_chunks(v)
    ic = gate_chunks(i_pre)
    lfc = jax.nn.log_sigmoid(gate_chunks(f_pre))
    causal = jnp.tril(jnp.ones((MLSTM_CHUNK, MLSTM_CHUNK), dtype=bool))

    def step(carry, inp):
        c_prev, n_prev, m_prev = carry
        q_, k_, v_, i_, lf_ = inp
        cum = jnp.cumsum(lf_, axis=-1)
        logw = cum[..., :, None] - cum[..., None, :] + i_[..., None, :]
        logw = jnp.where(causal, logw, -jnp.inf)
        log_inter = cum + m_prev[..., None]
        m_t = jnp.maximum(log_inter, jnp.max(logw, axis=-1))
        w_intra = jnp.exp(logw - m_t[..., None])
        w_inter = jnp.exp(log_inter - m_t)
        sc = jnp.einsum('bhtd,bhsd->bhts', q_, k_) * w_intra
        num = jnp.einsum('bhts,bhsv->bhtv', sc, v_) + w_inter[..., None] * jnp.einsum('bhtd,bhdv->bhtv', q_, c_prev)
        den = jnp.sum(sc, axis=-1) + w_inter * jnp.einsum('bhtd,bhd->bht', q_, n_prev)
        h = num / jnp.maximum(jnp.abs(den), jnp.exp(-m_t))[..., None]
        total = cum[..., -1]
        log_k = total[..., None] - cum + i_
        m_new = jnp.maximum(total + m_prev, jnp.max(log_k, axis=-1))
        wk = jnp.exp(log_k - m_new[..., None])
        decay = jnp.exp(total + m_prev - m_new)
        c_new = decay[..., None, None] * c_prev + jnp.einsum('bhs,bhsd,bhsv->bhdv', wk, k_, v_)
        n_new = decay[..., None] * n_prev + jnp.einsum('bhs,bhsd->bhd', wk, k_)
        return (c_new, n_new, m_new), h

    init = (jnp.zeros((b, MLSTM_HEADS, MLSTM_QK_DIM, MLSTM_V_DIM), f32),
            jnp.zeros((b, MLSTM_HEADS, MLSTM_QK_DIM), f32),
            jnp.zeros((b, MLSTM_HEADS), f32))
    _, hs = lax.scan(step, init, (qc, kc, vc, ic, lfc))
    return hs.transpose(1, 0, 3, 2, 4).reshape(b, s, MLSTM_HEADS, MLSTM_V_DIM)

def softcap(t):
    return GATE_SOFTCAP * jnp.tanh(t / GATE_SOFTCAP)

def second_inputs(seed: int = 0) -> dict:
    key = jax.random.key(seed)
    ks = jax.random.split(key, 24)
    f32 = jnp.float32

    def dense(k, fan_in, fan_out):
        return jax.random.normal(k, (DEPTH, fan_in, fan_out), f32) * fan_in ** -0.5

    def gain(k, shape):
        return 1.0 + 0.05 * jax.random.normal(k, shape, f32)

    b_in = 0.02 * jax.random.normal(ks[7], (DEPTH, IN_WIDTH), f32)
    f_bias = jnp.linspace(3.0, 6.0, MLSTM_HEADS, dtype=f32)
    b_in = b_in.at[:, F_OFFSET:F_OFFSET + SZ_MF].add(f_bias)
    return {
        "x": jax.random.normal(ks[0], (BATCH, SEQ, D_MODEL), f32),
        "ffn1_norm": gain(ks[1], (DEPTH, D_MODEL)),
        "ffn1_w_gate": dense(ks[2], D_MODEL, D_FF),
        "ffn1_w_up": dense(ks[3], D_MODEL, D_FF),
        "ffn1_w_down": dense(ks[4], D_FF, D_MODEL),
        "mix_norm": gain(ks[5], (DEPTH, D_MODEL)),
        "w_in": dense(ks[6], D_MODEL, IN_WIDTH),
        "b_in": b_in,
        "attn_sinks": 0.5 * jax.random.normal(ks[8], (DEPTH, ATTN_HEADS), f32),
        "mlstm_conv": jax.random.normal(ks[9], (DEPTH, CONV_WIDTH, SZ_MQ + SZ_MK), f32) * CONV_WIDTH ** -0.5,
        "mlstm_head_norm": gain(ks[10], (DEPTH, MLSTM_HEADS, MLSTM_V_DIM)),
        "w_proj_attn": dense(ks[11], SZ_AQ, D_MODEL),
        "w_proj_mlstm": dense(ks[12], SZ_MV, D_MODEL),
        "w_out": dense(ks[13], D_MODEL, D_MODEL),
        "ffn2_norm": gain(ks[14], (DEPTH, D_MODEL)),
        "ffn2_w_gate": dense(ks[15], D_MODEL, D_FF),
        "ffn2_w_up": dense(ks[16], D_MODEL, D_FF),
        "ffn2_w_down": dense(ks[17], D_FF, D_MODEL),
        "final_norm": gain(ks[18], (D_MODEL,)),
    }

def second_block(x, ffn1_norm, ffn1_w_gate, ffn1_w_up, ffn1_w_down, mix_norm, w_in, b_in,
              attn_sinks, mlstm_conv, mlstm_head_norm, w_proj_attn, w_proj_mlstm, w_out,
              ffn2_norm, ffn2_w_gate, ffn2_w_up, ffn2_w_down, final_norm):
    b, s, _ = x.shape
    for l in range(DEPTH):
        h = rms_norm_2(x, ffn1_norm[l])
        x = x + FFN_RESIDUAL_WEIGHT * swiglu(h, ffn1_w_gate[l], ffn1_w_up[l], ffn1_w_down[l])

        h = rms_norm_2(x, mix_norm[l])
        z = h @ w_in[l] + b_in[l]
        a_q, a_k, a_v, m_q, m_k, m_v, m_o, m_i, m_f, g_pre = jnp.split(z, SPLIT_POINTS, axis=-1)

        y_attn = sliding_window_attention(
            a_q.reshape(b, s, ATTN_HEADS, ATTN_HEAD_DIM),
            a_k.reshape(b, s, ATTN_KV_HEADS, ATTN_HEAD_DIM),
            a_v.reshape(b, s, ATTN_KV_HEADS, ATTN_HEAD_DIM),
            attn_sinks[l]) @ w_proj_attn[l]

        qk = jax.nn.silu(causal_depthwise_conv(jnp.concatenate([m_q, m_k], axis=-1), mlstm_conv[l]))
        mq = qk[..., :SZ_MQ].reshape(b, s, MLSTM_HEADS, MLSTM_QK_DIM)
        mk = qk[..., SZ_MQ:].reshape(b, s, MLSTM_HEADS, MLSTM_QK_DIM) * MLSTM_QK_DIM ** -0.5
        mv = m_v.reshape(b, s, MLSTM_HEADS, MLSTM_V_DIM)
        hm = mlstm_chunkwise(mq, mk, mv,
                             softcap(m_i.astype(jnp.float32)), softcap(m_f.astype(jnp.float32)))
        hm = rms_norm_2(hm, mlstm_head_norm[l]).reshape(b, s, SZ_MV)
        hm = (jax.nn.sigmoid(m_o.astype(jnp.float32)) * hm).astype(x.dtype)
        y_mlstm = hm @ w_proj_mlstm[l]

        gates = jax.nn.sigmoid(g_pre.astype(jnp.float32)).astype(x.dtype).reshape(b, s, 2, D_MODEL)
        merged = gates[:, :, 0] * y_attn + gates[:, :, 1] * y_mlstm
        x = x + merged @ w_out[l]

        h = rms_norm_2(x, ffn2_norm[l])
        x = x + FFN_RESIDUAL_WEIGHT * swiglu(h, ffn2_w_gate[l], ffn2_w_up[l], ffn2_w_down[l])
    return rms_norm_2(x, final_norm)


def setup_inputs(seed=0):
    out = dict(first_inputs(seed))
    for name, value in second_inputs(seed + 1).items():
        if name != "x":
            out[name + "_2"] = value
    return out


def reference(
    x, norm1_g, w_in, diff_q_g, diff_k_g, lambda_q1, lambda_k1, lambda_q2, lambda_k2,
    diff_sub_g, moba_q_g, moba_k_g, rel_bias, w_out, norm2_g, router_group, router_expert,
    w_gate, w_up, w_down, ffn1_norm_2, ffn1_w_gate_2, ffn1_w_up_2, ffn1_w_down_2, mix_norm_2,
    w_in_2, b_in_2, attn_sinks_2, mlstm_conv_2, mlstm_head_norm_2, w_proj_attn_2,
    w_proj_mlstm_2, w_out_2, ffn2_norm_2, ffn2_w_gate_2, ffn2_w_up_2, ffn2_w_down_2,
    final_norm_2,
):
    x = first_block(
        x, norm1_g, w_in, diff_q_g, diff_k_g, lambda_q1, lambda_k1, lambda_q2, lambda_k2,
        diff_sub_g, moba_q_g, moba_k_g, rel_bias, w_out, norm2_g, router_group, router_expert,
        w_gate, w_up, w_down,
    )
    return second_block(
        x, ffn1_norm_2, ffn1_w_gate_2, ffn1_w_up_2, ffn1_w_down_2, mix_norm_2, w_in_2, b_in_2,
        attn_sinks_2, mlstm_conv_2, mlstm_head_norm_2, w_proj_attn_2, w_proj_mlstm_2, w_out_2,
        ffn2_norm_2, ffn2_w_gate_2, ffn2_w_up_2, ffn2_w_down_2, final_norm_2,
    )


_drawn_inputs = setup_inputs


def setup_inputs(seed=0):
    import zlib

    import numpy as np

    out = dict(_drawn_inputs(seed))
    spreads = {}
    factors = {'lambda_q1': 35.519,
     'moba_q_g': 3.325,
     'moba_k_g': 3.103,
     'ffn1_norm_2': 2.984,
     'attn_sinks_2': 32.746,
     'mlstm_head_norm_2': 4.756,
     'ffn2_norm_2': 3.429}
    for name, (base, spread) in spreads.items():
        noise = np.random.default_rng([zlib.crc32(name.encode()), seed]).standard_normal(out[name].shape)
        drawn = base * np.exp(spread * noise) if base else spread * noise
        out[name] = __import__('jax').numpy.asarray(drawn.astype(out[name].dtype))
    for name, factor in factors.items():
        out[name] = (out[name] * factor).astype(out[name].dtype)
    return out
```

```python
from contextlib import ExitStack

import numpy as np

import concourse.bass as bass
from concourse import mybir

F32 = mybir.dt.float32
U32 = mybir.dt.uint32
I32 = mybir.dt.int32
ALU = mybir.AluOpType
ACT = mybir.ActivationFunctionType
AX_X = mybir.AxisListType.X

P = 128
SEQ = 256
TILES = SEQ // P
D = 1024
KT = D // P
HALF = 512
HALVES = D // HALF
HEAD = 64
EPS = 1e-6
MASKED = -1e30
SCALE = HEAD ** -0.5

DIFF_HEADS, MOBA_HEADS = 4, 8
MAPS = 2 * DIFF_HEADS + MOBA_HEADS
N_BIAS = DIFF_HEADS + MOBA_HEADS
BUCKETS, MAX_DISTANCE = 32, 2048
DIST_COLS = 384
LAMBDA_INIT = 0.8 - 0.6 * float(np.exp(-0.3 * 0))

GROUPS, PER_GROUP = 4, 8
EXPERTS = GROUPS * PER_GROUP
HIDDEN = 256
FT = HIDDEN // P
SLOTS = 64
ROUNDS = SEQ // SLOTS
PAIRS = EXPERTS // 2
ROUTES = GROUPS + EXPERTS

D_FF = ((8 * D // 3 + 127) // 128) * 128
CHUNKS = D_FF // HIDDEN
KV_HEADS, Q_HEADS = 4, 16
MLSTM_HEADS, V_DIM = 8, 128
SOFTCAP = 15.0
C_K, C_AV, C_MQ, C_MV, C_MO, C_IF, C_G, C_END = 1024, 1280, 1536, 2560, 3584, 4608, 4624, 6672

CONV = 4
V_BQ, V_BK, V_BM, V_CONV, V_QK, V_SUB, V_ROWS = 0, 8, 10, 18, 50, 54, 55
N_VEC = 4 + 1 + 1 + CONV + 8 + 1

RING = 4
PIECE = KT * HIDDEN
SLOT_DMAS = {"cols": 1, "expert": 3, "chunk": 3}


def weight_groups():
    g = [("cols", "w_in", c) for c in range(6)]
    g += [("cols", "w_out", c) for c in range(2)]
    g += [("expert", "moe", e) for e in range(EXPERTS)]
    g += [("chunk", "ffn1", c) for c in range(CHUNKS)]
    g += [("cols", "w_in_2", c) for c in range(13)]
    g += [("cols", w, c) for w in ("w_proj_attn", "w_proj_mlstm", "w_out_2") for c in range(2)]
    g += [("chunk", "ffn2", c) for c in range(CHUNKS)]
    return g


def distance_buckets():
    out = np.zeros((BUCKETS + 1, DIST_COLS), np.float32)
    exact = BUCKETS // 2
    for m in range(DIST_COLS):
        n = SEQ - 1 - m
        if n < 0:
            out[BUCKETS, m] = 1
        elif n < exact:
            out[n, m] = 1
        else:
            large = np.log(np.float32(n) / np.float32(exact)) / np.log(MAX_DISTANCE / exact) * (BUCKETS - exact)
            out[min(exact + int(large), BUCKETS - 1), m] = 1
    return out


def two_blocks(nc, A, buckets, out):
    GROUP = weight_groups()
    first = {}
    for n, (_, src, _) in enumerate(GROUP):
        first.setdefault(src, n)
    loaded_at, total = [], [0] * RING
    for n, (kind, _, _) in enumerate(GROUP):
        total[n % RING] += 16 * SLOT_DMAS[kind]
        loaded_at.append(total[n % RING])

    with ExitStack() as ctx:
        def sb(name, shape, dt=F32):
            return ctx.enter_context(nc.sbuf_tensor(name, shape, dt))

        def sem(name):
            return ctx.enter_context(nc.semaphore(name))

        PS = ctx.enter_context(nc.psum_tensor("banks", [P, 8, HALF], F32))

        bias_rows = nc.dram_tensor("bias_rows", [N_BIAS, P, DIST_COLS], F32, kind="Internal").ap()
        tokens = nc.dram_tensor("tokens", [SEQ, D], F32, kind="Internal").ap()
        expert_rows = nc.dram_tensor("expert_rows", [EXPERTS * SLOTS, D], F32, kind="Internal").ap()

        ring = [sb(f"weights{s}", [P, 3 * PIECE]) for s in range(RING)]
        res = sb("residual", [P, TILES, D])
        tok = sb("token_major", [P, TILES, D])
        hT = sb("normed_T", [P, KT, SEQ])
        yT = sb("mixed_T", [P, KT, SEQ])
        LP = sb("logits_and_T", [P, 2 * 16 * SEQ])
        L = LP[:, 0:16 * SEQ].rearrange("p (a k) -> p a k", a=16)
        PT = LP[:, 16 * SEQ:].rearrange("p (b q) -> p b q", q=P)
        AR = sb("stage", [P, 9216])

        def view(lo, *dims):
            n = int(np.prod(dims))
            names = " ".join("abc"[:len(dims)])
            return AR[:, lo:lo + n].rearrange(f"p ({names}) -> p {names}", **dict(zip("abc", dims)))

        qkT = [view(1024 * n, 4, SEQ) for n in range(4)]
        vals = view(4096, TILES, D)
        bias = view(6144, N_BIAS, SEQ)
        bias_stage = LP[:, 0:N_BIAS * DIST_COLS].rearrange("p (h m) -> p h m", h=N_BIAS)
        relb = AR[0:BUCKETS + 1, 0:N_BIAS * P].rearrange("p (h q) -> p h q", h=N_BIAS)
        onehot = AR[0:BUCKETS + 1, 1536:1536 + DIST_COLS]
        lam_rows = view(2048, 4, HEAD)
        xg, xgT = view(0, 2, D), view(2048, 2, KT, P)
        exo = view(4096, 2, D)
        act_e, hid_e, hidT_e = view(6144, 2, HIDDEN), view(6656, 2, HIDDEN), view(7168, 2, FT, P)
        select = LP[:, 0:TILES * EXPERTS * SLOTS].rearrange("p (t e c) -> p t e c", t=TILES, e=EXPERTS)
        routed = LP[:, 4096:8192].rearrange("p (n d) -> p n d", n=4)
        act_f, hid_f, hidT_f = view(0, 2, TILES, HIDDEN), view(1024, 2, TILES, HIDDEN), view(2048, 2, FT, SEQ)
        sqT, skT = view(0, 8, SEQ), view(2048, 2, SEQ)
        sv = view(2560, TILES, 256)
        mv, mo = view(3072, TILES, D), view(5120, TILES, D)
        mqk = view(7168, 8, SEQ)
        hmT = view(0, KT, SEQ)
        conv = yT[:, 0:2, :]
        raw = yT[:, 2:5, :].rearrange("p a b -> p (a b)")[:, 0:2 * (SEQ + CONV)].rearrange("p (a b) -> p a b", a=2)[:, :, 1:]
        gates = LP[:, 0:4096].rearrange("p (t g) -> p t g", t=TILES)
        bias_av, bias_mvo = LP[:, 0:256], LP[:, 256:2304]
        bias_g = LP[:, 4096:6144]

        gain = sb("gain_rows", [P, D])
        ident = sb("ident", [P, P])
        ones = sb("ones", [P, P])
        upto = sb("upto", [P, P])
        before = sb("before", [P, P])
        masks = sb("masks", [P, 4 * P])
        zero_causal, prev_causal = masks[:, 0:256], masks[:, 256:512]
        vec_rows = sb("vec_rows", [V_ROWS, P])
        vec = sb("vec", [P, V_ROWS])
        relx = sb("rel_bias", [BUCKETS + 1, N_BIAS])
        lam = sb("lambda_parts", [P, 6])
        router = sb("router", [P, KT, ROUTES])
        w_if, b_if = sb("w_if", [P, KT, 16]), sb("b_if", [P, 16])
        sink_nat, sink = sb("sink_natural", [P, Q_HEADS]), sb("sink", [P, Q_HEADS])
        iota_i, iota = sb("iota_int", [P, SLOTS], I32), sb("iota", [P, SLOTS])
        minus_half = sb("minus_half", [P, 8])
        token_i, token_id = sb("token_int", [P, TILES], I32), sb("token_id", [P, TILES])
        ss = sb("square_sums", [P, 16])
        rstd = sb("rstd", [P, 16])
        hs = sb("head_stats", [P, 8, 16])
        rt = sb("route_stats", [P, TILES, 96])
        rt8 = sb("route_top", [P, TILES, 4, 8])
        rt8u = sb("route_top_index", [P, TILES, 2, 8], U32)
        assign = sb("assign", [P, TILES, 3, EXPERTS])
        posn = sb("position", [P, TILES, 3, EXPERTS])
        row_u = sb("row_index", [P, TILES * 2], U32)
        slot_tok = sb("slot_token", [P, PAIRS], U32)
        most_f, most = sb("most_tokens_f", [P, 1]), sb("most_tokens", [P, 1], U32)
        ga = sb("gate_stats", [P, TILES, 8, 16])
        aT = sb("a_rows", [MLSTM_HEADS, SEQ])

        slot_loaded = [sem(f"slot_loaded{s}") for s in range(RING)]
        weights_used = sem("weights_used")
        x_loaded, vec_loaded, lam_loaded = sem("x_loaded"), sem("vec_loaded"), sem("lam_loaded")
        rel_loaded, router_loaded, if_loaded = sem("rel_loaded"), sem("router_loaded"), sem("if_loaded")
        gain_loaded, bias_loaded, bb_loaded = sem("gain_loaded"), sem("bias_loaded"), sem("bb_loaded")
        bias_stored, tokens_stored = sem("bias_stored"), sem("tokens_stored")
        out_stored = sem("out_stored")
        pool_seq, dve_seq, act_seq = sem("pool_seq"), sem("dve_seq"), sem("act_seq")
        consts, root_in, root_out = sem("consts"), sem("root_in"), sem("root_out")
        vec_T, vec_ready, rel_wide = sem("vec_T"), sem("vec_ready"), sem("rel_wide")
        bias_ps, bias_copied = sem("bias_ps"), sem("bias_copied")
        squared, normed = sem("squared"), sem("normed")
        t8_a, t8_d, t8c_a, t8c_d = sem("t8_a"), sem("t8_d"), sem("t8c_a"), sem("t8c_d")
        proj, proj_sq, proj_used = sem("proj"), sem("proj_sq"), sem("proj_used")
        proj_sq_read = sem("proj_sq_read")
        qk_ps, qk_done = sem("qk_ps"), sem("qk_done")
        score, score_used, maxed, expd = sem("score"), sem("score_used"), sem("maxed"), sem("expd")
        lam_sum, lam_exp = sem("lam_sum"), sem("lam_exp")
        weighted = sem("weighted")
        pT_ps, pT_a, pT_d = sem("pT_ps"), sem("pT_a"), sem("pT_d")
        pv, pv_sq, mixed = sem("pv"), sem("pv_sq"), sem("mixed")
        gemm, gemm_used = sem("gemm"), sem("gemm_used")
        route, route_exp_in, route_exp, assigned = sem("route"), sem("route_exp_in"), sem("route_exp"), sem("assigned")
        pos_ps, selected, slot_ps, slot_ready, rows_ready = (
            sem("pos_ps"), sem("selected"), sem("slot_ps"), sem("slot_ready"), sem("rows_ready"))
        gathered = [sem(f"gathered{b}") for b in range(2)]
        exT_a, exT_d, exTc_a, exTc_d = sem("exT_a"), sem("exT_d"), sem("exTc_a"), sem("exTc_d")
        ex_gu, ex_act, ex_hid = sem("ex_gu"), sem("ex_act"), sem("ex_hid")
        ex_hT, ex_hTc, ex_out_a, ex_out_d = sem("ex_hT"), sem("ex_hTc"), sem("ex_out_a"), sem("ex_out_d")
        ex_stored = [sem(f"ex_stored{b}") for b in range(2)]
        row_gathered = [sem(f"row_gathered{n}") for n in range(4)]
        moe_added = sem("moe_added")
        counted = sem("counted")
        ov_sel, ov_slot_ps, ov_slot, ov_gathered, ov_loaded = (
            sem("ov_sel"), sem("ov_slot_ps"), sem("ov_slot"), sem("ov_gathered"), sem("ov_loaded"))
        ov_xT, ov_xTc, ov_gu, ov_act, ov_hid, ov_hT, ov_hTc = (
            sem("ov_xT"), sem("ov_xTc"), sem("ov_gu"), sem("ov_act"), sem("ov_hid"), sem("ov_hT"), sem("ov_hTc"))
        ov_down, ov_out, ov_stored, ov_rows, ov_routed = (
            sem("ov_down"), sem("ov_out"), sem("ov_stored"), sem("ov_rows"), sem("ov_routed"))
        ov_step, ov_added = sem("ov_step"), sem("ov_added")
        OV_STEPS = TILES * (1 + 7)
        ff_gu, ff_act, ff_hid, ff_hT, ff_hTc, ff_added = (
            sem("ff_gu"), sem("ff_act"), sem("ff_hid"), sem("ff_hT"), sem("ff_hTc"), sem("ff_added"))
        z_unit, z_act, z_dve = sem("z_unit"), sem("z_act"), sem("z_dve")
        conv_done, conv_silu, pad_zeroed = sem("conv_done"), sem("conv_silu"), sem("pad_zeroed")
        gates_exp, gates_u, gates_ready = sem("gates_exp"), sem("gates_u"), sem("gates_ready")
        cum_ps, a_ready, a_ps, a_copied = sem("cum_ps"), sem("a_ready"), sem("a_ps"), sem("a_copied")
        sink_exp, sig_done = sem("sink_exp"), sem("sig_done")
        ml_a, ml_used, ml_max, ml_exp, ml_s, ml_sc = (
            sem("ml_a"), sem("ml_used"), sem("ml_max"), sem("ml_exp"), sem("ml_s"), sem("ml_sc"))
        ml_h, ml_hsq = sem("ml_h"), sem("ml_hsq")
        g_sig, merged = sem("g_sig"), sem("merged")

        N1, N2, NF1, NMIX, NF2, NFIN = range(6)
        T_N1, T_Y, T_N2, T_F1, T_MIX, T_SY, T_HM, T_MG, T_F2 = range(9)
        G_OUT, G_PA, G_PM, G_OUT2 = range(4)
        GB = {N1: 1, N2: 2, NF1: 3, NMIX: 4, "hm": 5, NF2: 6, NFIN: 7}

        def cols(s):
            return ring[s][:, 0:KT * HALF].rearrange("p (k f) -> p k f", k=KT)

        def gate_up(s):
            return ring[s][:, 0:2 * PIECE].rearrange("p (g k f) -> p k g f", g=2, k=KT)

        def down(s):
            return ring[s][:, 2 * PIECE:].rearrange("p (k n) -> p k n", k=FT)

        def flat(ap):
            return ap.rearrange("p a b -> p (a b)")

        def overflow(eng):
            eng.wait_ge(counted, 1)
            return eng.If(eng.value_load(most[0:1, 0:1], min_val=0, max_val=SEQ) > SLOTS)

        Z = [("q", gp, i) for gp in range(2) for i in range(4)] + [("k", 2, b) for b in range(2)]
        Z += [("av", 2, t) for t in range(TILES)]
        Z += [("m", 3 + b // 4, b) for b in range(8)]
        Z += [("mv" if g < 7 else "mo", g, t) for g in range(5, 9) for t in range(TILES)]
        Z += [("if", None, t) for t in range(TILES)]
        ZG = [("g", g, t) for g in range(9, 13) for t in range(TILES)]
        by_act = [u[0] in ("q", "k", "m") for u in Z]
        ZB = 4

        PT_BANKS = {(0, 0): 3, (0, 1): 6, (1, 0): 4, (1, 1): 8, (2, 0): 2, (2, 1): 4}
        PT_BASE, PT_A, PT_D, n_ps, n_a, n_d = {}, {}, {}, 0, 0, 0
        for key, banks in PT_BANKS.items():
            PT_BASE[key], PT_A[key], PT_D[key] = n_ps, n_a, n_d
            n_ps, n_a, n_d = n_ps + banks, n_a + banks // 2, n_d + (banks + 1) // 2

        def used_by(n):
            kind, src, c = GROUP[n]
            if src == "w_in":
                return proj, TILES * (c + 1)
            if kind in ("expert", "chunk"):
                return weights_used, c + 1 + {"moe": 0, "ffn1": EXPERTS, "ffn2": EXPERTS + CHUNKS}[src]
            if src == "w_in_2":
                return z_unit, 1 + max(x for x, u in enumerate(Z + ZG) if u[1] == c)
            v = {"w_out": G_OUT, "w_proj_attn": G_PA, "w_proj_mlstm": G_PM, "w_out_2": G_OUT2}[src]
            return gemm, 4 * v + TILES * (c + 1)

        block = ctx.enter_context(nc.Block())

        @block.sync
        def _(eng):
            def free(n):
                if n >= RING:
                    eng.wait_ge(*used_by(n - RING))

            def load_cols(n, src, c, order):
                free(n)
                eng.dma_start(cols(n % RING), A[src][0, :, c * HALF:(c + 1) * HALF].rearrange(order, k=KT)
                              if src != "w_in_2" else A[src][0, :, c[0]:c[1]].rearrange(order, k=KT)
                              ).then_inc(slot_loaded[n % RING], 16)

            def load_chunk(n, pre, c):
                free(n)
                s = n % RING
                for j, w in enumerate(("gate", "up")):
                    eng.dma_start(ring[s][:, j * PIECE:(j + 1) * PIECE].rearrange("p (k f) -> p k f", k=KT),
                                  A[f"{pre}_w_{w}_2"][0, :, c * HIDDEN:(c + 1) * HIDDEN].rearrange(
                                      "(p k) f -> p k f", k=KT)).then_inc(slot_loaded[s], 16)
                eng.dma_start(ring[s][:, 2 * PIECE:], A[f"{pre}_w_down_2"][0, c * HIDDEN:(c + 1) * HIDDEN, :].rearrange(
                    "(p k) n -> p (k n)", k=FT)).then_inc(slot_loaded[s], 16)

            def load_expert(s, e):
                for j, w in enumerate(("w_gate", "w_up")):
                    eng.dma_start(ring[s][:, j * PIECE:(j + 1) * PIECE],
                                  A[w][0, bass.ds(e, 1)].rearrange("a (p k) f -> p (a k f)", k=KT)).then_inc(slot_loaded[s], 16)
                eng.dma_start(ring[s][:, 2 * PIECE:], A["w_down"][0, bass.ds(e, 1)].rearrange(
                    "a (p k) n -> p (a k n)", k=FT)).then_inc(slot_loaded[s], 16)

            by_row, by_tile = "(p k) f -> p k f", "(k p) f -> p k f"
            for c in range(6):
                load_cols(first["w_in"] + c, "w_in", c, by_row)
            for c in range(2):
                load_cols(first["w_out"] + c, "w_out", c, by_tile)
            for s in range(RING):
                free(first["moe"] + s)
                load_expert(s, s)
            with eng.Fori(1, EXPERTS // RING) as it:
                for s in range(RING):
                    eng.wait_ge(weights_used, it * RING + (s + 1 - RING))
                    load_expert(s, it * RING + s)
            with overflow(eng):
                eng.wait_ge(weights_used, EXPERTS)
                rows = expert_rows.rearrange("(i r) d -> i r d", i=PAIRS)
                with eng.Fori(0, ROUNDS - 1) as r:
                    with eng.Fori(0, PAIRS) as i:
                        j = r * PAIRS + i
                        for m in range(2):
                            for x, w in enumerate(("w_gate", "w_up")):
                                eng.dma_start(ring[m][:, x * PIECE:(x + 1) * PIECE], A[w][0, bass.ds(2 * i + m, 1)].rearrange(
                                    "a (p k) f -> p (a k f)", k=KT)).then_inc(ov_loaded, 16)
                            eng.dma_start(ring[m][:, 2 * PIECE:], A["w_down"][0, bass.ds(2 * i + m, 1)].rearrange(
                                "a (p k) n -> p (a k n)", k=FT)).then_inc(ov_loaded, 16)
                        eng.wait_ge(ov_out, j + 1)
                        eng.dma_start(rows[bass.ds(i, 1)].rearrange("a r d -> (a r) d"), exo[:, 0, :]).then_inc(ov_stored, 16)
            for c in range(CHUNKS):
                load_chunk(first["ffn1"] + c, "ffn1", c)
            starts = [c * HALF for c in range(9)] + [C_G + c * HALF for c in range(4)]
            for c, lo in enumerate(starts):
                load_cols(first["w_in_2"] + c, "w_in_2", (lo, lo + HALF), by_row)
            for w in ("w_proj_attn", "w_proj_mlstm", "w_out_2"):
                for c in range(2):
                    load_cols(first[w] + c, w + ("" if w == "w_out_2" else "_2"), c, by_tile)
            for c in range(CHUNKS):
                load_chunk(first["ffn2"] + c, "ffn2", c)
            for t in range(TILES):
                eng.wait_ge(normed, TILES * NFIN + t + 1)
                eng.dma_start(out[0, t * P:(t + 1) * P, :], tok[:, t, :]).then_inc(out_stored, 16)
            eng.wait_ge(out_stored, 16 * TILES)

        @block.gpsimd
        def _(eng):
            seq = [0]

            def link(ins):
                seq[0] += 1
                ins.then_inc(pool_seq, 1)
                eng.wait_ge(pool_seq, seq[0])

            def load_gain(name):
                eng.dma_start(gain[:, :], A[name].rearrange("a d -> (a d)").partition_broadcast(P)
                              if name != "final_norm_2" else A[name].partition_broadcast(P)).then_inc(gain_loaded, 16)

            roots = [0]

            def root(dst):
                roots[0] += 1
                eng.wait_ge(root_in, roots[0])
                eng.tensor_tensor(dst, dst, minus_half[:, 0:dst.shape[1]], ALU.pow).then_inc(root_out, 1)
                eng.wait_ge(root_out, roots[0])

            def norm_root(k):
                for t in range(TILES):
                    root(rstd[:, TILES * k + t:TILES * k + t + 1])

            load_gain("norm1_g")
            link(eng.memset(minus_half[:, :], -0.5))
            link(eng.memset(ones[:, :], 1.0))
            link(eng.memset(ident[:, :], 0.0))
            link(eng.affine_select(out=ident[:, :], in_=ident[:, :], compare_op=ALU.not_equal, fill=1.0,
                                   base=0, pattern=[[-1, P]], channel_multiplier=1))
            for m, base in ((upto, 0), (before, -1)):
                link(eng.affine_select(out=m[:, :], in_=ones[:, :], compare_op=ALU.is_ge, fill=0.0,
                                       base=base, pattern=[[1, P]], channel_multiplier=-1))
            link(eng.memset(masks[:, :], 0.0))
            for lo in (P, 3 * P):
                link(eng.affine_select(out=masks[:, lo:lo + P], in_=masks[:, lo:lo + P], compare_op=ALU.is_ge,
                                       fill=MASKED, base=0, pattern=[[-1, P]], channel_multiplier=1))
            link(eng.affine_select(out=masks[:, 2 * P:3 * P], in_=masks[:, 2 * P:3 * P], compare_op=ALU.is_gt,
                                   fill=MASKED, base=0, pattern=[[1, P]], channel_multiplier=-1))
            link(eng.iota(iota_i[:, :], pattern=[[1, SLOTS]], base=0, channel_multiplier=0))
            link(eng.tensor_copy(iota[:, :], iota_i[:, :]))
            link(eng.iota(token_i[:, :], pattern=[[P, TILES]], base=0, channel_multiplier=1))
            link(eng.tensor_copy(token_id[:, :], token_i[:, :]))
            eng.memset(relx[BUCKETS:BUCKETS + 1, :], MASKED).then_inc(consts, 1)
            eng.wait_ge(consts, 1)
            norm_root(N1)

            eng.wait_ge(bias_copied, N_BIAS)
            eng.dma_start(bias_rows.rearrange("h p m -> p h m"), bias_stage).then_inc(bias_stored, 16)
            eng.wait_ge(bias_stored, 16)
            skewed = bass.AP(tensor=bias_rows.tensor, offset=P - 1,
                             ap=[[DIST_COLS - 1, P], [P * DIST_COLS, N_BIAS], [1, SEQ]])
            eng.dma_start(bias, skewed).then_inc(bias_loaded, 16)
            eng.wait_ge(normed, TILES * (N1 + 1))
            load_gain("norm2_g")
            for _ in range(4 * TILES):
                root(hs[:, 1, 0:8])
            for _ in range(TILES):
                root(hs[:, 7, 4:8])
            norm_root(N2)
            eng.wait_ge(normed, TILES * (N2 + 1))
            load_gain("ffn1_norm_2")
            eng.wait_ge(slot_ready, 1)
            eng.wait_ge(tokens_stored, 16 * TILES)
            for i in range(PAIRS):
                if i >= 2:
                    eng.wait_ge(exT_a, i - 1)
                    eng.wait_ge(exT_d, i - 1)
                eng.indirect_dma_start(out=xg[:, i % 2, :], out_offset=None, in_=tokens[:, :],
                                       in_offset=bass.IndirectOffsetOnAxis(ap=slot_tok[:, i:i + 1], axis=0)
                                       ).then_inc(gathered[i % 2], 16)
            eng.wait_ge(rows_ready, 1)
            for b in range(2):
                eng.wait_ge(ex_stored[b], 16 * PAIRS // 2)
            for n in range(2 * TILES):
                eng.indirect_dma_start(out=routed[:, n, :], out_offset=None, in_=expert_rows[:, :],
                                       in_offset=bass.IndirectOffsetOnAxis(ap=row_u[:, n:n + 1], axis=0)
                                       ).then_inc(row_gathered[n], 16)
            with overflow(eng):
                for r in range(ROUNDS - 1):
                    for i in range(PAIRS):
                        eng.wait_ge(ov_slot, r * PAIRS + i + 1)
                        eng.wait_ge(tokens_stored, 16 * TILES)
                        eng.indirect_dma_start(out=xg[:, 0, :], out_offset=None, in_=tokens[:, :],
                                               in_offset=bass.IndirectOffsetOnAxis(ap=slot_tok[:, 0:1], axis=0)
                                               ).then_inc(ov_gathered, 16)
                    eng.wait_ge(ov_rows, r + 1)
                    eng.wait_ge(rows_ready, 1)
                    for n in range(2 * TILES):
                        eng.indirect_dma_start(out=routed[:, n, :], out_offset=None, in_=expert_rows[:, :],
                                               in_offset=bass.IndirectOffsetOnAxis(ap=row_u[:, n:n + 1], axis=0)
                                               ).then_inc(ov_routed, 16)
            eng.wait_ge(moe_added, 1)
            b_in = A["b_in_2"][0]
            eng.dma_start(bias_av, b_in[C_AV:C_MQ].partition_broadcast(P)).then_inc(bb_loaded, 16)
            eng.dma_start(bias_mvo, b_in[C_MV:C_IF].partition_broadcast(P)).then_inc(bb_loaded, 16)
            norm_root(NF1)
            eng.wait_ge(normed, TILES * (NF1 + 1))
            load_gain("mix_norm_2")
            norm_root(NMIX)
            eng.wait_ge(normed, TILES * (NMIX + 1))
            eng.dma_start(gain[:, :], A["mlstm_head_norm_2"].rearrange("a h v -> (a h v)").partition_broadcast(P)
                          ).then_inc(gain_loaded, 16)
            for _ in range(TILES):
                root(hs[:, 3, 8:16])
            eng.wait_ge(mixed, 5 * TILES)
            eng.dma_start(bias_g, b_in[C_G:C_END].partition_broadcast(P)).then_inc(bb_loaded, 16)
            load_gain("ffn2_norm_2")
            norm_root(NF2)
            eng.wait_ge(normed, TILES * (NF2 + 1))
            load_gain("final_norm_2")
            norm_root(NFIN)

        @block.scalar
        def _(eng):
            seq = [0]

            def link(ins):
                seq[0] += 1
                ins.then_inc(act_seq, 1)
                eng.wait_ge(act_seq, seq[0])

            eng.dma_start(res[:, :, :], A["x"][0].rearrange("(t p) d -> p t d", p=P)).then_inc(x_loaded, 16)
            b_in = A["b_in_2"][0]
            n_vec = [0]

            def load_vec(dst, src):
                eng.dma_start(dst, src).then_inc(vec_loaded, 16)
                n_vec[0] += 1

            bq = b_in[0:C_K].rearrange("(g m i d) -> m g i d", g=2, m=2, i=4)
            for m in range(2):
                for g in range(2):
                    load_vec(vec_rows[V_BQ + 4 * g:V_BQ + 4 * g + 4, HEAD * m:HEAD * m + HEAD], bq[m, g])
            load_vec(vec_rows[V_BK:V_BM, :], b_in[C_K:C_AV].rearrange("(r p) -> r p", p=P))
            load_vec(vec_rows[V_BM:V_CONV, :], b_in[C_MQ:C_MV].rearrange("(r p) -> r p", p=P))
            for j in range(CONV):
                load_vec(vec_rows[V_CONV + 8 * j:V_CONV + 8 * j + 8, :],
                         A["mlstm_conv_2"][0, j].rearrange("(r p) -> r p", p=P))
            for n, name in enumerate(("diff_q_g", "diff_k_g", "moba_q_g", "moba_k_g")):
                for m in range(2):
                    load_vec(vec_rows[V_QK + n:V_QK + n + 1, HEAD * m:HEAD * m + HEAD], A[name][0:1, :])
            load_vec(vec_rows[V_SUB:V_SUB + 1, :], A["diff_sub_g"][0:1, :])
            assert n_vec[0] == N_VEC
            eng.dma_start(relx[0:BUCKETS, :], A["rel_bias"]).then_inc(rel_loaded, 16)
            eng.dma_start(onehot[:, :], buckets).then_inc(rel_loaded, 16)
            for n, name in enumerate(("lambda_q1", "lambda_k1", "lambda_q2", "lambda_k2")):
                eng.dma_start(lam_rows[:, n, :], A[name][0].partition_broadcast(P)).then_inc(lam_loaded, 16)
            eng.dma_start(router[:, :, 0:GROUPS], A["router_group"][0].rearrange("(p k) g -> p k g", k=KT)).then_inc(router_loaded, 16)
            for g in range(GROUPS):
                eng.dma_start(router[:, :, GROUPS + PER_GROUP * g:GROUPS + PER_GROUP * (g + 1)],
                              A["router_expert"][0, g].rearrange("(p k) e -> p k e", k=KT)).then_inc(router_loaded, 16)
            eng.dma_start(w_if[:, :, :], A["w_in_2"][0, :, C_IF:C_G].rearrange("(p k) f -> p k f", k=KT)).then_inc(if_loaded, 16)
            eng.dma_start(b_if[:, :], b_in[C_IF:C_G].partition_broadcast(P)).then_inc(if_loaded, 16)
            eng.dma_start(sink_nat[:, :], A["attn_sinks_2"][0].partition_broadcast(P)).then_inc(if_loaded, 16)

            def square(k, ready):
                for t in range(TILES):
                    eng.wait_ge(*ready(t))
                    eng.activation(tok[:, t, :], res[:, t, :], ACT.Square,
                                   accum_out=ss[:, TILES * k + t:TILES * k + t + 1]).then_inc(squared, 1)

            def t8_copy(u, dst, scale=None):
                for t in range(TILES):
                    eng.wait_ge(t8_a, TILES * u + t + 1)
                    src = PS[:, 4 + 2 * t, :].rearrange("p (k q) -> p k q", q=P)
                    eng.activation(dst[:, 0:4, t * P:(t + 1) * P], src, ACT.Copy,
                                   scale=1.0 if scale is None else scale).then_inc(t8c_a, 1)

            def pT_copy(key):
                for b in range(1, PT_BANKS[key], 2):
                    eng.wait_ge(pT_ps, PT_BASE[key] + b + 1)
                    eng.activation(flat(PT[:, 4 * b:4 * b + 4, :]), PS[:, 4 + b % 4, :], ACT.Copy).then_inc(pT_a, 1)

            square(N1, lambda t: (x_loaded, 16))
            eng.wait_ge(lam_sum, 1)
            eng.activation(lam[:, 2:4], lam[:, 0:2], ACT.Exp).then_inc(lam_exp, 1)
            t8_copy(T_N1, hT)

            eng.wait_ge(vec_ready, 1)
            units = [(c, t) for c in (0, 1, 3, 4) for t in range(TILES)]

            def qk_copy(n):
                c, t = units[n]
                w = {0: 0, 1: 1, 3: 2, 4: 3}[c]
                eng.wait_ge(qk_ps, n + 1)
                eng.activation(qkT[w][:, :, t * P:(t + 1) * P], PS[:, 4 + n % 2, :].rearrange("p (j q) -> p j q", j=4),
                               ACT.Copy, scale=vec[:, V_QK + w:V_QK + w + 1]).then_inc(qk_done, 1)

            for n, (c, t) in enumerate(units):
                eng.wait_ge(proj, TILES * c + t + 1)
                if n >= 2:
                    eng.wait_ge(proj_sq_read, n - 1)
                eng.activation(tok[:, t, HALF:], PS[:, (TILES * c + t) % 4, :], ACT.Square).then_inc(proj_sq, 1)
                if n >= 2:
                    qk_copy(n - 2)
            for n in range(len(units) - 2, len(units)):
                qk_copy(n)

            def exps(t, nheads, row):
                n = P * (t + 1)
                for a in range(nheads):
                    eng.activation(L[:, a, 0:n], L[:, a, 0:n], ACT.Exp, bias=hs[:, row, a:a + 1],
                                   accum_out=hs[:, row + 1, a:a + 1]).then_inc(expd, 1)

            for t in range(TILES):
                eng.wait_ge(maxed, t + 1)
                exps(t, MAPS, 1)
                pT_copy((0, t))
                eng.wait_ge(pv, 2 * t + 1)
                eng.activation(L[:, 0:2, :], PS[:, 0, :].rearrange("p (a b) -> p a b", a=2), ACT.Square).then_inc(pv_sq, 1)
            for t in range(TILES):
                eng.wait_ge(t8_a, TILES * T_Y + t + 1)
                src = PS[:, 4 + 2 * t, :].rearrange("p (k q) -> p k q", q=P)
                eng.activation(yT[:, 0:4, t * P:(t + 1) * P], src, ACT.Copy,
                               scale=vec[:, V_SUB:V_SUB + 1]).then_inc(t8c_a, 1)

            square(N2, lambda t: (gemm_used, 4 * G_OUT + 3 + t))
            t8_copy(T_N2, hT)
            for t in range(TILES):
                eng.wait_ge(normed, TILES * N2 + t + 1)
                eng.dma_start(tokens[t * P:(t + 1) * P, :], tok[:, t, :]).then_inc(tokens_stored, 16)
            for t in range(TILES):
                eng.wait_ge(route_exp_in, t + 1)
                eng.activation(rt[:, t, 80:84], rt8[:, t, 0, 0:4], ACT.Exp, bias=rt[:, t, 84:85],
                               accum_out=rt[:, t, 85:86])
                eng.activation(rt[:, t, 86:87], rt[:, t, 87:88], ACT.Exp).then_inc(route_exp, 1)

            def expert_pair(i, it, u, early):
                eng.wait_ge(exT_a, i + 1)
                if not early:
                    eng.wait_ge(ex_gu, i - 1)
                eng.activation(flat(xgT[:, u, 0:4, :]), PS[:, 6, :], ACT.Copy).then_inc(exTc_a, 1)
                eng.wait_ge(ex_gu, i + 1)
                if not early:
                    eng.wait_ge(ex_hid, i - 1)
                eng.activation(act_e[:, u, :], PS[:, 4 + u, 0:HIDDEN], ACT.Silu).then_inc(ex_act, 1)
                eng.wait_ge(weights_used, i * 2 + 2)
                if not early:
                    eng.wait_ge(ex_stored[u], it * 16)
                eng.activation(exo[:, u, 0:HALF], PS[:, 2 * u, :], ACT.Copy).then_inc(ex_out_a, 1)
                eng.wait_ge(ex_out_a, i + 1)
                eng.wait_ge(ex_out_d, i + 1)
                rows = expert_rows.rearrange("(i r) d -> i r d", i=PAIRS)
                eng.dma_start(rows[bass.ds(i, 1)].rearrange("a r d -> (a r) d"), exo[:, u, :]).then_inc(ex_stored[u], 16)

            for u in range(2):
                expert_pair(u, 0, u, True)
            with eng.Fori(1, PAIRS // 2) as it:
                for u in range(2):
                    expert_pair(it * 2 + u, it, u, False)
            with overflow(eng):
                with eng.Fori(0, ROUNDS - 1) as r:
                    with eng.Fori(0, PAIRS) as i:
                        eng.wait_ge(ov_gu, r * PAIRS + i + 1)
                        eng.activation(act_e[:, 0, :], PS[:, 4, 0:HIDDEN], ACT.Silu).then_inc(ov_act, 1)

            def ffn(f):
                for c in range(CHUNKS):
                    n = f * CHUNKS + c
                    for t in range(TILES):
                        eng.wait_ge(ff_gu, TILES * n + t + 1)
                        if n >= 2:
                            eng.wait_ge(ff_hid, TILES * (n - 2) + t + 1)
                        eng.activation(act_f[:, c % 2, t, :], PS[:, 4 + t, 0:HIDDEN], ACT.Silu).then_inc(ff_act, 1)

            square(NF1, lambda t: (moe_added, 1))
            t8_copy(T_F1, hT)
            ffn(0)

            square(NMIX, lambda t: (ff_added, 2 * t + 2))
            t8_copy(T_MIX, hT)
            n_silu = [0]

            def silu_conv():
                b = n_silu[0]
                eng.wait_ge(conv_done, b + 1)
                eng.activation(mqk[:, b, :], conv[:, b % 2, :], ACT.Silu).then_inc(conv_silu, 1)
                n_silu[0] += 1

            for n, (kind, g, i) in enumerate(Z):
                if not by_act[n]:
                    continue
                eng.wait_ge(z_unit, n + 1)
                src = PS[:, n % ZB, 0:SEQ]
                if kind == "q":
                    eng.activation(sqT[:, 4 * g + i, :], src, ACT.Identity, scale=SCALE,
                                   bias=vec[:, V_BQ + 4 * g + i:V_BQ + 4 * g + i + 1]).then_inc(z_act, 1)
                elif kind == "k":
                    eng.activation(skT[:, i, :], src, ACT.Identity, bias=vec[:, V_BK + i:V_BK + i + 1]).then_inc(z_act, 1)
                else:
                    if i >= 2:
                        eng.wait_ge(conv_done, i - 1)
                    eng.activation(raw[:, i % 2, CONV - 1:], src, ACT.Identity,
                                   bias=vec[:, V_BM + i:V_BM + i + 1]).then_inc(z_act, 1)
                    if i >= 1:
                        silu_conv()
            silu_conv()
            for t in range(TILES):
                eng.wait_ge(z_dve, sum(not a for a in by_act) - TILES + t + 1)
                link(eng.activation(ga[:, t, 1, :], ga[:, t, 0, :], ACT.Tanh, scale=1.0 / SOFTCAP))
                eng.activation(ga[:, t, 2, 8:16], ga[:, t, 1, 8:16], ACT.Exp, scale=-SOFTCAP).then_inc(gates_exp, 1)
                eng.wait_ge(gates_u, t + 1)
                eng.activation(ga[:, t, 3, 8:16], ga[:, t, 3, 0:8], ACT.Ln).then_inc(gates_exp, 1)
            for t in range(TILES):
                eng.wait_ge(maxed, TILES + t + 1)
                exps(t, Q_HEADS, 1)
                eng.activation(hs[:, 4, :], hs[:, 3, :], ACT.Exp).then_inc(sink_exp, 1)
                pT_copy((1, t))
            t8_copy(T_SY, yT)
            for t in range(TILES):
                eng.wait_ge(ml_max, t + 1)
                n = P * (t + 1)
                for a in range(MLSTM_HEADS):
                    eng.activation(L[:, a, 0:n], L[:, a, 0:n], ACT.Exp, bias=hs[:, 1, a:a + 1]).then_inc(ml_exp, 1)
                eng.activation(hs[:, 5, 0:8], hs[:, 4, 0:8], ACT.Exp, scale=-1.0).then_inc(ml_exp, 1)
                pT_copy((2, t))
                eng.wait_ge(ml_h, t + 1)
                eng.activation(L[:, 0:4, :], tok[:, t, :].rearrange("p (a b) -> p a b", a=4), ACT.Square).then_inc(ml_hsq, 1)
                eng.activation(mo[:, t, :], mo[:, t, :], ACT.Sigmoid).then_inc(sig_done, 1)
            t8_copy(T_HM, hmT)
            for n in range(len(ZG)):
                eng.wait_ge(g_sig, n + 1)
                g, t = ZG[n][1] - 9, ZG[n][2]
                eng.activation(gates[:, t, g * HALF:(g + 1) * HALF], gates[:, t, g * HALF:(g + 1) * HALF],
                               ACT.Sigmoid).then_inc(sig_done, 1)
            t8_copy(T_MG, yT)
            square(NF2, lambda t: (gemm_used, 4 * G_OUT2 + 3 + t))
            t8_copy(T_F2, hT)
            ffn(1)
            square(NFIN, lambda t: (ff_added, 4 + 2 * t + 2))

        @block.tensor
        def _(eng):
            def weights(n):
                eng.wait_ge(slot_loaded[n % RING], loaded_at[n])

            def transpose8(u, src, ready, strided):
                for t in range(TILES):
                    eng.wait_ge(*ready(t))
                    for k in range(KT):
                        cut = src[:, t, k:D:KT] if strided else src[:, t, k * P:(k + 1) * P]
                        mm = eng.transpose(PS[:, 4 + 2 * t + k // 4, (k % 4) * P:(k % 4 + 1) * P], cut, ident[:, :])
                        if k == 3:
                            mm.then_inc(t8_a, 1)
                    mm.then_inc(t8_d, 1)

            def copied8(u):
                eng.wait_ge(t8c_a, TILES * (u + 1))
                eng.wait_ge(t8c_d, TILES * (u + 1))

            eng.wait_ge(consts, 1)
            eng.wait_ge(vec_loaded, 16 * N_VEC)
            eng.transpose(PS[:, 0, 0:V_ROWS], vec_rows[:, :], ident[0:V_ROWS, 0:V_ROWS]).then_inc(vec_T, 1)
            transpose8(T_N1, tok, lambda t: (normed, TILES * N1 + t + 1), True)
            eng.wait_ge(rel_wide, 1)
            for h in range(N_BIAS):
                if h >= 2:
                    eng.wait_ge(bias_copied, h - 1)
                eng.matmul(PS[:, 2 + h % 2, 0:DIST_COLS], relb[:, h, :], onehot[:, :], start=True, stop=True).then_inc(bias_ps, 1)
            copied8(T_N1)
            eng.wait_ge(bias_copied, N_BIAS)
            eng.wait_ge(vec_ready, 1)

            units = [(c, t) for c in range(6) for t in range(TILES)]
            qk_units = [(c, t) for c in (0, 1, 3, 4) for t in range(TILES)]
            n_qk = [0]

            def qk_transposes(j):
                c, t = units[j]
                if (c, t) not in qk_units:
                    return
                n = n_qk[0]
                eng.wait_ge(proj_used, j + 1)
                if n >= 2:
                    eng.wait_ge(qk_done, n - 1)
                for b in range(4):
                    mm = eng.transpose(PS[:, 4 + n % 2, b * P:(b + 1) * P], tok[:, t, b * P:(b + 1) * P], ident[:, :])
                mm.then_inc(qk_ps, 1)
                n_qk[0] += 1

            for j, (c, t) in enumerate(units):
                n = first["w_in"] + c
                weights(n)
                if j >= 4:
                    eng.wait_ge(proj_used, j - 3)
                for k in range(KT):
                    mm = eng.matmul(PS[:, j % 4, :], hT[:, k, t * P:(t + 1) * P], cols(n % RING)[:, k, :],
                                    start=(k == 0), stop=(k == KT - 1))
                mm.then_inc(proj, 1)
                if j >= 2:
                    qk_transposes(j - 2)
            for j in range(len(units) - 2, len(units)):
                qk_transposes(j)

            def scores(base, t, q, k, pairs):
                n = P * (t + 1)
                for g in range(pairs):
                    if g >= 2:
                        eng.wait_ge(score_used, base + g - 1)
                    for m in range(2):
                        a, b = HEAD * m, HEAD * (m + 1)
                        mm = eng.matmul(PS[:, 2 * (g % 2) + m, 0:n], q(g)[a:b, t * P:(t + 1) * P], k(g)[a:b, 0:n],
                                        start=True, stop=True)
                    mm.then_inc(score, 1)

            def weight_transposes(key, blocks, ready):
                assert (len(blocks) + 3) // 4 == PT_BANKS[key]
                for x, (a, kb) in enumerate(blocks):
                    j = x // 4
                    if x % 4 == 0 and j >= 4:
                        done, base = (pT_a, PT_A[key]) if j % 2 else (pT_d, PT_D[key])
                        eng.wait_ge(done, base + (j - 4) // 2 + 1)
                    if kb == 0:
                        eng.wait_ge(*ready(a))
                    mm = eng.transpose(PS[:, 4 + j % 4, (x % 4) * P:(x % 4 + 1) * P],
                                       L[:, a, kb * P:(kb + 1) * P], ident[:, :])
                    if x % 4 == 3 or x == len(blocks) - 1:
                        mm.then_inc(pT_ps, 1)
                banks = PT_BANKS[key]
                eng.wait_ge(pT_a, PT_A[key] + banks // 2)
                eng.wait_ge(pT_d, PT_D[key] + (banks + 1) // 2)

            eng.wait_ge(qk_done, 8)
            eng.wait_ge(proj_used, len(units))
            for t in range(TILES):
                if t > 0:
                    eng.wait_ge(mixed, 2 * t)
                scores(8 * t, t, lambda g: qkT[2 * (g // 4)][:, g % 4, :], lambda g: qkT[2 * (g // 4) + 1][:, g % 4, :], 8)
                maps = [2 * j for j in range(4)] + list(range(8, MAPS))
                blocks = [(a, kb) for a in maps for kb in range(t + 1)]

                weight_transposes((0, t), blocks, lambda a: (weighted, 4 * t + a // 2 + 1) if a < 8
                                  else (expd, MAPS * t + a + 1))
                for u in range(12):
                    for kb in range(t + 1):
                        lhs = PT[:, u * (t + 1) + kb, :]
                        if u < 4:
                            dst, v = PS[:, 0, u * P:(u + 1) * P], vals[:, kb, u * P:(u + 1) * P]
                        else:
                            h = u - 4
                            dst, v = PS[:, 1, h * HEAD:(h + 1) * HEAD], vals[:, kb, HALF + h * HEAD:HALF + (h + 1) * HEAD]
                        mm = eng.matmul(dst, lhs, v, start=(kb == 0), stop=(kb == t))
                    if u == 3 or u == 11:
                        mm.then_inc(pv, 1)
            transpose8(T_Y, tok, lambda t: (mixed, 2 * t + 2), False)

            def gemm_1024(v, src, u, name):
                copied8(u)
                if v > 0:
                    eng.wait_ge(gemm_used, 4 * v)
                for h in range(HALVES):
                    n = first[name] + h
                    weights(n)
                    for t in range(TILES):
                        for k in range(KT):
                            mm = eng.matmul(PS[:, 2 * h + t, :], src[:, k, t * P:(t + 1) * P], cols(n % RING)[:, k, :],
                                            start=(k == 0), stop=(k == KT - 1))
                        mm.then_inc(gemm, 1)

            eng.wait_ge(mixed, 2 * TILES)
            gemm_1024(G_OUT, yT, T_Y, "w_out")

            transpose8(T_N2, tok, lambda t: (normed, TILES * N2 + t + 1), True)
            copied8(T_N2)
            eng.wait_ge(router_loaded, 16 * (1 + GROUPS))
            for t in range(TILES):
                for k in range(KT):
                    mm = eng.matmul(PS[:, t, 0:ROUTES], hT[:, k, t * P:(t + 1) * P], router[:, k, :],
                                    start=(k == 0), stop=(k == KT - 1))
                mm.then_inc(route, 1)
            eng.wait_ge(assigned, TILES)
            eng.matmul(PS[:, 2, 0:EXPERTS], before[:, :], assign[:, 0, 2, :], start=True, stop=True).then_inc(pos_ps, 1)
            eng.matmul(PS[:, 3, 0:EXPERTS], ones[:, :], assign[:, 0, 2, :], start=True, stop=False)
            eng.matmul(PS[:, 3, 0:EXPERTS], before[:, :], assign[:, 1, 2, :], start=False, stop=True).then_inc(pos_ps, 1)
            eng.wait_ge(selected, TILES)
            for t in range(TILES):
                mm = eng.matmul(PS[:, 2, HALF - EXPERTS:], ones[:, :], assign[:, t, 2, :], start=(t == 0), stop=(t == TILES - 1))
            mm.then_inc(pos_ps, 1)
            for i in range(PAIRS):
                for t in range(TILES):
                    mm = eng.matmul(PS[:, 0, i:i + 1], flat(select[:, t, 2 * i:2 * i + 2, :]), token_id[:, t:t + 1],
                                    start=(t == 0), stop=(t == TILES - 1))
            mm.then_inc(slot_ps, 1)

            def expert_pair(i, it, u, early):
                slots = [2 * u, 2 * u + 1]
                eng.wait_ge(gathered[u], (i - u) * 8 + 16)
                if not early:
                    eng.wait_ge(exTc_a, i)
                    eng.wait_ge(exTc_d, i)
                    eng.wait_ge(ex_hTc, i)
                elif u:
                    eng.wait_ge(exTc_d, i)
                    eng.wait_ge(ex_hTc, i)
                for k in range(KT):
                    mm = eng.transpose(PS[:, 6 + k // 4, (k % 4) * P:(k % 4 + 1) * P], xg[:, u, k:D:KT], ident[:, :])
                    if k == 3:
                        mm.then_inc(exT_a, 1)
                mm.then_inc(exT_d, 1)
                eng.wait_ge(exTc_a, i + 1)
                eng.wait_ge(exTc_d, i + 1)
                if not early:
                    eng.wait_ge(ex_hid, i - 1)
                for s in slots:
                    eng.wait_ge(slot_loaded[s], it * 48 + loaded_at[first["moe"] + s])
                for k in range(KT):
                    for m, s in enumerate(slots):
                        mm = eng.matmul(PS[SLOTS * m:SLOTS * (m + 1), 4 + u, :], xgT[:, u, k, SLOTS * m:SLOTS * (m + 1)],
                                        gate_up(s)[:, k], start=(k == 0), stop=(k == KT - 1))
                mm.then_inc(ex_gu, 1)
                eng.wait_ge(ex_hid, i + 1)
                for k in range(FT):
                    mm = eng.transpose(PS[:, 6, k * P:(k + 1) * P], hid_e[:, u, k:HIDDEN:FT], ident[:, :])
                mm.then_inc(ex_hT, 1)
                eng.wait_ge(ex_hTc, i + 1)
                if not early:
                    eng.wait_ge(ex_out_a, i - 1)
                    eng.wait_ge(ex_out_d, i - 1)
                for h in range(HALVES):
                    for k in range(FT):
                        for m, s in enumerate(slots):
                            mm = eng.matmul(PS[SLOTS * m:SLOTS * (m + 1), 2 * u + h, :],
                                            hidT_e[:, u, k, SLOTS * m:SLOTS * (m + 1)],
                                            down(s)[:, k, h * HALF:(h + 1) * HALF], start=(k == 0), stop=(k == FT - 1))
                            if h == HALVES - 1 and k == FT - 1 and m == 0:
                                mm.then_inc(weights_used, 1)
                mm.then_inc(weights_used, 1)
                return mm

            eng.wait_ge(slot_ready, 1)
            for u in range(2):
                expert_pair(u, 0, u, True)
            with eng.Fori(1, PAIRS // 2) as it:
                for u in range(2):
                    expert_pair(it * 2 + u, it, u, False)

            with overflow(eng):
                with eng.Fori(0, ROUNDS - 1) as r:
                    with eng.Fori(0, PAIRS) as i:
                        j = r * PAIRS + i
                        eng.wait_ge(ov_sel, j + 1)
                        for t in range(TILES):
                            mm = eng.matmul(PS[:, 0, 0:1], flat(select[:, t, 0:2, :]), token_id[:, t:t + 1],
                                            start=(t == 0), stop=(t == TILES - 1))
                        mm.then_inc(ov_slot_ps, 1)
                        eng.wait_ge(ov_gathered, 16 * j + 16)
                        for k in range(KT):
                            mm = eng.transpose(PS[:, 6 + k // 4, (k % 4) * P:(k % 4 + 1) * P], xg[:, 0, k:D:KT], ident[:, :])
                        mm.then_inc(ov_xT, 1)
                        eng.wait_ge(ov_xTc, j + 1)
                        eng.wait_ge(ov_loaded, 96 * j + 96)
                        for k in range(KT):
                            for m in range(2):
                                mm = eng.matmul(PS[SLOTS * m:SLOTS * (m + 1), 4, :], xgT[:, 0, k, SLOTS * m:SLOTS * (m + 1)],
                                                gate_up(m)[:, k], start=(k == 0), stop=(k == KT - 1))
                        mm.then_inc(ov_gu, 1)
                        eng.wait_ge(ov_hid, j + 1)
                        for k in range(FT):
                            mm = eng.transpose(PS[:, 6, k * P:(k + 1) * P], hid_e[:, 0, k:HIDDEN:FT], ident[:, :])
                        mm.then_inc(ov_hT, 1)
                        eng.wait_ge(ov_hTc, j + 1)
                        for h in range(HALVES):
                            for k in range(FT):
                                for m in range(2):
                                    mm = eng.matmul(PS[SLOTS * m:SLOTS * (m + 1), h, :],
                                                    hidT_e[:, 0, k, SLOTS * m:SLOTS * (m + 1)],
                                                    down(m)[:, k, h * HALF:(h + 1) * HALF], start=(k == 0), stop=(k == FT - 1))
                        mm.then_inc(ov_down, 1)

            def ffn(f, u, name):
                copied8(u)

                def gate_and_up(c):
                    n, g = first[name] + c, f * CHUNKS + c
                    weights(n)
                    for t in range(TILES):
                        if g >= 1:
                            eng.wait_ge(ff_hid, TILES * (g - 1) + t + 1)
                        for k in range(KT):
                            mm = eng.matmul(PS[:, 4 + t, :], hT[:, k, t * P:(t + 1) * P], gate_up(n % RING)[:, k],
                                            start=(k == 0), stop=(k == KT - 1))
                        mm.then_inc(ff_gu, 1)

                def down_chunk(c):
                    n, g = first[name] + c, f * CHUNKS + c
                    eng.wait_ge(ff_hid, TILES * (g + 1))
                    if g >= 2:
                        eng.wait_ge(ff_hTc, g - 1)
                    for t in range(TILES):
                        for k in range(FT):
                            mm = eng.transpose(PS[:, 6 + g % 2, k * SEQ + t * P:k * SEQ + (t + 1) * P],
                                               hid_f[:, c % 2, t, k:HIDDEN:FT], ident[:, :])
                    mm.then_inc(ff_hT, 1)
                    eng.wait_ge(ff_hTc, g + 1)
                    for t in range(TILES):
                        for h in range(HALVES):
                            for k in range(FT):
                                mm = eng.matmul(PS[:, 2 * t + h, :], hidT_f[:, c % 2, k, t * P:(t + 1) * P],
                                                down(n % RING)[:, k, h * HALF:(h + 1) * HALF],
                                                start=(c == 0 and k == 0), stop=(c == CHUNKS - 1 and k == FT - 1))
                    mm.then_inc(weights_used, 1)

                for c in range(CHUNKS + 1):
                    if c < CHUNKS:
                        gate_and_up(c)
                    if c >= 1:
                        down_chunk(c - 1)

            transpose8(T_F1, tok, lambda t: (normed, TILES * NF1 + t + 1), True)
            ffn(0, T_F1, "ffn1")


            transpose8(T_MIX, tok, lambda t: (normed, TILES * NMIX + t + 1), True)
            copied8(T_MIX)
            for n, (kind, g, i) in enumerate(Z):
                if g is not None and (n == 0 or Z[n - 1][1] != g):
                    weights(first["w_in_2"] + g)
                if n >= ZB:
                    eng.wait_ge(z_act if by_act[n - ZB] else z_dve,
                                sum(x == by_act[n - ZB] for x in by_act[:n - ZB + 1]))
                w = cols((first["w_in_2"] + g) % RING) if g is not None else None
                if kind == "if":
                    eng.wait_ge(if_loaded, 16 * 3)
                for k in range(KT):
                    flags = dict(start=(k == 0), stop=(k == KT - 1))
                    if kind == "q":
                        for m in range(2):
                            lo = 4 * HEAD * m + HEAD * i
                            mm = eng.matmul(PS[HEAD * m:HEAD * (m + 1), n % ZB, 0:SEQ], w[:, k, lo:lo + HEAD], hT[:, k, :], **flags)
                    elif kind in ("k", "m"):
                        mm = eng.matmul(PS[:, n % ZB, 0:SEQ], w[:, k, (i % 4) * P:(i % 4 + 1) * P], hT[:, k, :], **flags)
                    else:
                        rhs = {"av": lambda: w[:, k, 256:HALF], "mv": lambda: w[:, k, :], "mo": lambda: w[:, k, :],
                               "if": lambda: w_if[:, k, :]}[kind]()
                        width = {"av": 256, "if": 16}.get(kind, HALF)
                        mm = eng.matmul(PS[:, n % ZB, 0:width], hT[:, k, i * P:(i + 1) * P], rhs, **flags)
                mm.then_inc(z_unit, 1)
            eng.wait_ge(z_dve, sum(not x for x in by_act))
            eng.wait_ge(z_act, sum(by_act))
            eng.wait_ge(gates_ready, 1)
            eng.matmul(PS[:, 0, 0:8], upto[:, :], ga[:, 0, 6, 8:16], start=True, stop=True).then_inc(cum_ps, 1)
            eng.wait_ge(gates_ready, 2)
            eng.matmul(PS[:, 1, 0:8], ones[:, :], ga[:, 0, 6, 8:16], start=True, stop=False)
            eng.matmul(PS[:, 1, 0:8], upto[:, :], ga[:, 1, 6, 8:16], start=False, stop=True).then_inc(cum_ps, 1)
            for t in range(TILES):
                eng.wait_ge(a_ready, t + 1)
                mm = eng.transpose(PS[0:8, 2, t * P:(t + 1) * P], ga[:, t, 7, 8:16], ident[:, :])
            mm.then_inc(a_ps, 1)
            eng.wait_ge(a_copied, 1)
            for t in range(TILES):
                if t > 0:
                    eng.wait_ge(mixed, 4 + 2 * t)
                scores(16 + 8 * t, t, lambda g: sqT[:, g, :], lambda g: skT[:, g // 4, :], 8)
                weight_transposes((1, t), [(a, kb) for a in range(Q_HEADS) for kb in range(t + 1)],
                                  lambda a: (expd, MAPS * TILES + Q_HEADS * t + a + 1))
                for a in range(Q_HEADS):
                    g, i, m = a // 8, a % 8 // 2, a % 2
                    kv = 2 * g + m
                    for kb in range(t + 1):
                        mm = eng.matmul(PS[:, g, (4 * m + i) * HEAD:(4 * m + i + 1) * HEAD], PT[:, a * (t + 1) + kb, :],
                                        sv[:, kb, kv * HEAD:(kv + 1) * HEAD], start=(kb == 0), stop=(kb == t))
                    if a % 8 == 7:
                        mm.then_inc(pv, 1)
            transpose8(T_SY, tok, lambda t: (mixed, 4 + 2 * t + 2), False)
            eng.wait_ge(conv_silu, 8)
            for t in range(TILES):
                n = P * (t + 1)
                if t > 0:
                    eng.wait_ge(ml_h, t)
                for j in range(4):
                    for m in range(2):
                        mm = eng.matmul(PS[:, j, m * SEQ:m * SEQ + n], ident[0:8, 2 * j + m:2 * j + m + 1].broadcast_to([8, P]), aT[:, 0:n], start=True, stop=True)
                    mm.then_inc(ml_a, 1)
                eng.wait_ge(ml_used, 4 * (t + 1))
                for j in range(4):
                    if j >= 2:
                        eng.wait_ge(ml_sc, 8 * t + 2 * (j - 1))
                    for m in range(2):
                        a, b = HEAD * m, HEAD * (m + 1)
                        mm = eng.matmul(PS[:, 2 * (j % 2) + m, 0:n], mqk[a:b, j, t * P:(t + 1) * P], mqk[a:b, 4 + j, 0:n],
                                        start=True, stop=True)
                    mm.then_inc(ml_s, 1)
                weight_transposes((2, t), [(a, kb) for a in range(MLSTM_HEADS) for kb in range(t + 1)],
                                  lambda a: (ml_sc, 8 * t + a + 1))
                for a in range(MLSTM_HEADS):
                    for kb in range(t + 1):
                        mm = eng.matmul(PS[:, a // 4, (a % 4) * P:(a % 4 + 1) * P], PT[:, a * (t + 1) + kb, :],
                                        mv[:, kb, a * P:(a + 1) * P], start=(kb == 0), stop=(kb == t))
                    if a % 4 == 3:
                        mm.then_inc(pv, 1)
            transpose8(T_HM, tok, lambda t: (mixed, 8 + t + 1), False)
            for n, (_, g, t) in enumerate(ZG):
                weights(first["w_in_2"] + g)
                if n >= ZB:
                    eng.wait_ge(g_sig, n - ZB + 1)
                for k in range(KT):
                    mm = eng.matmul(PS[:, n % ZB, :], hT[:, k, t * P:(t + 1) * P], cols((first["w_in_2"] + g) % RING)[:, k, :],
                                    start=(k == 0), stop=(k == KT - 1))
                mm.then_inc(z_unit, 1)
            eng.wait_ge(g_sig, len(ZG))
            gemm_1024(G_PA, yT, T_SY, "w_proj_attn")
            gemm_1024(G_PM, hmT, T_HM, "w_proj_mlstm")
            transpose8(T_MG, tok, lambda t: (merged, 3 + t), False)
            gemm_1024(G_OUT2, yT, T_MG, "w_out_2")
            transpose8(T_F2, tok, lambda t: (normed, TILES * NF2 + t + 1), True)
            ffn(1, T_F2, "ffn2")

        @block.vector
        def _(eng):
            seq, roots = [0], [0]

            def link(ins):
                seq[0] += 1
                ins.then_inc(dve_seq, 1)
                eng.wait_ge(dve_seq, seq[0])

            def wide(ap, n):
                return ap.unsqueeze(len(ap.shape)).broadcast_to([*ap.shape, n])

            def rsqrt(dst, sums, n):
                roots[0] += 1
                eng.tensor_scalar(dst, sums, 1.0 / n, EPS, ALU.mult, ALU.add).then_inc(root_in, 1)
                eng.wait_ge(root_out, roots[0])

            def norm(k):
                for t in range(TILES):
                    c = TILES * k + t
                    eng.wait_ge(squared, c + 1)
                    rsqrt(rstd[:, c:c + 1], ss[:, c:c + 1], D)
                    eng.wait_ge(gain_loaded, 16 * GB[k])
                    eng.scalar_tensor_tensor(tok[:, t, :], res[:, t, :], rstd[:, c:c + 1], gain[:, :],
                                             ALU.mult, ALU.mult).then_inc(normed, 1)

            def t8_copy(u, dst):
                for t in range(TILES):
                    eng.wait_ge(t8_d, TILES * u + t + 1)
                    eng.tensor_copy(dst[:, 4:8, t * P:(t + 1) * P],
                                    PS[:, 5 + 2 * t, :].rearrange("p (k q) -> p k q", q=P)).then_inc(t8c_d, 1)

            def pT_copy(key):
                for b in range(0, PT_BANKS[key], 2):
                    eng.wait_ge(pT_ps, PT_BASE[key] + b + 1)
                    n = 4
                    eng.tensor_copy(flat(PT[:, 4 * b:4 * b + n, :]), PS[:, 4 + b % 4, :]).then_inc(pT_d, 1)

            def add_to_residual(v):
                for h in range(HALVES):
                    for t in range(TILES):
                        x = res[:, t, h * HALF:(h + 1) * HALF]
                        eng.wait_ge(gemm, 4 * v + TILES * h + t + 1)
                        eng.tensor_tensor(x, x, PS[:, 2 * h + t, :], ALU.add).then_inc(gemm_used, 1)

            link(eng.memset(rt8[:, :, 0, :], -3e38))
            norm(N1)
            eng.wait_ge(vec_T, 1)
            link(eng.tensor_copy(vec[:, :], PS[:, 0, 0:V_ROWS]))
            for c, n, f in ((V_BQ, 8, SCALE), (V_QK, 1, SCALE), (V_QK + 2, 1, SCALE)):
                link(eng.tensor_scalar(vec[:, c:c + n], vec[:, c:c + n], f, None, ALU.mult))
            eng.tensor_scalar(vec[:, V_SUB:V_SUB + 1], vec[:, V_SUB:V_SUB + 1], 1.0 - LAMBDA_INIT, None,
                              ALU.mult).then_inc(vec_ready, 1)
            t8_copy(T_N1, hT)
            eng.wait_ge(rel_loaded, 32)
            eng.wait_ge(consts, 1)
            eng.tensor_copy(relb[:, :, :], wide(relx[:, :], P)).then_inc(rel_wide, 1)
            eng.wait_ge(lam_loaded, 64)
            for n in range(2):
                ins = eng.tensor_tensor_reduce(lam_rows[:, 2 * n, :], lam_rows[:, 2 * n, :], lam_rows[:, 2 * n + 1, :], 1.0, 0.0,
                                               ALU.mult, ALU.add, lam[:, n:n + 1])
            ins.then_inc(lam_sum, 1)
            for h in range(N_BIAS):
                eng.wait_ge(bias_ps, h + 1)
                eng.tensor_copy(bias_stage[:, h, :], PS[:, 2 + h % 2, 0:DIST_COLS]).then_inc(bias_copied, 1)
            eng.wait_ge(lam_exp, 1)
            link(eng.tensor_tensor(lam[:, 4:5], lam[:, 2:3], lam[:, 3:4], ALU.subtract))
            link(eng.tensor_scalar(lam[:, 5:6], lam[:, 4:5], LAMBDA_INIT, -1.0, ALU.add, ALU.mult))
            eng.wait_ge(if_loaded, 48)
            link(eng.tensor_copy(sink[:, :].rearrange("p (g i m) -> p g m i", g=2, i=4),
                                 sink_nat[:, :].rearrange("p (g m i) -> p g m i", g=2, m=2)))

            n = 0
            for c in range(6):
                for t in range(TILES):
                    j = TILES * c + t
                    bank = PS[:, j % 4, :]
                    if c in (2, 5):
                        eng.wait_ge(proj, j + 1)
                        lo = 0 if c == 2 else HALF
                        eng.tensor_copy(vals[:, t, lo:lo + HALF], bank).then_inc(proj_used, 1)
                        continue
                    eng.wait_ge(proj_sq, n + 1)
                    eng.tensor_reduce(hs[:, 0, 0:8], tok[:, t, HALF:].rearrange("p (h d) -> p h d", d=HEAD),
                                      AX_X, ALU.add).then_inc(proj_sq_read, 1)
                    eng.wait_ge(proj_sq_read, n + 1)
                    rsqrt(hs[:, 1, 0:8], hs[:, 0, 0:8], HEAD)
                    if n >= 2:
                        eng.wait_ge(qk_ps, n - 1)
                    eng.tensor_tensor(tok[:, t, 0:HALF].rearrange("p (h d) -> p h d", d=HEAD),
                                      bank.rearrange("p (h d) -> p h d", d=HEAD), wide(hs[:, 1, 0:8], HEAD),
                                      ALU.mult).then_inc(proj_used, 1)
                    n += 1

            eng.wait_ge(bias_loaded, 16)
            for t in range(TILES):
                n = P * (t + 1)
                for g in range(8):
                    eng.wait_ge(score, 8 * t + g + 1)
                    b = 2 * (g % 2)
                    if g < 4:
                        add = bias[:, g:g + 1, SEQ - n:].broadcast_to([P, 2, n])
                    else:
                        add = bias[:, DIFF_HEADS + 2 * (g - 4):DIFF_HEADS + 2 * (g - 4) + 2, SEQ - n:]
                    eng.tensor_tensor(L[:, 2 * g:2 * g + 2, 0:n], PS[:, b:b + 2, 0:n], add, ALU.add).then_inc(score_used, 1)
                eng.wait_ge(score_used, 8 * (t + 1))
                link(eng.tensor_reduce(hs[:, 0, :], L[:, :, 0:n], AX_X, ALU.max))
                eng.tensor_scalar(hs[:, 1, :], hs[:, 0, :], -1.0, None, ALU.mult).then_inc(maxed, 1)
                eng.wait_ge(expd, MAPS * (t + 1))
                link(eng.reciprocal(hs[:, 5, :], hs[:, 2, :]))
                link(eng.tensor_scalar(hs[:, 6, 0:4], hs[:, 5, 1:8:2], lam[:, 5:6], None, ALU.mult))
                for j in range(DIFF_HEADS):
                    ins = eng.tensor_scalar(L[:, 2 * j, 0:n], L[:, 2 * j, 0:n], hs[:, 5, 2 * j:2 * j + 1], None, ALU.mult)
                link(ins)
                for j in range(DIFF_HEADS):
                    eng.scalar_tensor_tensor(L[:, 2 * j, 0:n], L[:, 2 * j + 1, 0:n], hs[:, 6, j:j + 1], L[:, 2 * j, 0:n],
                                             ALU.mult, ALU.add).then_inc(weighted, 1)
                pT_copy((0, t))
                eng.wait_ge(pv_sq, t + 1)
                link(eng.tensor_reduce(hs[:, 7, 0:4], flat(L[:, 0:2, :]).rearrange("p (h c) -> p h c", h=4), AX_X, ALU.add))
                rsqrt(hs[:, 7, 4:8], hs[:, 7, 0:4], 2 * HEAD)
                eng.tensor_tensor(tok[:, t, 0:HALF].rearrange("p (h c) -> p h c", h=4),
                                  PS[:, 0, :].rearrange("p (h c) -> p h c", h=4), wide(hs[:, 7, 4:8], P),
                                  ALU.mult).then_inc(mixed, 1)
                eng.wait_ge(pv, 2 * t + 2)
                eng.tensor_tensor(tok[:, t, HALF:].rearrange("p (h c) -> p h c", h=8),
                                  PS[:, 1, :].rearrange("p (h c) -> p h c", h=8), wide(hs[:, 5, 8:16], HEAD),
                                  ALU.mult).then_inc(mixed, 1)
            t8_copy(T_Y, yT)
            add_to_residual(G_OUT)

            norm(N2)
            t8_copy(T_N2, hT)
            for t in range(TILES):
                r, top, idx = rt[:, t, :], rt8[:, t], rt8u[:, t]
                eng.wait_ge(route, t + 1)
                link(eng.tensor_copy(top[:, 0, 0:GROUPS], PS[:, t, 0:GROUPS]))
                link(eng.max(top[:, 1, :], top[:, 0, :]))
                link(eng.max_index(idx[:, 0, :], top[:, 1, :], top[:, 0, :]))
                link(eng.tensor_copy(r[:, 88:89], idx[:, 0, 0:1]))
                link(eng.tensor_scalar(r[:, 84:85], top[:, 1, 0:1], -1.0, None, ALU.mult))
                link(eng.tensor_scalar(r[:, 40:44], iota[:, 0:GROUPS], r[:, 88:89], None, ALU.is_equal))
                link(eng.tensor_tensor(r[:, 8:40].rearrange("p (g e) -> p g e", g=GROUPS),
                                       PS[:, t, GROUPS:ROUTES].rearrange("p (g e) -> p g e", g=GROUPS),
                                       wide(r[:, 40:44], PER_GROUP), ALU.mult))
                link(eng.tensor_reduce(r[:, 0:8], r[:, 8:40].rearrange("p (g e) -> p e g", g=GROUPS), AX_X, ALU.add))
                link(eng.max(top[:, 2, :], r[:, 0:8]))
                link(eng.max_index(idx[:, 1, :], top[:, 2, :], r[:, 0:8]))
                eng.tensor_tensor(r[:, 87:88], top[:, 2, 1:2], top[:, 2, 0:1], ALU.subtract).then_inc(route_exp_in, 1)
                link(eng.tensor_copy(r[:, 89:91], idx[:, 1, 0:2]))
                link(eng.tensor_scalar(r[:, 91:92], r[:, 88:89], float(PER_GROUP), None, ALU.mult))
                link(eng.tensor_scalar(r[:, 89:91], r[:, 89:91], r[:, 91:92], None, ALU.add))
                for c in range(2):
                    ins = eng.tensor_scalar(assign[:, t, c, :], iota[:, 0:EXPERTS], r[:, 89 + c:90 + c], None, ALU.is_equal)
                link(ins)
                eng.tensor_tensor(assign[:, t, 2, :], assign[:, t, 0, :], assign[:, t, 1, :], ALU.add).then_inc(assigned, 1)
            for t in range(TILES):
                eng.wait_ge(pos_ps, t + 1)
                link(eng.tensor_copy(posn[:, t, 0, :], PS[:, 2 + t, 0:EXPERTS]))
                link(eng.scalar_tensor_tensor(posn[:, t, 1, :], posn[:, t, 0, :], 1.0, assign[:, t, 2, :], ALU.add, ALU.mult))
                link(eng.tensor_scalar(posn[:, t, 1, :], posn[:, t, 1, :], -1.0, None, ALU.add))
                eng.tensor_tensor(select[:, t], iota[:, :].unsqueeze(1).broadcast_to([P, EXPERTS, SLOTS]),
                                  wide(posn[:, t, 1, :], SLOTS), ALU.is_equal).then_inc(selected, 1)
            eng.wait_ge(slot_ps, 1)
            eng.tensor_copy(slot_tok[:, :], PS[:, 0, 0:PAIRS]).then_inc(slot_ready, 1)
            eng.wait_ge(pos_ps, TILES + 1)
            link(eng.tensor_reduce(most_f[:, :], PS[:, 2, HALF - EXPERTS:], AX_X, ALU.max))
            eng.tensor_copy(most[:, :], most_f[:, :]).then_inc(counted, 1)
            for t in range(TILES):
                r = rt[:, t, :]
                for c in range(2):
                    link(eng.tensor_tensor_reduce(posn[:, t, 2, :], posn[:, t, 0, :], assign[:, t, c, :], 1.0, 0.0,
                                                  ALU.mult, ALU.add, r[:, 44 + c:45 + c]))
                link(eng.tensor_scalar(r[:, 42:44], r[:, 44:46], float(SLOTS - 1), None, ALU.min))
                link(eng.tensor_scalar(r[:, 48:50], r[:, 44:46], float(SLOTS), None, ALU.is_lt))
                link(eng.scalar_tensor_tensor(r[:, 46:48], r[:, 89:91], float(SLOTS), r[:, 42:44], ALU.mult, ALU.add))
                link(eng.tensor_copy(row_u[:, 2 * t:2 * t + 2], r[:, 46:48]))
                eng.wait_ge(route_exp, t + 1)
                link(eng.reciprocal(r[:, 91:92], r[:, 85:86]))
                link(eng.tensor_scalar(r[:, 94:95], r[:, 86:87], 1.0, None, ALU.add))
                link(eng.reciprocal(r[:, 95:96], r[:, 94:95]))
                link(eng.tensor_tensor(r[:, 92:93], r[:, 91:92], r[:, 95:96], ALU.mult))
                link(eng.tensor_tensor(r[:, 93:94], r[:, 92:93], r[:, 86:87], ALU.mult))
                ins = eng.tensor_tensor(r[:, 50:52], r[:, 92:94], r[:, 48:50], ALU.mult)
                if t < TILES - 1:
                    link(ins)
            ins.then_inc(rows_ready, 1)

            def expert_pair(i, it, u, early):
                eng.wait_ge(exT_d, i + 1)
                if not early:
                    eng.wait_ge(ex_gu, i - 1)
                eng.tensor_copy(flat(xgT[:, u, 4:8, :]), PS[:, 7, :]).then_inc(exTc_d, 1)
                eng.wait_ge(ex_act, i + 1)
                if not early:
                    eng.wait_ge(ex_hT, i - 1)
                eng.tensor_tensor(hid_e[:, u, :], act_e[:, u, :], PS[:, 4 + u, HIDDEN:], ALU.mult).then_inc(ex_hid, 1)
                eng.wait_ge(ex_hT, i + 1)
                if not early:
                    eng.wait_ge(weights_used, i * 2 - 2)
                eng.tensor_copy(flat(hidT_e[:, u]), PS[:, 6, 0:HIDDEN]).then_inc(ex_hTc, 1)
                eng.wait_ge(weights_used, i * 2 + 2)
                if not early:
                    eng.wait_ge(ex_stored[u], it * 16)
                eng.tensor_copy(exo[:, u, HALF:], PS[:, 2 * u + 1, :]).then_inc(ex_out_d, 1)

            for u in range(2):
                expert_pair(u, 0, u, True)
            with eng.Fori(1, PAIRS // 2) as it:
                for u in range(2):
                    expert_pair(it * 2 + u, it, u, False)
            for t in range(TILES):
                for c in range(2):
                    n = 2 * t + c
                    eng.wait_ge(row_gathered[n], 16)
                    ins = eng.scalar_tensor_tensor(res[:, t, :], routed[:, n, :], rt[:, t, 50 + c:51 + c], res[:, t, :],
                                                   ALU.mult, ALU.add)
                    link(ins)
            with overflow(eng):
                with eng.Fori(0, ROUNDS - 1) as r:
                    for t in range(TILES):
                        eng.tensor_scalar(posn[:, t, 1, :], posn[:, t, 1, :], -float(SLOTS), None, ALU.add).then_inc(ov_step, 1)
                    with eng.Fori(0, PAIRS) as i:
                        j = r * PAIRS + i
                        eng.wait_ge(ov_step, OV_STEPS * r + 2)
                        for t in range(TILES):
                            ins = eng.tensor_tensor(select[:, t, 0:2, :], iota[:, :].unsqueeze(1).broadcast_to([P, 2, SLOTS]),
                                                    wide(posn[:, t, 1, bass.ds(2 * i, 2)], SLOTS), ALU.is_equal)
                        ins.then_inc(ov_sel, 1)
                        eng.wait_ge(ov_slot_ps, j + 1)
                        eng.tensor_copy(slot_tok[:, 0:1], PS[:, 0, 0:1]).then_inc(ov_slot, 1)
                        eng.wait_ge(ov_xT, j + 1)
                        for b in range(2):
                            ins = eng.tensor_copy(flat(xgT[:, 0, 4 * b:4 * b + 4, :]), PS[:, 6 + b, :])
                        ins.then_inc(ov_xTc, 1)
                        eng.wait_ge(ov_act, j + 1)
                        eng.tensor_tensor(hid_e[:, 0, :], act_e[:, 0, :], PS[:, 4, HIDDEN:], ALU.mult).then_inc(ov_hid, 1)
                        eng.wait_ge(ov_hT, j + 1)
                        eng.tensor_copy(flat(hidT_e[:, 0]), PS[:, 6, 0:HIDDEN]).then_inc(ov_hTc, 1)
                        eng.wait_ge(ov_down, j + 1)
                        for h in range(HALVES):
                            ins = eng.tensor_copy(exo[:, 0, h * HALF:(h + 1) * HALF], PS[:, h, :])
                        ins.then_inc(ov_out, 1)
                        eng.wait_ge(ov_stored, 16 * j + 16)
                    for t in range(TILES):
                        q = rt[:, t, :]
                        steps = [lambda: eng.tensor_scalar(q[:, 44:46], q[:, 44:46], -float(SLOTS), None, ALU.add),
                                 lambda: eng.tensor_scalar(q[:, 42:44], q[:, 44:46], float(SLOTS - 1), 0.0, ALU.min, ALU.max),
                                 lambda: eng.tensor_scalar(q[:, 48:50], q[:, 44:46], float(SLOTS), None, ALU.is_lt),
                                 lambda: eng.tensor_scalar(q[:, 52:54], q[:, 44:46], 0.0, None, ALU.is_ge),
                                 lambda: eng.tensor_tensor(q[:, 48:50], q[:, 48:50], q[:, 52:54], ALU.mult),
                                 lambda: eng.tensor_tensor(q[:, 50:52], q[:, 92:94], q[:, 48:50], ALU.mult),
                                 lambda: eng.scalar_tensor_tensor(q[:, 46:48], q[:, 89:91], float(SLOTS), q[:, 42:44],
                                                                  ALU.mult, ALU.add)]
                        for n, step in enumerate(steps):
                            step().then_inc(ov_step, 1)
                            eng.wait_ge(ov_step, OV_STEPS * r + 2 + 7 * t + n + 1)
                        ins = eng.tensor_copy(row_u[:, 2 * t:2 * t + 2], q[:, 46:48])
                    ins.then_inc(ov_rows, 1)
                    eng.wait_ge(ov_routed, 64 * r + 64)
                    for n in range(2 * TILES):
                        t, c = n // 2, n % 2
                        eng.scalar_tensor_tensor(res[:, t, :], routed[:, n, :], rt[:, t, 50 + c:51 + c], res[:, t, :],
                                                 ALU.mult, ALU.add).then_inc(ov_added, 1)
                        eng.wait_ge(ov_added, 4 * r + n + 1)
            eng.tensor_copy(most_f[:, :], ones[:, 0:1]).then_inc(moe_added, 1)

            def ffn(f):
                for c in range(CHUNKS + 1):
                    n = f * CHUNKS + c
                    for t in range(TILES):
                        if c < CHUNKS:
                            eng.wait_ge(ff_act, TILES * n + t + 1)
                            if n >= 2:
                                eng.wait_ge(ff_hT, n - 1)
                            eng.tensor_tensor(hid_f[:, c % 2, t, :], act_f[:, c % 2, t, :], PS[:, 4 + t, HIDDEN:],
                                              ALU.mult).then_inc(ff_hid, 1)
                        if t == 0 and c >= 1:
                            eng.wait_ge(ff_hT, n)
                            eng.tensor_copy(flat(hidT_f[:, (c - 1) % 2]), PS[:, 6 + (n - 1) % 2, :]).then_inc(ff_hTc, 1)
                eng.wait_ge(weights_used, EXPERTS + CHUNKS * (f + 1))
                for t in range(TILES):
                    for h in range(HALVES):
                        x = res[:, t, h * HALF:(h + 1) * HALF]
                        eng.scalar_tensor_tensor(x, PS[:, 2 * t + h, :], 0.5, x, ALU.mult, ALU.add).then_inc(ff_added, 1)

            norm(NF1)
            t8_copy(T_F1, hT)
            ffn(0)

            norm(NMIX)
            t8_copy(T_MIX, hT)
            eng.wait_ge(bb_loaded, 32)
            eng.wait_ge(t8c_a, TILES * (T_MIX + 1))
            eng.memset(raw[:, :, 0:CONV - 1], 0.0).then_inc(pad_zeroed, 1)
            for n, (kind, g, i) in enumerate(Z):
                if kind == "m":
                    eng.wait_ge(z_act, sum(by_act[:n + 1]))
                    if i == 0:
                        eng.wait_ge(pad_zeroed, 1)
                    if i >= 2:
                        eng.wait_ge(conv_silu, i - 1)
                    acc = conv[:, i % 2, :]
                    tap = lambda j: vec[:, V_CONV + 8 * j + i:V_CONV + 8 * j + i + 1]
                    link(eng.tensor_scalar(acc, raw[:, i % 2, 0:SEQ], tap(0), None, ALU.mult))
                    for j in range(1, CONV):
                        ins = eng.scalar_tensor_tensor(acc, raw[:, i % 2, j:j + SEQ], tap(j), acc, ALU.mult, ALU.add)
                        if j < CONV - 1:
                            link(ins)
                    ins.then_inc(conv_done, 1)
                if by_act[n]:
                    continue
                eng.wait_ge(z_unit, n + 1)
                bank = PS[:, n % ZB, :]
                if kind == "av":
                    dst, src, add = sv[:, i, :], bank[:, 0:256], bias_av
                elif kind == "if":
                    dst, src, add = ga[:, i, 0, :], bank[:, 0:16], b_if[:, :]
                else:
                    lo = (g - 5) % 2 * HALF
                    dst, src = (mv if kind == "mv" else mo)[:, i, lo:lo + HALF], bank
                    add = bias_mvo[:, (g - 5) * HALF:(g - 4) * HALF]
                eng.tensor_tensor(dst, src, add, ALU.add).then_inc(z_dve, 1)
            for t in range(TILES):
                G = ga[:, t]
                e = G[:, 2, 8:16]
                eng.wait_ge(gates_exp, 2 * t + 1)
                eng.tensor_scalar(G[:, 3, 0:8], e, 1.0, None, ALU.add).then_inc(gates_u, 1)
                eng.wait_ge(gates_u, t + 1)
                link(eng.tensor_scalar(G[:, 4, 0:8], G[:, 3, 0:8], -1.0, None, ALU.add))
                link(eng.tensor_scalar(G[:, 4, 8:16], G[:, 4, 0:8], 0.0, None, ALU.is_equal))
                link(eng.tensor_tensor(G[:, 5, 0:8], G[:, 4, 0:8], G[:, 4, 8:16], ALU.add))
                link(eng.reciprocal(G[:, 5, 8:16], G[:, 5, 0:8]))
                eng.wait_ge(gates_exp, 2 * t + 2)
                link(eng.tensor_tensor(G[:, 5, 8:16], G[:, 5, 8:16], G[:, 3, 8:16], ALU.mult))
                link(eng.tensor_tensor(G[:, 5, 8:16], G[:, 5, 8:16], G[:, 4, 8:16], ALU.add))
                link(eng.tensor_scalar(G[:, 6, 0:8], G[:, 1, 0:8], SOFTCAP, None, ALU.mult))
                eng.scalar_tensor_tensor(G[:, 6, 8:16], G[:, 5, 8:16], -1.0, e, ALU.mult, ALU.mult).then_inc(gates_ready, 1)
            for t in range(TILES):
                G = ga[:, t]
                eng.wait_ge(cum_ps, t + 1)
                link(eng.tensor_copy(G[:, 7, 0:8], PS[:, t, 0:8]))
                eng.tensor_tensor(G[:, 7, 8:16], G[:, 6, 0:8], G[:, 7, 0:8], ALU.subtract).then_inc(a_ready, 1)
            eng.wait_ge(a_ps, 1)
            eng.tensor_copy(aT[:, :], PS[0:8, 2, 0:SEQ]).then_inc(a_copied, 1)

            for t in range(TILES):
                n = P * (t + 1)
                mask = prev_causal[:, SEQ - n:].unsqueeze(1).broadcast_to([P, 2, n])
                for g in range(8):
                    eng.wait_ge(score, 16 + 8 * t + g + 1)
                    b = 2 * (g % 2)
                    eng.tensor_tensor(L[:, 2 * g:2 * g + 2, 0:n], PS[:, b:b + 2, 0:n], mask, ALU.add).then_inc(score_used, 1)
                eng.wait_ge(score_used, 16 + 8 * (t + 1))
                link(eng.tensor_reduce(hs[:, 0, :], L[:, :, 0:n], AX_X, ALU.max))
                link(eng.tensor_tensor(hs[:, 0, :], hs[:, 0, :], sink[:, :], ALU.max))
                link(eng.tensor_scalar(hs[:, 1, :], hs[:, 0, :], -1.0, None, ALU.mult))
                eng.tensor_tensor(hs[:, 3, :], sink[:, :], hs[:, 0, :], ALU.subtract).then_inc(maxed, 1)
                pT_copy((1, t))
                eng.wait_ge(sink_exp, t + 1)
                link(eng.tensor_tensor(hs[:, 5, :], hs[:, 2, :], hs[:, 4, :], ALU.add))
                link(eng.reciprocal(hs[:, 6, :], hs[:, 5, :]))
                for g in range(2):
                    eng.wait_ge(pv, 4 + 2 * t + g + 1)
                    inv = hs[:, 6, 8 * g:8 * g + 8].rearrange("p (i m) -> p m i", m=2)
                    eng.tensor_tensor(tok[:, t, g * HALF:(g + 1) * HALF].rearrange("p (m i c) -> p m i c", m=2, i=4),
                                      PS[:, g, :].rearrange("p (m i c) -> p m i c", m=2, i=4), wide(inv, HEAD),
                                      ALU.mult).then_inc(mixed, 1)
            t8_copy(T_SY, yT)

            for t in range(TILES):
                n = P * (t + 1)
                mask = zero_causal[:, SEQ - n:].unsqueeze(1).broadcast_to([P, 2, n])
                for j in range(4):
                    eng.wait_ge(ml_a, 4 * t + j + 1)
                    eng.tensor_tensor(L[:, 2 * j:2 * j + 2, 0:n], PS[:, j, :].rearrange("p (m k) -> p m k", m=2)[:, :, 0:n],
                                      mask, ALU.add).then_inc(ml_used, 1)
                eng.wait_ge(ml_used, 4 * (t + 1))
                link(eng.tensor_reduce(hs[:, 0, 0:8], L[:, 0:8, 0:n], AX_X, ALU.max))
                link(eng.tensor_scalar(hs[:, 0, 0:8], hs[:, 0, 0:8], 0.0, None, ALU.max))
                link(eng.tensor_scalar(hs[:, 1, 0:8], hs[:, 0, 0:8], -1.0, None, ALU.mult))
                eng.tensor_tensor(hs[:, 4, 0:8], ga[:, t, 7, 0:8], hs[:, 0, 0:8], ALU.add).then_inc(ml_max, 1)
                for a in range(MLSTM_HEADS):
                    eng.wait_ge(ml_exp, 9 * t + a + 1)
                    eng.wait_ge(ml_s, 4 * t + a // 2 + 1)
                    eng.scalar_tensor_tensor(L[:, a, 0:n], PS[:, 2 * (a // 2 % 2) + a % 2, 0:n], SCALE, L[:, a, 0:n],
                                             ALU.mult, ALU.mult, accum_out=hs[:, 2, a:a + 1]).then_inc(ml_sc, 1)
                pT_copy((2, t))
                eng.wait_ge(ml_exp, 9 * t + 9)
                eng.wait_ge(ml_sc, 8 * (t + 1))
                link(eng.tensor_scalar(hs[:, 6, 0:8], hs[:, 2, 0:8], -1.0, None, ALU.mult))
                link(eng.tensor_tensor(hs[:, 6, 0:8], hs[:, 6, 0:8], hs[:, 2, 0:8], ALU.max))
                link(eng.tensor_tensor(hs[:, 6, 0:8], hs[:, 6, 0:8], hs[:, 5, 0:8], ALU.max))
                link(eng.reciprocal(hs[:, 7, 0:8], hs[:, 6, 0:8]))
                for b in range(2):
                    eng.wait_ge(pv, 8 + 2 * t + b + 1)
                    ins = eng.tensor_tensor(tok[:, t, b * HALF:(b + 1) * HALF].rearrange("p (h v) -> p h v", h=4),
                                            PS[:, b, :].rearrange("p (h v) -> p h v", h=4), wide(hs[:, 7, 4 * b:4 * b + 4], P),
                                            ALU.mult)
                ins.then_inc(ml_h, 1)
                eng.wait_ge(ml_hsq, t + 1)
                link(eng.tensor_reduce(hs[:, 3, 0:8], flat(L[:, 0:4, :]).rearrange("p (h v) -> p h v", h=8), AX_X, ALU.add))
                rsqrt(hs[:, 3, 8:16], hs[:, 3, 0:8], V_DIM)
                rows = tok[:, t, :].rearrange("p (h v) -> p h v", h=8)
                link(eng.tensor_tensor(rows, rows, wide(hs[:, 3, 8:16], P), ALU.mult))
                eng.wait_ge(sig_done, t + 1)
                link(eng.tensor_tensor(tok[:, t, :], tok[:, t, :], mo[:, t, :], ALU.mult))
                eng.wait_ge(gain_loaded, 16 * GB["hm"])
                eng.tensor_tensor(tok[:, t, :], tok[:, t, :], gain[:, :], ALU.mult).then_inc(mixed, 1)
            t8_copy(T_HM, hmT)

            eng.wait_ge(bb_loaded, 48)
            for n, (_, g, t) in enumerate(ZG):
                lo = (g - 9) * HALF
                eng.wait_ge(z_unit, len(Z) + n + 1)
                eng.tensor_tensor(gates[:, t, lo:lo + HALF], PS[:, n % ZB, :], bias_g[:, lo:lo + HALF], ALU.add).then_inc(g_sig, 1)
            for v in (G_PA, G_PM):
                for h in range(HALVES):
                    for t in range(TILES):
                        x = tok[:, t, h * HALF:(h + 1) * HALF]
                        lo = (v - G_PA) * D + h * HALF
                        g = gates[:, t, lo:lo + HALF]
                        eng.wait_ge(sig_done, TILES + len(ZG))
                        eng.wait_ge(gemm, 4 * v + TILES * h + t + 1)
                        if v == G_PA:
                            eng.tensor_tensor(x, PS[:, 2 * h + t, :], g, ALU.mult).then_inc(gemm_used, 1)
                        else:
                            eng.tensor_tensor(g, PS[:, 2 * h + t, :], g, ALU.mult).then_inc(gemm_used, 1)
                            eng.wait_ge(gemm_used, 4 * v + TILES * h + t + 1)
                            eng.tensor_tensor(x, x, g, ALU.add).then_inc(merged, 1)
            t8_copy(T_MG, yT)
            add_to_residual(G_OUT2)
            norm(NF2)
            t8_copy(T_F2, hT)
            ffn(1)
            norm(NFIN)


_OUT = ((1, SEQ, D), "float32")


def kernel(**inputs):
    import concourse.bacc as _bacc
    from concourse.bass_utils import run_bass_kernel_spmd as _run

    nc = _bacc.Bacc("TRN2", target_bir_lowering=False, num_devices=1, dynamic_dma_scratch_size=8192)
    arrays, args = {}, {}
    for name, a in inputs.items():
        a = np.ascontiguousarray(a)
        arrays[f"in_{name}"] = a
        args[name] = nc.dram_tensor(f"in_{name}", a.shape, mybir.dt.from_np(a.dtype), kind="ExternalInput").ap()
    b = distance_buckets()
    arrays["in_buckets"] = b
    buckets = nc.dram_tensor("in_buckets", b.shape, F32, kind="ExternalInput").ap()
    out = nc.dram_tensor("out_0", _OUT[0], F32, kind="ExternalOutput").ap()
    two_blocks(nc, args, buckets, out)
    r = _run(nc, [arrays], core_ids=[0])
    return r.results[0]["out_0"]
```

```python
from contextlib import ExitStack

import numpy as np

import concourse.bass as bass
from concourse import mybir

F32 = mybir.dt.float32
F32R = mybir.dt.float32r
U32 = mybir.dt.uint32
I32 = mybir.dt.int32
ALU = mybir.AluOpType
ACT = mybir.ActivationFunctionType
AX_X = mybir.AxisListType.X

P = 128
SEQ = 256
TILES = SEQ // P
D = 1024
KT = D // P
HALF = 512
HALVES = D // HALF
HEAD = 64
EPS = 1e-6
MASKED = -1e30
SCALE = HEAD ** -0.5

DIFF_HEADS, MOBA_HEADS = 4, 8
MAPS = 2 * DIFF_HEADS + MOBA_HEADS
N_BIAS = DIFF_HEADS + MOBA_HEADS
BUCKETS, MAX_DISTANCE = 32, 2048
DIST_COLS = 384
LAMBDA_INIT = 0.8 - 0.6 * float(np.exp(-0.3 * 0))

GROUPS, PER_GROUP = 4, 8
EXPERTS = GROUPS * PER_GROUP
HIDDEN = 256
FT = HIDDEN // P
SLOTS = 64
ROUNDS = SEQ // SLOTS
PAIRS = EXPERTS // 2
ROUTES = GROUPS + EXPERTS

D_FF = ((8 * D // 3 + 127) // 128) * 128
CHUNKS = D_FF // HIDDEN
KV_HEADS, Q_HEADS = 4, 16
MLSTM_HEADS, V_DIM = 8, 128
SOFTCAP = 15.0
C_K, C_AV, C_MQ, C_MV, C_MO, C_IF, C_G, C_END = 1024, 1280, 1536, 2560, 3584, 4608, 4624, 6672

CONV = 4
V_BQ, V_BK, V_BM, V_CONV, V_QK, V_SUB, V_ROWS = 0, 8, 10, 18, 50, 54, 55
N_VEC = 4 + 1 + 1 + CONV + 8 + 1

RING = 4
PIECE = KT * HIDDEN
STEPS = 3
KH = KT // 2


def weight_pieces():
    def feed_forward(f):
        out = [(f, "gate", 0), (f, "up", 0)]
        for c in range(1, CHUNKS):
            out += [(f, "gate", c), (f, "down", c - 1), (f, "up", c)]
        return out + [(f, "down", CHUNKS - 1)]

    def cols(src, n):
        return [(src, c, kh) for c in range(n) for kh in range(2)]

    p = cols("w_in", 6) + cols("w_out", 2) + feed_forward("ffn1") + cols("w_in_2", 13)
    for w in ("w_proj_attn", "w_proj_mlstm", "w_out_2"):
        p += cols(w, 2)
    return p + feed_forward("ffn2")


def distance_buckets():
    out = np.zeros((BUCKETS + 1, DIST_COLS), np.float32)
    exact = BUCKETS // 2
    for m in range(DIST_COLS):
        n = SEQ - 1 - m
        if n < 0:
            out[BUCKETS, m] = 1
        elif n < exact:
            out[n, m] = 1
        else:
            large = np.log(np.float32(n) / np.float32(exact)) / np.log(MAX_DISTANCE / exact) * (BUCKETS - exact)
            out[min(exact + int(large), BUCKETS - 1), m] = 1
    return out


def two_blocks(nc, A, buckets, out):
    PIECES = weight_pieces()
    first = {}
    for n, (src, _, _) in enumerate(PIECES):
        first.setdefault(src, n)
    BEFORE_MOE = first["ffn1"]

    with ExitStack() as ctx:
        def sb(name, shape, dt=F32):
            return ctx.enter_context(nc.sbuf_tensor(name, shape, dt))

        def sem(name):
            return ctx.enter_context(nc.semaphore(name))

        PS = ctx.enter_context(nc.psum_tensor("banks", [P, 8, HALF], F32))

        bias_rows = nc.dram_tensor("bias_rows", [N_BIAS, P, DIST_COLS], F32, kind="Internal").ap()

        raw_w = sb("raw_weights", [P, STEPS * PIECE])
        with ExitStack() as room:
            w_hi = room.enter_context(nc.sbuf_tensor("weights_hi", [P, STEPS, PIECE], F32R))
            w_lo = room.enter_context(nc.sbuf_tensor("weights_lo", [P, STEPS, PIECE], F32R))
        expert_room = sb("expert_weights", [P, 2 * STEPS * PIECE])
        res = sb("residual", [P, TILES, D])
        tok = sb("token_major", [P, TILES, D])
        hT = [sb(f"normed_T_{part}", [P, KT, SEQ], F32R) for part in ("hi", "lo")]
        with ExitStack() as room:
            yT = [room.enter_context(nc.sbuf_tensor(f"mixed_T_{part}", [P, KT, SEQ], F32R)) for part in ("hi", "lo")]
        conv_room = sb("conv_room", [P, 2 * KT * SEQ])
        tok_parts = [y[:, :, :].rearrange("p k q -> p (k q)").rearrange("p (t k d) -> p t k d", t=TILES, k=KT) for y in yT]
        with ExitStack() as room:
            def part(name, shape, dt=F32R):
                return room.enter_context(nc.sbuf_tensor(name, shape, dt))

            part("room_of_activations", [P, 2048], F32)
            hidT_f = [part(f"ffn_hidden_T_{x}", [P, FT, SEQ]) for x in ("hi", "lo")]
            part("room_of_expert", [P, 3 * PIECE - 2048 - 2 * FT * SEQ], F32)
            sel = part("select", [P, TILES, RING * SLOTS])
            selT = part("select_T", [P, 2, SEQ])
            exo = [part(f"expert_out_{x}", [P, D]) for x in ("hi", "lo")]
        STAGE = sb("stage", [P, 9216 + 2 * 16 * SEQ])
        AR = STAGE[:, 0:9216]
        LP = STAGE[:, 9216:]
        def blocks(where, lo, n, width):
            return where[:, lo:lo + n * width].rearrange("p (a k) -> p a k", a=n)

        L = [blocks(conv_room, 0, 16, P), blocks(LP, 0, 16, SEQ)]
        PT = [blocks(conv_room, 16 * P, 16, P), blocks(LP, 16 * SEQ, 32, P)]
        ML = [blocks(LP, 0, 8, P), blocks(LP, 8 * P, 8, SEQ)]
        MPT = [blocks(LP, 16 * SEQ, 8, P), blocks(LP, 16 * SEQ + 8 * P, 16, P)]
        head_squares = LP[:, 3 * D:4 * D]
        ring = [raw_w[:, :], expert_room[:, 0:3 * PIECE], expert_room[:, 3 * PIECE:], AR[:, 0:3 * PIECE]]

        def view(lo, *dims):
            n = int(np.prod(dims))
            names = " ".join("abc"[:len(dims)])
            return AR[:, lo:lo + n].rearrange(f"p ({names}) -> p {names}", **dict(zip("abc", dims)))

        qkT = [view(1024 * n, 4, SEQ) for n in range(4)]
        vals = view(4096, TILES, D)
        bias = view(6144, N_BIAS, SEQ)
        bias_stage = LP[:, 0:N_BIAS * DIST_COLS].rearrange("p (h m) -> p h m", h=N_BIAS)
        BS = N_BIAS * DIST_COLS
        relb = LP[0:BUCKETS + 1, BS:BS + N_BIAS * P].rearrange("p (h q) -> p h q", h=N_BIAS)
        onehot = LP[0:BUCKETS + 1, BS + N_BIAS * P:BS + N_BIAS * P + DIST_COLS]
        lam_rows = LP[:, BS + N_BIAS * P + DIST_COLS:BS + N_BIAS * P + DIST_COLS + 4 * HEAD].rearrange("p (n d) -> p n d", n=4)
        xgT = LP[:, 0:KT * RING * SLOTS].rearrange("p (k s) -> p k s", k=KT)
        selw = LP[:, 4096:4096 + TILES * P].rearrange("p (t s) -> p t s", t=TILES)
        act_e = LP[:, 4608:4608 + HIDDEN]
        hid_e = LP[:, 5120:5120 + HIDDEN]
        hidT_e = LP[:, 5632:5632 + HIDDEN].rearrange("p (k s) -> p k s", k=FT)
        act_f, hid_f = view(0, TILES, HIDDEN), view(1024, TILES, HIDDEN)
        sqT, skT = view(0, 8, SEQ), view(2048, 2, SEQ)
        sv = view(2560, TILES, 256)
        mv, mo = view(3072, TILES, D), view(5120, TILES, D)
        mqk = view(7168, 8, SEQ)
        conv = conv_room[:, 0:2 * SEQ].rearrange("p (a b) -> p a b", a=2)
        raw = conv_room[:, 2 * SEQ:2 * SEQ + 2 * (SEQ + CONV)].rearrange("p (a b) -> p a b", a=2)[:, :, 1:]
        gates = LP[:, 0:4096].rearrange("p (t g) -> p t g", t=TILES)
        bias_av, bias_mvo = LP[:, 0:256], LP[:, 256:2304]
        bias_g = LP[:, 4096:6144]

        gain = sb("gain_rows", [P, D])
        ident = sb("ident", [P, P])
        ones = sb("ones", [P, P])
        upto = sb("upto", [P, P])
        before = sb("before", [P, P])
        masks = sb("masks", [P, 4 * P])
        zero_causal, prev_causal = masks[:, 0:256], masks[:, 256:512]
        vec_rows = sb("vec_rows", [V_ROWS, P])
        vec = sb("vec", [P, V_ROWS])
        relx = sb("rel_bias", [BUCKETS + 1, N_BIAS])
        lam = sb("lambda_parts", [P, 6])
        router = sb("router", [P, KT, ROUTES])
        router_parts = [sb(f"router_{x}", [P, KT, ROUTES], F32R) for x in ("hi", "lo")]
        w_if_parts = [sb(f"w_if_{x}", [P, KT, 16], F32R) for x in ("hi", "lo")]
        w_if, b_if = sb("w_if", [P, KT, 16]), sb("b_if", [P, 16])
        sink_nat, sink = sb("sink_natural", [P, Q_HEADS]), sb("sink", [P, Q_HEADS])
        iota_i, iota = sb("iota_int", [P, SLOTS], I32), sb("iota", [P, SLOTS])
        minus_half = sb("minus_half", [P, 8])
        ss = sb("square_sums", [P, 16])
        rstd = sb("rstd", [P, 16])
        hs = sb("head_stats", [P, TILES, 8, 16])
        rt = sb("route_stats", [P, TILES, 96])
        rt8 = sb("route_top", [P, TILES, 4, 8])
        rt8u = sb("route_top_index", [P, TILES, 2, 8], U32)
        assign = sb("assign", [P, TILES, 3, EXPERTS])
        posn = sb("position", [P, TILES, 3, EXPERTS])
        wtok = sb("token_weights", [P, TILES, EXPERTS])
        wslot = sb("slot_weights", [P, 1])
        most_f, most = sb("most_tokens_f", [P, 1]), sb("most_tokens", [P, 1], U32)
        ga = sb("gate_stats", [P, TILES, 8, 16])
        aT = sb("a_rows", [MLSTM_HEADS, SEQ])

        piece_loaded = [sem(f"piece_loaded{s}") for s in range(STEPS)]
        split_hi, split_lo, piece_used = sem("split_hi"), sem("split_lo"), sem("piece_used")
        gate_up_loaded = [sem(f"gate_up_loaded{s}") for s in range(RING)]
        down_loaded = [sem(f"down_loaded{s}") for s in range(RING)]
        x_loaded, vec_loaded, lam_loaded = sem("x_loaded"), sem("vec_loaded"), sem("lam_loaded")
        rel_loaded, router_loaded, if_loaded = sem("rel_loaded"), sem("router_loaded"), sem("if_loaded")
        gain_loaded, bias_loaded, bb_loaded = sem("gain_loaded"), sem("bias_loaded"), sem("bb_loaded")
        bias_stored = sem("bias_stored")
        out_stored = sem("out_stored")
        pool_seq, dve_seq, act_seq = sem("pool_seq"), sem("dve_seq"), sem("act_seq")
        consts, root_in, root_out = sem("consts"), sem("root_in"), sem("root_out")
        vec_T, vec_ready, rel_wide = sem("vec_T"), sem("vec_ready"), sem("rel_wide")
        bias_ps, bias_copied = sem("bias_ps"), sem("bias_copied")
        squared, normed = sem("squared"), sem("normed")
        t8, t8_hi, t8_lo = sem("t8"), sem("t8_hi"), sem("t8_lo")
        small_hi, small_lo = sem("small_hi"), sem("small_lo")
        proj_sq, proj_used = sem("proj_sq"), sem("proj_used")
        proj_sq_read = sem("proj_sq_read")
        qk_ps, qk_done = sem("qk_ps"), sem("qk_done")
        score, score_used, maxed, expd = sem("score"), sem("score_used"), sem("maxed"), sem("expd")
        lam_sum, lam_exp = sem("lam_sum"), sem("lam_exp")
        weighted = sem("weighted")
        pT_ps, pT_a, pT_d = sem("pT_ps"), sem("pT_a"), sem("pT_d")
        pv, pv_sq, mixed = sem("pv"), sem("pv_sq"), sem("mixed")
        gemm_used = sem("gemm_used")
        route, route_exp_in, route_exp, assigned = sem("route"), sem("route_exp_in"), sem("route_exp"), sem("assigned")
        pos_ps, tok_hi, tok_lo, weighed = sem("pos_ps"), sem("tok_hi"), sem("tok_lo"), sem("weighed")
        sel_ready, ex_gath, ex_xT = sem("sel_ready"), sem("ex_gath"), sem("ex_xT")
        ex_gu, ex_act, ex_hid, ex_hT, ex_hTc = sem("ex_gu"), sem("ex_act"), sem("ex_hid"), sem("ex_hT"), sem("ex_hTc")
        selw_ready, ex_selTc = sem("selw_ready"), sem("ex_selTc")
        ex_down, ex_hi, ex_lo, ex_sum = sem("ex_down"), sem("ex_hi"), sem("ex_lo"), sem("ex_sum")
        moe_added, counted = sem("moe_added"), sem("counted")
        ov_step, ov_sel, ov_gath, ov_xT, ov_loaded = (
            sem("ov_step"), sem("ov_sel"), sem("ov_gath"), sem("ov_xT"), sem("ov_loaded"))
        ov_gu, ov_act, ov_hid, ov_hT, ov_hTc = (
            sem("ov_gu"), sem("ov_act"), sem("ov_hid"), sem("ov_hT"), sem("ov_hTc"))
        ov_selTc, ov_down, ov_hi, ov_lo, ov_sum, ov_added = (
            sem("ov_selTc"), sem("ov_down"), sem("ov_hi"), sem("ov_lo"), sem("ov_sum"), sem("ov_added"))
        ff_gate, ff_up, ff_act, ff_hid, ff_hT, ff_hTh, ff_hTl, ff_added = (
            sem("ff_gate"), sem("ff_up"), sem("ff_act"), sem("ff_hid"), sem("ff_hT"), sem("ff_hTh"), sem("ff_hTl"),
            sem("ff_added"))
        z_unit, z_act, z_dve = sem("z_unit"), sem("z_act"), sem("z_dve")
        conv_done, conv_silu, pad_zeroed = sem("conv_done"), sem("conv_silu"), sem("pad_zeroed")
        gates_exp, gates_u, gates_ready = sem("gates_exp"), sem("gates_u"), sem("gates_ready")
        cum_ps, a_ready, a_ps, a_copied = sem("cum_ps"), sem("a_ready"), sem("a_ps"), sem("a_copied")
        sink_exp, sig_done = sem("sink_exp"), sem("sig_done")
        ml_a, ml_used, ml_max, ml_exp, ml_s, ml_sc = (
            sem("ml_a"), sem("ml_used"), sem("ml_max"), sem("ml_exp"), sem("ml_s"), sem("ml_sc"))
        ml_h, ml_hsq = sem("ml_h"), sem("ml_hsq")
        g_sig, merged = sem("g_sig"), sem("merged")

        N1, N2, NF1, NMIX, NF2, NFIN = range(6)
        T_N1, T_Y, T_N2, T_F1, T_MIX, T_SY, T_HM, T_MG, T_F2 = range(9)
        G_OUT, G_PA, G_PM, G_OUT2 = range(4)
        GB = {N1: 1, N2: 2, NF1: 3, NMIX: 4, "hm": 5, NF2: 6, NFIN: 7}

        def raw_piece(n):
            return raw_w[:, n % STEPS * PIECE:(n % STEPS + 1) * PIECE]

        def cols(w, n):
            return w[:, n % STEPS, :].rearrange("p (k f) -> p k f", k=KH)

        def hidden(w, n):
            return w[:, n % STEPS, :].rearrange("p (k f) -> p k f", k=KT)

        def down_piece(w, n):
            return w[:, n % STEPS, :].rearrange("p (k n) -> p k n", k=FT)

        def by_pairs(ap):
            return ap.rearrange("p (k m i d) -> p k m i d", k=KH, m=2, i=4)

        def by_pairs_split(ap):
            return ap.rearrange("p (k i m d) -> p k i m d", k=KH, m=2, i=4)

        def gate_up(s):
            return ring[s][:, 0:2 * PIECE].rearrange("p (g k f) -> p k g f", g=2, k=KT)

        def down(s):
            return ring[s][:, 2 * PIECE:].rearrange("p (k n) -> p k n", k=FT)

        def flat(ap):
            return ap.rearrange("p a b -> p (a b)")

        def overflow(eng):
            eng.wait_ge(counted, 1)
            return eng.If(eng.value_load(most[0:1, 0:1], min_val=0, max_val=SEQ) > SLOTS)

        Z = [("q", gp, i) for gp in range(2) for i in range(4)] + [("k", 2, b) for b in range(2)]
        Z += [("av", 2, t) for t in range(TILES)]
        Z += [("m", 3 + b // 4, b) for b in range(8)]
        Z += [("mv" if g < 7 else "mo", g, t) for g in range(5, 9) for t in range(TILES)]
        Z += [("if", None, t) for t in range(TILES)]
        ZG = [("g", g, t) for g in range(9, 13) for t in range(TILES)]
        by_act = [u[0] in ("q", "k", "m") for u in Z]
        units_of = [[n for n, u in enumerate(Z) if u[1] == g] for g in range(9)]
        units_of.append([n for n, u in enumerate(Z) if u[1] is None])

        def z_bank(n):
            g = next(g for g, us in enumerate(units_of) if n in us)
            return PS[:, 4 * (g % 2) + units_of[g].index(n), :]

        PT_BANKS = {(0, 0): 3, (0, 1): 6, (1, 0): 4, (1, 1): 8, (2, 0): 2, (2, 1): 4}
        PT_BASE, PT_A, PT_D, n_ps, n_a, n_d = {}, {}, {}, 0, 0, 0
        for key, banks in PT_BANKS.items():
            PT_BASE[key], PT_A[key], PT_D[key] = n_ps, n_a, n_d
            n_ps, n_a, n_d = n_ps + banks, n_a + banks // 2, n_d + (banks + 1) // 2

        block = ctx.enter_context(nc.Block())

        @block.sync
        def _(eng):
            by_row, by_tile = "(p k) f -> p k f", "(k p) f -> p k f"

            def load(n, moe_over=False):
                src, c, kh = PIECES[n]
                if n >= STEPS:
                    eng.wait_ge(split_lo, n - STEPS + 1)
                if moe_over and n < BEFORE_MOE + STEPS:
                    eng.wait_ge(ex_down, 2 * PAIRS - 2)
                if src in ("ffn1", "ffn2"):
                    part, c = c, kh
                    w = A[f"{src}_w_{part}_2"][0]
                    if part == "down":
                        cut = w[c * HIDDEN:(c + 1) * HIDDEN, :].rearrange("(p k) n -> p (k n)", k=FT)
                        eng.dma_start(raw_piece(n), cut).then_inc(piece_loaded[n % STEPS], 16)
                        return
                    cut = w[:, c * HIDDEN:(c + 1) * HIDDEN].rearrange(by_row, k=KT)
                else:
                    lo = c * HALF if src != "w_in_2" or c < 9 else C_G + (c - 9) * HALF
                    w = A[src if src in ("w_in", "w_out", "w_in_2", "w_out_2") else src + "_2"][0]
                    order = by_row if src in ("w_in", "w_in_2") else by_tile
                    cut = w.rearrange(order, k=KT)[:, kh * KH:(kh + 1) * KH, lo:lo + HALF]
                eng.dma_start(raw_piece(n).rearrange("p (k f) -> p k f", k=cut.shape[1]), cut
                              ).then_inc(piece_loaded[n % STEPS], 16)

            def load_gate_up(s, e, done):
                for j, w in enumerate(("w_gate", "w_up")):
                    eng.dma_start(ring[s][:, j * PIECE:(j + 1) * PIECE],
                                  A[w][0, bass.ds(e, 1)].rearrange("a (p k) f -> p (a k f)", k=KT)).then_inc(done, 16)

            def load_down(s, e, done):
                eng.dma_start(ring[s][:, 2 * PIECE:], A["w_down"][0, bass.ds(e, 1)].rearrange(
                    "a (p k) n -> p (a k n)", k=FT)).then_inc(done, 16)

            for n in range(BEFORE_MOE):
                load(n)
            eng.wait_ge(split_lo, BEFORE_MOE)
            for s in range(RING):
                if s == 1:
                    eng.wait_ge(piece_used, BEFORE_MOE)
                load_gate_up(s, s, gate_up_loaded[s])
                load_down(s, s, down_loaded[s])
            with eng.Fori(1, EXPERTS // RING) as it:
                for u in range(2):
                    slots = (2 * u, 2 * u + 1)
                    eng.wait_ge(ex_gu, it * 2 + (u - 1))
                    for s in slots:
                        load_gate_up(s, it * RING + s, gate_up_loaded[s])
                    eng.wait_ge(ex_down, it * 4 + (2 * u - 2))
                    for s in slots:
                        load_down(s, it * RING + s, down_loaded[s])
            with overflow(eng):
                eng.wait_ge(ex_down, 2 * PAIRS)
                with eng.Fori(0, ROUNDS - 1) as r:
                    with eng.Fori(0, PAIRS) as i:
                        eng.wait_ge(ov_step, r * (PAIRS + 1) + i + 2)
                        for m in range(2):
                            load_gate_up(m, 2 * i + m, ov_loaded)
                            load_down(m, 2 * i + m, ov_loaded)
                eng.wait_ge(ov_down, 2 * (ROUNDS - 1) * PAIRS)
            for n in range(BEFORE_MOE, len(PIECES)):
                load(n, True)
            for t in range(TILES):
                eng.wait_ge(normed, TILES * NFIN + t + 1)
                eng.dma_start(out[0, t * P:(t + 1) * P, :], tok[:, t, :]).then_inc(out_stored, 16)
            eng.wait_ge(out_stored, 16 * TILES)

        @block.gpsimd
        def _(eng):
            seq = [0]

            def link(ins):
                seq[0] += 1
                ins.then_inc(pool_seq, 1)
                eng.wait_ge(pool_seq, seq[0])

            def load_gain(name):
                eng.dma_start(gain[:, :], A[name].rearrange("a d -> (a d)").partition_broadcast(P)
                              if name != "final_norm_2" else A[name].partition_broadcast(P)).then_inc(gain_loaded, 16)

            roots = [0]

            def root(dst):
                roots[0] += 1
                eng.wait_ge(root_in, roots[0])
                eng.tensor_tensor(dst, dst, minus_half[:, 0:dst.shape[1]], ALU.pow).then_inc(root_out, 1)
                eng.wait_ge(root_out, roots[0])

            def norm_root(k):
                for t in range(TILES):
                    root(rstd[:, TILES * k + t:TILES * k + t + 1])

            load_gain("norm1_g")
            link(eng.memset(minus_half[:, :], -0.5))
            link(eng.memset(ones[:, :], 1.0))
            link(eng.memset(ident[:, :], 0.0))
            link(eng.affine_select(out=ident[:, :], in_=ident[:, :], compare_op=ALU.not_equal, fill=1.0,
                                   base=0, pattern=[[-1, P]], channel_multiplier=1))
            for m, base in ((upto, 0), (before, -1)):
                link(eng.affine_select(out=m[:, :], in_=ones[:, :], compare_op=ALU.is_ge, fill=0.0,
                                       base=base, pattern=[[1, P]], channel_multiplier=-1))
            link(eng.memset(masks[:, :], 0.0))
            for lo in (P, 3 * P):
                link(eng.affine_select(out=masks[:, lo:lo + P], in_=masks[:, lo:lo + P], compare_op=ALU.is_ge,
                                       fill=MASKED, base=0, pattern=[[-1, P]], channel_multiplier=1))
            link(eng.affine_select(out=masks[:, 2 * P:3 * P], in_=masks[:, 2 * P:3 * P], compare_op=ALU.is_gt,
                                   fill=MASKED, base=0, pattern=[[1, P]], channel_multiplier=-1))
            link(eng.iota(iota_i[:, :], pattern=[[1, SLOTS]], base=0, channel_multiplier=0))
            link(eng.tensor_copy(iota[:, :], iota_i[:, :]))
            eng.memset(relx[BUCKETS:BUCKETS + 1, :], MASKED).then_inc(consts, 1)
            eng.wait_ge(consts, 1)
            norm_root(N1)

            for _ in range(2 * TILES):
                root(hs[:, 0, 1, 0:8])
            eng.wait_ge(bias_copied, N_BIAS)
            eng.dma_start(bias_rows.rearrange("h p m -> p h m"), bias_stage).then_inc(bias_stored, 16)
            eng.wait_ge(bias_stored, 16)
            skewed = bass.AP(tensor=bias_rows.tensor, offset=P - 1,
                             ap=[[DIST_COLS - 1, P], [P * DIST_COLS, N_BIAS], [1, SEQ]])
            eng.dma_start(bias, skewed).then_inc(bias_loaded, 16)
            eng.wait_ge(normed, TILES * (N1 + 1))
            load_gain("norm2_g")
            for _ in range(2 * TILES):
                root(hs[:, 0, 1, 0:8])
            for t in range(TILES):
                root(hs[:, t, 7, 4:8])
            norm_root(N2)
            eng.wait_ge(normed, TILES * (N2 + 1))
            load_gain("ffn1_norm_2")
            eng.wait_ge(moe_added, 1)
            b_in = A["b_in_2"][0]
            eng.dma_start(bias_av, b_in[C_AV:C_MQ].partition_broadcast(P)).then_inc(bb_loaded, 16)
            eng.dma_start(bias_mvo, b_in[C_MV:C_IF].partition_broadcast(P)).then_inc(bb_loaded, 16)
            norm_root(NF1)
            eng.wait_ge(normed, TILES * (NF1 + 1))
            load_gain("mix_norm_2")
            norm_root(NMIX)
            eng.wait_ge(normed, TILES * (NMIX + 1))
            eng.dma_start(gain[:, :], A["mlstm_head_norm_2"].rearrange("a h v -> (a h v)").partition_broadcast(P)
                          ).then_inc(gain_loaded, 16)
            for t in range(TILES):
                root(hs[:, t, 3, 8:16])
            eng.wait_ge(mixed, 5 * TILES)
            eng.dma_start(bias_g, b_in[C_G:C_END].partition_broadcast(P)).then_inc(bb_loaded, 16)
            load_gain("ffn2_norm_2")
            norm_root(NF2)
            eng.wait_ge(normed, TILES * (NF2 + 1))
            load_gain("final_norm_2")
            norm_root(NFIN)

        @block.scalar
        def _(eng):
            seq = [0]

            def link(ins):
                seq[0] += 1
                ins.then_inc(act_seq, 1)
                eng.wait_ge(act_seq, seq[0])

            eng.dma_start(res[:, :, :], A["x"][0].rearrange("(t p) d -> p t d", p=P)).then_inc(x_loaded, 16)
            b_in = A["b_in_2"][0]
            n_vec = [0]

            def load_vec(dst, src):
                eng.dma_start(dst, src).then_inc(vec_loaded, 16)
                n_vec[0] += 1

            bq = b_in[0:C_K].rearrange("(g m i d) -> m g i d", g=2, m=2, i=4)
            for m in range(2):
                for g in range(2):
                    load_vec(vec_rows[V_BQ + 4 * g:V_BQ + 4 * g + 4, HEAD * m:HEAD * m + HEAD], bq[m, g])
            load_vec(vec_rows[V_BK:V_BM, :], b_in[C_K:C_AV].rearrange("(r p) -> r p", p=P))
            load_vec(vec_rows[V_BM:V_CONV, :], b_in[C_MQ:C_MV].rearrange("(r p) -> r p", p=P))
            for j in range(CONV):
                load_vec(vec_rows[V_CONV + 8 * j:V_CONV + 8 * j + 8, :],
                         A["mlstm_conv_2"][0, j].rearrange("(r p) -> r p", p=P))
            for n, name in enumerate(("diff_q_g", "diff_k_g", "moba_q_g", "moba_k_g")):
                for m in range(2):
                    load_vec(vec_rows[V_QK + n:V_QK + n + 1, HEAD * m:HEAD * m + HEAD], A[name][0:1, :])
            load_vec(vec_rows[V_SUB:V_SUB + 1, :], A["diff_sub_g"][0:1, :])
            assert n_vec[0] == N_VEC
            eng.dma_start(relx[0:BUCKETS, :], A["rel_bias"]).then_inc(rel_loaded, 16)
            eng.dma_start(onehot[:, :], buckets).then_inc(rel_loaded, 16)
            for n, name in enumerate(("lambda_q1", "lambda_k1", "lambda_q2", "lambda_k2")):
                eng.dma_start(lam_rows[:, n, :], A[name][0].partition_broadcast(P)).then_inc(lam_loaded, 16)
            eng.dma_start(router[:, :, 0:GROUPS], A["router_group"][0].rearrange("(p k) g -> p k g", k=KT)).then_inc(router_loaded, 16)
            for g in range(GROUPS):
                eng.dma_start(router[:, :, GROUPS + PER_GROUP * g:GROUPS + PER_GROUP * (g + 1)],
                              A["router_expert"][0, g].rearrange("(p k) e -> p k e", k=KT)).then_inc(router_loaded, 16)
            eng.dma_start(w_if[:, :, :], A["w_in_2"][0, :, C_IF:C_G].rearrange("(p k) f -> p k f", k=KT)).then_inc(if_loaded, 16)
            eng.dma_start(b_if[:, :], b_in[C_IF:C_G].partition_broadcast(P)).then_inc(if_loaded, 16)
            eng.dma_start(sink_nat[:, :], A["attn_sinks_2"][0].partition_broadcast(P)).then_inc(if_loaded, 16)

            def square(k, ready):
                for t in range(TILES):
                    eng.wait_ge(*ready(t))
                    eng.activation(tok[:, t, :], res[:, t, :], ACT.Square,
                                   accum_out=ss[:, TILES * k + t:TILES * k + t + 1]).then_inc(squared, 1)

            done = [0]

            def split_at(n, slot, turn, permute=False):
                eng.wait_ge(piece_loaded[slot], turn * 16 + 16)
                if not isinstance(n, int) or n >= STEPS:
                    eng.wait_ge(piece_used, n - (STEPS - 1))
                raw = raw_w[:, slot * PIECE:(slot + 1) * PIECE]
                if permute:
                    for m in range(2):
                        ins = eng.activation(by_pairs_split(w_hi[:, slot, :])[:, :, :, m], by_pairs(raw)[:, :, m], ACT.Copy)
                else:
                    ins = eng.activation(w_hi[:, slot, :], raw, ACT.Copy)
                ins.then_inc(split_hi, 1)

            def split(n):
                if BEFORE_MOE <= n < BEFORE_MOE + STEPS:
                    eng.wait_ge(ex_down, 2 * PAIRS)
                split_at(n, n % STEPS, n // STEPS, PIECES[n][0] == "w_in_2" and PIECES[n][1] < 2)

            def feed(q, limit=len(PIECES)):
                while done[0] < min(q + STEPS, limit):
                    split(done[0])
                    done[0] += 1

            def t8_split(u, dst, scale=None):
                for t in range(TILES):
                    eng.wait_ge(t8, TILES * u + t + 1)
                    src = PS[:, 4 + 2 * t:6 + 2 * t, :].rearrange("p b (k q) -> p (b k) q", q=P)
                    to = dst[0][:, :, t * P:(t + 1) * P]
                    if scale is None:
                        eng.activation(to, src, ACT.Copy).then_inc(t8_hi, 1)
                    else:
                        eng.activation(to[:, 0:4], src[:, 0:4], ACT.Copy, scale=scale)
                        eng.activation(to[:, 4:8], src[:, 4:8], ACT.Copy).then_inc(t8_hi, 1)

            def pT_copy(key):
                for b in range(1, PT_BANKS[key], 2):
                    eng.wait_ge(pT_ps, PT_BASE[key] + b + 1)
                    to = (MPT if key[0] == 2 else PT)[key[1]]
                    eng.activation(flat(to[:, 4 * b:4 * b + 4, :]), PS[:, 4 + b % 4, :], ACT.Copy).then_inc(pT_a, 1)

            square(N1, lambda t: (x_loaded, 16))
            feed(0, 1)
            t8_split(T_N1, hT)
            feed(0)

            units = [(c, t) for c in (0, 1, 3, 4) for t in range(TILES)]
            def qk_copies(c):
                for n, (uc, t) in enumerate(units):
                    if uc != c:
                        continue
                    w = n // TILES
                    if n == 0:
                        eng.wait_ge(vec_ready, 1)
                    eng.wait_ge(qk_ps, n + 1)
                    eng.activation(qkT[w][:, :, t * P:(t + 1) * P], PS[:, 4 + n % 2, :].rearrange("p (j q) -> p j q", j=4),
                                   ACT.Copy, scale=vec[:, V_QK + w:V_QK + w + 1]).then_inc(qk_done, 1)

            for c in range(6):
                for n, (uc, t) in enumerate(units):
                    if uc != c - 1:
                        continue
                    eng.wait_ge(piece_used, 2 * c)
                    if n >= 2:
                        eng.wait_ge(proj_sq_read, n - 1)
                    eng.activation(tok[:, t, HALF:], PS[:, (TILES * (c - 1) + t) % 4, :], ACT.Square).then_inc(proj_sq, 1)
                feed(2 * c)
                qk_copies(c - 2)
                feed(2 * c + 1, BEFORE_MOE)
                if c == 3:
                    eng.wait_ge(lam_sum, 1)
                    eng.activation(lam[:, 2:4], lam[:, 0:2], ACT.Exp).then_inc(lam_exp, 1)
                    eng.wait_ge(router_loaded, 16 * (1 + GROUPS))
                    eng.activation(router_parts[0][:, :, :], router[:, :, :], ACT.Copy).then_inc(small_hi, 1)
                    eng.wait_ge(if_loaded, 48)
                    eng.activation(w_if_parts[0][:, :, :], w_if[:, :, :], ACT.Copy).then_inc(small_hi, 1)
            qk_copies(4)
            feed(12, BEFORE_MOE)

            def exps(t, nheads, row):
                n = P * (t + 1)
                for a in range(nheads):
                    eng.activation(L[t][:, a, 0:n], L[t][:, a, 0:n], ACT.Exp, bias=hs[:, t, row, a:a + 1],
                                   accum_out=hs[:, t, row + 1, a:a + 1]).then_inc(expd, 1)

            for t in range(TILES):
                eng.wait_ge(maxed, t + 1)
                exps(t, MAPS, 1)
            for t in range(TILES):
                pT_copy((0, t))
                eng.wait_ge(pv, 2 * t + 1)
                eng.activation(flat(L[t])[:, 0:HALF], PS[:, 2 * t, :], ACT.Square).then_inc(pv_sq, 1)
            t8_split(T_Y, yT, vec[:, V_SUB:V_SUB + 1])
            feed(13, BEFORE_MOE)

            square(N2, lambda t: (gemm_used, 3 + t))
            t8_split(T_N2, hT)
            for t in range(TILES):
                eng.activation(tok_parts[0][:, t], tok[:, t, :].rearrange("p (d k) -> p k d", k=KT), ACT.Copy).then_inc(tok_hi, 1)
            eng.wait_ge(route_exp_in, 1)
            for t in range(TILES):
                eng.activation(rt[:, t, 80:84], rt8[:, t, 0, 0:4], ACT.Exp, bias=rt[:, t, 84:85],
                               accum_out=rt[:, t, 85:86])
            eng.activation(rt[:, :, 86:87], rt[:, :, 87:88], ACT.Exp).then_inc(route_exp, 1)

            def gathered(it, kh):
                eng.wait_ge(ex_gath, 2 * it + (kh + 1))
                eng.activation(flat(xgT[:, kh * KH:(kh + 1) * KH, :]), flat(PS[:, 4:6, :]), ACT.Copy).then_inc(ex_xT, 1)

            def expert_pair(it, u, more):
                j = it * 2 + u
                eng.wait_ge(ex_gu, j + 1)
                eng.activation(act_e, PS[:, 6, 0:HIDDEN], ACT.Silu).then_inc(ex_act, 1)
                if u and more:
                    for kh in range(2):
                        gathered(it + 1, kh)
                eng.wait_ge(ex_selTc, j + 1)
                for x, h in enumerate((1, 0)):
                    eng.wait_ge(ex_down, j * 2 + (x + 1))
                    eng.activation(exo[0][:, h * HALF:(h + 1) * HALF], PS[:, 7 - h, :], ACT.Copy,
                                   scale=wslot[:, 0:1]).then_inc(ex_hi, 1)

            for kh in range(2):
                gathered(0, kh)
            for u in range(2):
                expert_pair(0, u, True)
            with eng.Fori(1, PAIRS // 2 - 1) as it:
                for u in range(2):
                    expert_pair(it, u, True)
            for u in range(2):
                expert_pair(PAIRS // 2 - 1, u, False)
            with overflow(eng):
                with eng.Fori(0, ROUNDS - 1) as r:
                    with eng.Fori(0, PAIRS) as i:
                        j = r * PAIRS + i
                        eng.wait_ge(ov_gath, j + 1)
                        eng.activation(xgT[:, :, 0:P], PS[:, 4:6, :].rearrange("p b (k s) -> p (b k) s", s=P),
                                       ACT.Copy).then_inc(ov_xT, 1)
                        eng.wait_ge(ov_gu, j + 1)
                        eng.activation(act_e, PS[:, 6, 0:HIDDEN], ACT.Silu).then_inc(ov_act, 1)
                        eng.wait_ge(ov_selTc, j + 1)
                        for x, h in enumerate((1, 0)):
                            eng.wait_ge(ov_down, j * 2 + (x + 1))
                            eng.activation(exo[0][:, h * HALF:(h + 1) * HALF], PS[:, 7 - h, :], ACT.Copy,
                                           scale=wslot[:, 0:1]).then_inc(ov_hi, 1)

            def ffn(f):
                base, g0 = first[("ffn1", "ffn2")[f]], f * CHUNKS

                def silu(c, n):
                    eng.wait_ge(piece_used, n + 1)
                    eng.activation(flat(act_f), PS[:, 4, :], ACT.Silu).then_inc(ff_act, 1)

                def hidden_T(c):
                    eng.wait_ge(ff_hT, c + (g0 + 1))
                    eng.activation(flat(hidT_f[0][:, :, :]), PS[:, 6, :], ACT.Copy).then_inc(ff_hTh, 1)

                def chunk(c, n, parts):
                    parts(2)
                    hidden_T(c - 1)
                    parts(3)
                    silu(c, n)
                    parts(4)

                def part_of(n):
                    return lambda j: feed(n + j - 2)

                def part_in_loop(c):
                    return lambda j: split_at(c * 3 + (base - 1 + j), (base - 1 + j) % STEPS, c + (base - 1 + j) // STEPS)

                feed(base)
                silu(0, base)
                feed(base + 1)
                chunk(1, base + 2, part_of(base + 2))
                with eng.Fori(2, CHUNKS - 1) as c:
                    chunk(c, c * 3 + (base - 1), part_in_loop(c))
                last = base + 3 * (CHUNKS - 1) - 1
                done[0] = last + 2
                chunk(CHUNKS - 1, last, part_of(last))
                hidden_T(CHUNKS - 1)
                feed(last + 3)

            feed(BEFORE_MOE, BEFORE_MOE + 2)
            square(NF1, lambda t: (moe_added, 1))
            feed(BEFORE_MOE)
            t8_split(T_F1, hT)
            ffn(0)

            square(NMIX, lambda t: (ff_added, 2 * t + 2))
            t8_split(T_MIX, hT)
            n_silu = [0]

            def silu_conv():
                b = n_silu[0]
                eng.wait_ge(conv_done, b + 1)
                eng.activation(mqk[:, b, :], conv[:, b % 2, :], ACT.Silu).then_inc(conv_silu, 1)
                n_silu[0] += 1

            def take(g):
                for n in units_of[g]:
                    kind, _, i = Z[n]
                    if not by_act[n]:
                        continue
                    eng.wait_ge(piece_used, first["w_in_2"] + 2 * g + 2)
                    src = z_bank(n)[:, 0:SEQ]
                    if kind == "q":
                        eng.activation(sqT[:, 4 * g + i, :], src, ACT.Identity, scale=SCALE,
                                       bias=vec[:, V_BQ + 4 * g + i:V_BQ + 4 * g + i + 1]).then_inc(z_act, 1)
                    elif kind == "k":
                        eng.activation(skT[:, i, :], src, ACT.Identity, bias=vec[:, V_BK + i:V_BK + i + 1]).then_inc(z_act, 1)
                    else:
                        if i >= 2:
                            eng.wait_ge(conv_done, i - 1)
                        eng.activation(raw[:, i % 2, CONV - 1:], src, ACT.Identity,
                                       bias=vec[:, V_BM + i:V_BM + i + 1]).then_inc(z_act, 1)
                        if i >= 1:
                            silu_conv()
                        if i == 7:
                            silu_conv()

            for g in range(9):
                feed(first["w_in_2"] + 2 * g)
                if g:
                    take(g - 1)
                feed(first["w_in_2"] + 2 * g + 1)
            feed(first["w_in_2"] + 18)
            for t in range(TILES):
                eng.wait_ge(z_dve, sum(not a for a in by_act) - TILES + t + 1)
                link(eng.activation(ga[:, t, 1, :], ga[:, t, 0, :], ACT.Tanh, scale=1.0 / SOFTCAP))
                eng.activation(ga[:, t, 2, 8:16], ga[:, t, 1, 8:16], ACT.Exp, scale=-SOFTCAP).then_inc(gates_exp, 1)
                eng.wait_ge(gates_u, t + 1)
                eng.activation(ga[:, t, 3, 8:16], ga[:, t, 3, 0:8], ACT.Ln).then_inc(gates_exp, 1)
            for t in range(TILES):
                eng.wait_ge(maxed, TILES + t + 1)
                exps(t, Q_HEADS, 1)
                eng.activation(hs[:, t, 4, :], hs[:, t, 3, :], ACT.Exp).then_inc(sink_exp, 1)
            for t in range(TILES):
                pT_copy((1, t))
            t8_split(T_SY, yT)
            for t in range(TILES):
                eng.wait_ge(ml_max, t + 1)
                n = P * (t + 1)
                for a in range(MLSTM_HEADS):
                    eng.activation(ML[t][:, a, 0:n], ML[t][:, a, 0:n], ACT.Exp, bias=hs[:, t, 1, a:a + 1]).then_inc(ml_exp, 1)
                eng.activation(hs[:, t, 5, 0:8], hs[:, t, 4, 0:8], ACT.Exp, scale=-1.0).then_inc(ml_exp, 1)
            for t in range(TILES):
                eng.activation(mo[:, t, :], mo[:, t, :], ACT.Sigmoid).then_inc(sig_done, 1)
            for t in range(TILES):
                pT_copy((2, t))
                eng.wait_ge(ml_h, t + 1)
                eng.activation(head_squares, tok[:, t, :], ACT.Square).then_inc(ml_hsq, 1)
            def sigmoids(j):
                for t in range(TILES):
                    eng.wait_ge(g_sig, TILES * j + t + 1)
                    x = gates[:, t, j * HALF:(j + 1) * HALF]
                    eng.activation(x, x, ACT.Sigmoid).then_inc(sig_done, 1)

            for j in range(4):
                feed(first["w_in_2"] + 18 + 2 * j)
                if j:
                    sigmoids(j - 1)
                feed(first["w_in_2"] + 18 + 2 * j + 1)
            feed(first["w_proj_attn"])
            sigmoids(3)
            t8_split(T_HM, hT)
            for n in range(first["w_proj_attn"], first["w_out_2"] + 1):
                feed(n)
            t8_split(T_MG, yT)
            for n in range(first["w_out_2"] + 1, first["ffn2"]):
                feed(n)
            square(NF2, lambda t: (gemm_used, 4 + 3 + t))
            t8_split(T_F2, hT)
            ffn(1)
            square(NFIN, lambda t: (ff_added, 4 + 2 * t + 2))

        @block.tensor
        def _(eng):
            def product(dst, x, w, first_one, last_one):
                eng.matmul(dst, x[0], w[0], start=first_one, stop=False)
                eng.matmul(dst, x[0], w[1], start=False, stop=False)
                return eng.matmul(dst, x[1], w[0], start=False, stop=last_one)

            def both(parts, cut):
                return [cut(x) for x in parts]

            def transpose8(u, src, ready, strided):
                for t in range(TILES):
                    eng.wait_ge(*ready(t))
                    for k in range(KT):
                        cut = src[:, t, k:D:KT] if strided else src[:, t, k * P:(k + 1) * P]
                        mm = eng.transpose(PS[:, 4 + 2 * t + k // 4, (k % 4) * P:(k % 4 + 1) * P], cut, ident[:, :])
                    mm.then_inc(t8, 1)

            def copied8(u):
                eng.wait_ge(t8_lo, TILES * (u + 1))

            def half_gemm(n, dst, src, kh):
                eng.wait_ge(split_lo, n + 1)
                for t in range(TILES):
                    for k in range(KH):
                        mm = product(dst(t), both(src, lambda x: x[:, kh * KH + k, t * P:(t + 1) * P]),
                                     both((w_hi, w_lo), lambda w: cols(w, n)[:, k, :]),
                                     kh == 0 and k == 0, kh == 1 and k == KH - 1)
                mm.then_inc(piece_used, 1)

            eng.wait_ge(consts, 1)
            transpose8(T_N1, tok, lambda t: (normed, TILES * N1 + t + 1), True)
            eng.wait_ge(vec_loaded, 16 * N_VEC)
            eng.transpose(PS[:, 3, 0:V_ROWS], vec_rows[:, :], ident[0:V_ROWS, 0:V_ROWS]).then_inc(vec_T, 1)
            copied8(T_N1)

            qk_groups = (0, 1, 3, 4)

            def qk_transposes(c):
                for t in range(TILES):
                    n = TILES * qk_groups.index(c) + t
                    eng.wait_ge(proj_used, TILES * c + t + 1)
                    if n >= 2:
                        eng.wait_ge(qk_done, n - 1)
                    for b in range(4):
                        mm = eng.transpose(PS[:, 4 + n % 2, b * P:(b + 1) * P], tok[:, t, b * P:(b + 1) * P], ident[:, :])
                    mm.then_inc(qk_ps, 1)

            for c in range(6):
                if c == 1:
                    eng.wait_ge(vec_ready, 1)
                if c >= 2:
                    eng.wait_ge(proj_used, TILES * (c - 1))
                for kh in range(2):
                    half_gemm(2 * c + kh, lambda t: PS[:, (TILES * c + t) % 4, :], hT, kh)
                    if kh == 1 and c - 1 in qk_groups:
                        qk_transposes(c - 1)
                    if kh == 0 and c == 2:
                        eng.wait_ge(rel_wide, 1)
                        for h in range(N_BIAS):
                            if h >= 2:
                                eng.wait_ge(bias_copied, h - 1)
                            eng.matmul(PS[:, 6 + h % 2, 0:DIST_COLS], relb[:, h, :], onehot[:, :], start=True, stop=True
                                       ).then_inc(bias_ps, 1)

            def scores(base, t, q, k, pairs):
                n = P * (t + 1)
                for g in range(pairs):
                    if t > 0 or g >= 2:
                        eng.wait_ge(score_used, base + g - 1)
                    for m in range(2):
                        a, b = HEAD * m, HEAD * (m + 1)
                        mm = eng.matmul(PS[:, 2 * (g % 2) + m, 0:n], q(g)[a:b, t * P:(t + 1) * P], k(g)[a:b, 0:n],
                                        start=True, stop=True)
                    mm.then_inc(score, 1)

            def weight_transposes(key, blocks, ready):
                assert (len(blocks) + 3) // 4 == PT_BANKS[key]
                for x, (a, kb) in enumerate(blocks):
                    j = x // 4
                    if x % 4 == 0 and j >= 4:
                        done, base = (pT_a, PT_A[key]) if j % 2 else (pT_d, PT_D[key])
                        eng.wait_ge(done, base + (j - 4) // 2 + 1)
                    if kb == 0:
                        eng.wait_ge(*ready(a))
                    src = (ML if key[0] == 2 else L)[key[1]]
                    mm = eng.transpose(PS[:, 4 + j % 4, (x % 4) * P:(x % 4 + 1) * P],
                                       src[:, a, kb * P:(kb + 1) * P], ident[:, :])
                    if x % 4 == 3 or x == len(blocks) - 1:
                        mm.then_inc(pT_ps, 1)
                banks = PT_BANKS[key]
                eng.wait_ge(pT_a, PT_A[key] + banks // 2)
                eng.wait_ge(pT_d, PT_D[key] + (banks + 1) // 2)

            eng.wait_ge(qk_done, 8)
            eng.wait_ge(proj_used, 6 * TILES)
            eng.wait_ge(bias_copied, N_BIAS)
            for t in range(TILES):
                scores(8 * t, t, lambda g: qkT[2 * (g // 4)][:, g % 4, :], lambda g: qkT[2 * (g // 4) + 1][:, g % 4, :], 8)
            for t in range(TILES):
                maps = [2 * j for j in range(4)] + list(range(8, MAPS))
                blocks = [(a, kb) for a in maps for kb in range(t + 1)]

                weight_transposes((0, t), blocks, lambda a: (weighted, 4 * t + a // 2 + 1) if a < 8
                                  else (expd, MAPS * t + a + 1))
                eng.wait_ge(score_used, 8 * TILES)
                for u in range(12):
                    for kb in range(t + 1):
                        lhs = PT[t][:, u * (t + 1) + kb, :]
                        if u < 4:
                            dst, v = PS[:, 2 * t, u * P:(u + 1) * P], vals[:, kb, u * P:(u + 1) * P]
                        else:
                            h = u - 4
                            dst, v = PS[:, 2 * t + 1, h * HEAD:(h + 1) * HEAD], vals[:, kb, HALF + h * HEAD:HALF + (h + 1) * HEAD]
                        mm = eng.matmul(dst, lhs, v, start=(kb == 0), stop=(kb == t))
                    if u == 3 or u == 11:
                        mm.then_inc(pv, 1)
            transpose8(T_Y, tok, lambda t: (mixed, 2 * t + 2), False)

            def gemm_1024(v, src, u, name):
                copied8(u)
                bank = 4 if v == G_PM else 0
                for h in range(HALVES):
                    for kh in range(2):
                        half_gemm(first[name] + 2 * h + kh, lambda t: PS[:, bank + 2 * h + t, :], src, kh)

            eng.wait_ge(mixed, 2 * TILES)
            gemm_1024(G_OUT, yT, T_Y, "w_out")

            transpose8(T_N2, tok, lambda t: (normed, TILES * N2 + t + 1), True)
            copied8(T_N2)
            eng.wait_ge(small_lo, 1)
            for t in range(TILES):
                for k in range(KT):
                    mm = product(PS[:, t, 0:ROUTES], both(hT, lambda x: x[:, k, t * P:(t + 1) * P]),
                                 both(router_parts, lambda w: w[:, k, :]), k == 0, k == KT - 1)
                mm.then_inc(route, 1)
            eng.wait_ge(assigned, 1)
            eng.matmul(PS[:, 2, 0:EXPERTS], before[:, :], assign[:, 0, 2, :], start=True, stop=True)
            eng.matmul(PS[:, 2, EXPERTS:2 * EXPERTS], ones[:, :], assign[:, 0, 2, :], start=True, stop=False)
            eng.matmul(PS[:, 2, EXPERTS:2 * EXPERTS], before[:, :], assign[:, 1, 2, :], start=False, stop=True).then_inc(pos_ps, 1)
            for t in range(TILES):
                mm = eng.matmul(PS[:, 3, 0:EXPERTS], ones[:, :], assign[:, t, 2, :], start=(t == 0), stop=(t == TILES - 1))
            mm.then_inc(pos_ps, 1)

            def gather(it, kh):
                if kh == 0:
                    eng.wait_ge(sel_ready, it + 1)
                for k in range(KH):
                    dst = PS[:, 4 + k // 2, (k % 2) * SEQ:(k % 2 + 1) * SEQ]
                    for t in range(TILES):
                        for x in range(2):
                            mm = eng.matmul(dst, tok_parts[x][:, t, kh * KH + k, :], sel[:, t, :],
                                            start=(t == 0 and x == 0), stop=(t == 1 and x == 1))
                mm.then_inc(ex_gath, 1)

            def combine(u, first_one, last_one, done):
                for t in range(TILES):
                    for h in range(HALVES):
                        for x in range(2):
                            mm = eng.matmul(PS[:, 2 * t + h, :], selT[:, u, t * P:(t + 1) * P],
                                            exo[x][:, h * HALF:(h + 1) * HALF], start=(first_one and x == 0),
                                            stop=(last_one and x == 1))
                mm.then_inc(done, 1)

            def gate_and_up_pair(slots, at, done):
                for k in range(KT):
                    for m, s in enumerate(slots):
                        mm = eng.matmul(PS[SLOTS * m:SLOTS * (m + 1), 6, :], xgT[:, k, at + SLOTS * m:at + SLOTS * (m + 1)],
                                        gate_up(s)[:, k], start=(k == 0), stop=(k == KT - 1))
                mm.then_inc(done, 1)

            def transposed_pair(done):
                for t in range(TILES):
                    eng.transpose(PS[:, 7, SEQ + t * P:SEQ + (t + 1) * P], selw[:, t, :], ident[:, :])
                for k in range(FT):
                    mm = eng.transpose(PS[:, 7, k * P:(k + 1) * P], hid_e[:, k:HIDDEN:FT], ident[:, :])
                mm.then_inc(done, 1)

            def down_pair(slots, h, done):
                for k in range(FT):
                    for m, s in enumerate(slots):
                        mm = eng.matmul(PS[SLOTS * m:SLOTS * (m + 1), 7 - h, :], hidT_e[:, k, SLOTS * m:SLOTS * (m + 1)],
                                        down(s)[:, k, h * HALF:(h + 1) * HALF], start=(k == 0), stop=(k == FT - 1))
                mm.then_inc(done, 1)

            def expert_pair(it, u, more, first_one=False):
                j, slots = it * 2 + u, [2 * u, 2 * u + 1]
                if u == 0:
                    eng.wait_ge(ex_xT, it * 2 + 2)
                for s in slots:
                    eng.wait_ge(gate_up_loaded[s], it * 32 + 32)
                if not (first_one and u == 0):
                    eng.wait_ge(ex_lo, j * 2)
                gate_and_up_pair(slots, P * u, ex_gu)
                if not (first_one and u == 0):
                    combine(1 - u, first_one and u == 1, False, ex_sum)
                if more and u == 0:
                    gather(it + 1, 0)
                eng.wait_ge(selw_ready, j * 2 + 2)
                eng.wait_ge(ex_hid, j + 1)
                transposed_pair(ex_hT)
                if more and u == 1:
                    eng.wait_ge(ex_xT, it * 2 + 3)
                    gather(it + 1, 1)
                for s in slots:
                    eng.wait_ge(down_loaded[s], it * 16 + 16)
                eng.wait_ge(ex_hTc, j + 1)
                down_pair(slots, 1, ex_down)
                eng.wait_ge(ex_selTc, j + 1)
                down_pair(slots, 0, ex_down)

            for t in range(TILES):
                eng.wait_ge(tok_lo, t + 1)
            gather(0, 0)
            eng.wait_ge(ex_xT, 1)
            gather(0, 1)
            for u in range(2):
                expert_pair(0, u, True, True)
            with eng.Fori(1, PAIRS // 2 - 1) as it:
                for u in range(2):
                    expert_pair(it, u, True)
            for u in range(2):
                expert_pair(PAIRS // 2 - 1, u, False)
            eng.wait_ge(ex_lo, 2 * PAIRS)
            combine(1, False, True, ex_sum)

            with overflow(eng):
                with eng.Fori(0, ROUNDS - 1) as r:
                    with eng.Fori(0, PAIRS) as i:
                        j = r * PAIRS + i
                        eng.wait_ge(ov_sel, j + 1)
                        for k in range(KT):
                            for t in range(TILES):
                                for x in range(2):
                                    mm = eng.matmul(PS[:, 4 + k // 4, (k % 4) * P:(k % 4 + 1) * P], tok_parts[x][:, t, k, :],
                                                    sel[:, t, 0:P], start=(t == 0 and x == 0), stop=(t == 1 and x == 1))
                        mm.then_inc(ov_gath, 1)
                        eng.wait_ge(ov_xT, j + 1)
                        eng.wait_ge(ov_loaded, 96 * j + 96)
                        gate_and_up_pair((0, 1), 0, ov_gu)
                        eng.wait_ge(ov_hid, j + 1)
                        transposed_pair(ov_hT)
                        eng.wait_ge(ov_hTc, j + 1)
                        down_pair((0, 1), 1, ov_down)
                        eng.wait_ge(ov_selTc, j + 1)
                        down_pair((0, 1), 0, ov_down)
                        eng.wait_ge(ov_lo, j * 2 + 2)
                        combine(0, True, True, ov_sum)

            def ffn(f, u):
                base, g0 = first[("ffn1", "ffn2")[f]], f * CHUNKS
                copied8(u)

                def hidden_columns(x, slot, side, t):
                    for k in range(KT):
                        mm = product(PS[:, 4 + side, t * HIDDEN:(t + 1) * HIDDEN],
                                     both(hT, lambda h: h[:, k, t * P:(t + 1) * P]),
                                     both((w_hi, w_lo), lambda w: hidden(w, slot)[:, k, :]), k == 0, k == KT - 1)
                    return mm

                def transposes(c):
                    eng.wait_ge(ff_hid, c + (g0 + 1))
                    for t in range(TILES):
                        for k in range(FT):
                            mm = eng.transpose(PS[:, 6, k * SEQ + t * P:k * SEQ + (t + 1) * P],
                                               hid_f[:, t, k:HIDDEN:FT], ident[:, :])
                    mm.then_inc(ff_hT, 1)

                def down_chunk(c, slot, first_one, last_one):
                    eng.wait_ge(ff_hTl, c + (g0 + 1))
                    for t in range(TILES):
                        for h in range(HALVES):
                            for k in range(FT):
                                mm = product(PS[:, 2 * t + h, :], both(hidT_f, lambda x: x[:, k, t * P:(t + 1) * P]),
                                             both((w_hi, w_lo), lambda w: down_piece(w, slot)[:, k, h * HALF:(h + 1) * HALF]),
                                             first_one and k == 0, last_one and k == FT - 1)
                    mm.then_inc(piece_used, 1)

                def chunk(c, n, slot, first_one=False):
                    eng.wait_ge(split_lo, n + 1)
                    eng.wait_ge(ff_act, c + g0)
                    hidden_columns(hT, slot, 0, 0)
                    transposes(c - 1)
                    hidden_columns(hT, slot, 0, 1).then_inc(piece_used, 1)
                    eng.wait_ge(split_lo, n + 2)
                    down_chunk(c - 1, slot + 1, first_one, False)
                    eng.wait_ge(split_lo, n + 3)
                    for t in range(TILES):
                        mm = hidden_columns(hT, slot + 2, 1, t)
                    mm.then_inc(piece_used, 1)

                for side in range(2):
                    eng.wait_ge(split_lo, base + side + 1)
                    for t in range(TILES):
                        mm = hidden_columns(hT, base + side, side, t)
                    mm.then_inc(piece_used, 1)
                chunk(1, base + 2, base + 2, True)
                with eng.Fori(2, CHUNKS - 1) as c:
                    chunk(c, c * 3 + (base - 1), base + 2)
                last = base + 3 * (CHUNKS - 1) - 1
                chunk(CHUNKS - 1, last, last)
                transposes(CHUNKS - 1)
                eng.wait_ge(split_lo, last + 4)
                down_chunk(CHUNKS - 1, last + 3, False, True)

            transpose8(T_F1, tok, lambda t: (normed, TILES * NF1 + t + 1), True)
            ffn(0, T_F1)

            transpose8(T_MIX, tok, lambda t: (normed, TILES * NMIX + t + 1), True)
            copied8(T_MIX)

            def all_taken(us):
                last = us[-1] + 1
                if sum(by_act[:last]):
                    eng.wait_ge(z_act, sum(by_act[:last]))
                if last - sum(by_act[:last]):
                    eng.wait_ge(z_dve, last - sum(by_act[:last]))

            for g in range(9):
                if g >= 2:
                    all_taken(units_of[g - 2])
                for kh in range(2):
                    p = first["w_in_2"] + 2 * g + kh
                    eng.wait_ge(split_lo, p + 1)
                    for n in units_of[g]:
                        kind, _, i = Z[n]
                        for k in range(KH):
                            x = both(hT, lambda h: h[:, kh * KH + k, :])
                            w = both((w_hi, w_lo), lambda w: cols(w, p)[:, k, :])
                            flags = (kh == 0 and k == 0, kh == 1 and k == KH - 1)
                            if kind in ("q", "k", "m"):
                                mm = product(z_bank(n)[:, 0:SEQ], both(w, lambda a: a[:, i % 4 * P:(i % 4 + 1) * P]), x, *flags)
                            else:
                                lo = 256 if kind == "av" else 0
                                mm = product(z_bank(n)[:, 0:HALF - lo], both(x, lambda a: a[:, i * P:(i + 1) * P]),
                                             both(w, lambda a: a[:, lo:]), *flags)
                    mm.then_inc(piece_used, 1)
            all_taken(units_of[7])
            eng.wait_ge(small_lo, 2)
            for n in units_of[9]:
                i = Z[n][2]
                for k in range(KT):
                    mm = product(z_bank(n)[:, 0:16], both(hT, lambda h: h[:, k, i * P:(i + 1) * P]),
                                 both(w_if_parts, lambda w: w[:, k, :]), k == 0, k == KT - 1)
                mm.then_inc(z_unit, 1)
            eng.wait_ge(z_dve, sum(not x for x in by_act))
            eng.wait_ge(z_act, sum(by_act))
            eng.wait_ge(gates_ready, 1)
            eng.matmul(PS[:, 0, 0:8], upto[:, :], ga[:, 0, 6, 8:16], start=True, stop=True).then_inc(cum_ps, 1)
            eng.wait_ge(gates_ready, 2)
            eng.matmul(PS[:, 1, 0:8], ones[:, :], ga[:, 0, 6, 8:16], start=True, stop=False)
            eng.matmul(PS[:, 1, 0:8], upto[:, :], ga[:, 1, 6, 8:16], start=False, stop=True).then_inc(cum_ps, 1)
            for t in range(TILES):
                eng.wait_ge(a_ready, t + 1)
                mm = eng.transpose(PS[0:8, 2, t * P:(t + 1) * P], ga[:, t, 7, 8:16], ident[:, :])
            mm.then_inc(a_ps, 1)
            eng.wait_ge(a_copied, 1)
            for t in range(TILES):
                scores(16 + 8 * t, t, lambda g: sqT[:, g, :], lambda g: skT[:, g // 4, :], 8)
            for t in range(TILES):
                weight_transposes((1, t), [(a, kb) for a in range(Q_HEADS) for kb in range(t + 1)],
                                  lambda a: (expd, MAPS * TILES + Q_HEADS * t + a + 1))
                eng.wait_ge(score_used, 8 * TILES * 2)
                for a in range(Q_HEADS):
                    g, i, m = a // 8, a % 8 // 2, a % 2
                    kv = 2 * g + m
                    for kb in range(t + 1):
                        mm = eng.matmul(PS[:, 2 * t + g, (4 * m + i) * HEAD:(4 * m + i + 1) * HEAD], PT[t][:, a * (t + 1) + kb, :],
                                        sv[:, kb, kv * HEAD:(kv + 1) * HEAD], start=(kb == 0), stop=(kb == t))
                    if a % 8 == 7:
                        mm.then_inc(pv, 1)
            transpose8(T_SY, tok, lambda t: (mixed, 4 + 2 * t + 2), False)
            eng.wait_ge(conv_silu, 8)
            eng.wait_ge(mixed, 4 * TILES)
            for t in range(TILES):
                n = P * (t + 1)
                for j in range(4):
                    if t > 0:
                        eng.wait_ge(ml_used, 4 * (t - 1) + j + 1)
                    for m in range(2):
                        mm = eng.matmul(PS[:, j, m * SEQ:m * SEQ + n], ident[0:8, 2 * j + m:2 * j + m + 1].broadcast_to([8, P]),
                                        aT[:, 0:n], start=True, stop=True)
                    mm.then_inc(ml_a, 1)
            for t in range(TILES):
                n = P * (t + 1)
                for j in range(4):
                    if t > 0 or j >= 2:
                        eng.wait_ge(ml_sc, 8 * t + 2 * (j - 1))
                    else:
                        eng.wait_ge(ml_used, 4 * (TILES - 1) + 2 * j + 2)
                    for m in range(2):
                        a, b = HEAD * m, HEAD * (m + 1)
                        mm = eng.matmul(PS[:, 2 * (j % 2) + m, 0:n], mqk[a:b, j, t * P:(t + 1) * P], mqk[a:b, 4 + j, 0:n],
                                        start=True, stop=True)
                    mm.then_inc(ml_s, 1)
                if t == 0:
                    weight_transposes((2, 0), [(a, 0) for a in range(MLSTM_HEADS)], lambda a: (ml_sc, a + 1))
            for t in range(TILES):
                if t > 0:
                    weight_transposes((2, t), [(a, kb) for a in range(MLSTM_HEADS) for kb in range(t + 1)],
                                      lambda a: (ml_sc, 8 * t + a + 1))
                eng.wait_ge(ml_sc, 8 * TILES)
                for a in range(MLSTM_HEADS):
                    for kb in range(t + 1):
                        mm = eng.matmul(PS[:, 2 * t + a // 4, (a % 4) * P:(a % 4 + 1) * P], MPT[t][:, a * (t + 1) + kb, :],
                                        mv[:, kb, a * P:(a + 1) * P], start=(kb == 0), stop=(kb == t))
                    if a % 4 == 3:
                        mm.then_inc(pv, 1)
            eng.wait_ge(ml_h, TILES)
            for j in range(4):
                if j >= 2:
                    eng.wait_ge(g_sig, TILES * (j - 1))
                for kh in range(2):
                    half_gemm(first["w_in_2"] + 18 + 2 * j + kh, lambda t: PS[:, 2 * (j % 2) + t, :], hT, kh)
            transpose8(T_HM, tok, lambda t: (mixed, 8 + t + 1), False)
            eng.wait_ge(g_sig, len(ZG))
            gemm_1024(G_PA, yT, T_SY, "w_proj_attn")
            gemm_1024(G_PM, hT, T_HM, "w_proj_mlstm")
            transpose8(T_MG, tok, lambda t: (merged, 3 + t), False)
            gemm_1024(G_OUT2, yT, T_MG, "w_out_2")
            transpose8(T_F2, tok, lambda t: (normed, TILES * NF2 + t + 1), True)
            ffn(1, T_F2)

        @block.vector
        def _(eng):
            seq, roots = [0], [0]

            def link(ins):
                seq[0] += 1
                ins.then_inc(dve_seq, 1)
                eng.wait_ge(dve_seq, seq[0])

            def wide(ap, n):
                return ap.unsqueeze(len(ap.shape)).broadcast_to([*ap.shape, n])

            def rsqrt(dst, sums, n):
                roots[0] += 1
                eng.tensor_scalar(dst, sums, 1.0 / n, EPS, ALU.mult, ALU.add).then_inc(root_in, 1)
                eng.wait_ge(root_out, roots[0])

            def norm(k):
                for t in range(TILES):
                    c = TILES * k + t
                    eng.wait_ge(squared, c + 1)
                    rsqrt(rstd[:, c:c + 1], ss[:, c:c + 1], D)
                    eng.wait_ge(gain_loaded, 16 * GB[k])
                    eng.scalar_tensor_tensor(tok[:, t, :], res[:, t, :], rstd[:, c:c + 1], gain[:, :],
                                             ALU.mult, ALU.mult).then_inc(normed, 1)

            done = [0]

            def split_at(n, slot, permute=False):
                eng.wait_ge(split_hi, n + 1)
                raw = raw_w[:, slot * PIECE:(slot + 1) * PIECE]
                if permute:
                    for m in range(2):
                        ins = eng.tensor_tensor(by_pairs_split(w_lo[:, slot, :])[:, :, :, m], by_pairs(raw)[:, :, m],
                                                by_pairs_split(w_hi[:, slot, :])[:, :, :, m], ALU.subtract)
                else:
                    ins = eng.tensor_tensor(w_lo[:, slot, :], raw, w_hi[:, slot, :], ALU.subtract)
                ins.then_inc(split_lo, 1)

            def feed(q, limit=len(PIECES)):
                while done[0] < min(q + STEPS, limit):
                    n = done[0]
                    split_at(n, n % STEPS, PIECES[n][0] == "w_in_2" and PIECES[n][1] < 2)
                    done[0] += 1

            def t8_split(u, dst, scale=None):
                for t in range(TILES):
                    eng.wait_ge(t8_hi, TILES * u + t + 1)
                    src = PS[:, 4 + 2 * t:6 + 2 * t, :].rearrange("p b (k q) -> p (b k) q", q=P)
                    hi, lo = [x[:, :, t * P:(t + 1) * P] for x in dst]
                    if scale is None:
                        eng.tensor_tensor(lo, src, hi, ALU.subtract).then_inc(t8_lo, 1)
                    else:
                        eng.scalar_tensor_tensor(lo[:, 0:4], src[:, 0:4], scale, hi[:, 0:4], ALU.mult, ALU.subtract)
                        eng.tensor_tensor(lo[:, 4:8], src[:, 4:8], hi[:, 4:8], ALU.subtract).then_inc(t8_lo, 1)

            def pT_copy(key):
                for b in range(0, PT_BANKS[key], 2):
                    eng.wait_ge(pT_ps, PT_BASE[key] + b + 1)
                    to, n = (MPT if key[0] == 2 else PT)[key[1]], min(4, 4 * PT_BANKS[key] - 4 * b)
                    eng.tensor_copy(flat(to[:, 4 * b:4 * b + n, :]), PS[:, 4 + b % 4, 0:n * P]).then_inc(pT_d, 1)

            def add_to_residual(name, h):
                eng.wait_ge(piece_used, first[name] + 2 * h + 2)
                for t in range(TILES):
                    x = res[:, t, h * HALF:(h + 1) * HALF]
                    eng.tensor_tensor(x, x, PS[:, 2 * h + t, :], ALU.add).then_inc(gemm_used, 1)

            link(eng.memset(rt8[:, :, 0, :], -3e38))
            norm(N1)
            feed(0, 1)
            t8_split(T_N1, hT)
            eng.wait_ge(vec_T, 1)
            link(eng.tensor_copy(vec[:, :], PS[:, 3, 0:V_ROWS]))
            for c, n, f in ((V_BQ, 8, SCALE), (V_QK, 1, SCALE), (V_QK + 2, 1, SCALE)):
                link(eng.tensor_scalar(vec[:, c:c + n], vec[:, c:c + n], f, None, ALU.mult))
            eng.tensor_scalar(vec[:, V_SUB:V_SUB + 1], vec[:, V_SUB:V_SUB + 1], 1.0 - LAMBDA_INIT, None,
                              ALU.mult).then_inc(vec_ready, 1)
            feed(0)
            eng.wait_ge(rel_loaded, 32)
            eng.tensor_copy(relb[:, :, :], wide(relx[:, :], P)).then_inc(rel_wide, 1)
            eng.wait_ge(lam_loaded, 64)
            for n in range(2):
                ins = eng.tensor_tensor_reduce(lam_rows[:, 2 * n, :], lam_rows[:, 2 * n, :], lam_rows[:, 2 * n + 1, :], 1.0, 0.0,
                                               ALU.mult, ALU.add, lam[:, n:n + 1])
            ins.then_inc(lam_sum, 1)

            n_qk = [0]

            def take_projection(c):
                eng.wait_ge(piece_used, 2 * c + 2)
                for t in range(TILES):
                    bank, n = PS[:, (TILES * c + t) % 4, :], n_qk[0]
                    if c in (2, 5):
                        lo = 0 if c == 2 else HALF
                        eng.tensor_copy(vals[:, t, lo:lo + HALF], bank).then_inc(proj_used, 1)
                        continue
                    eng.wait_ge(proj_sq, n + 1)
                    eng.tensor_reduce(hs[:, 0, 0, 0:8], tok[:, t, HALF:].rearrange("p (h d) -> p h d", d=HEAD),
                                      AX_X, ALU.add).then_inc(proj_sq_read, 1)
                    eng.wait_ge(proj_sq_read, n + 1)
                    rsqrt(hs[:, 0, 1, 0:8], hs[:, 0, 0, 0:8], HEAD)
                    if n >= 2:
                        eng.wait_ge(qk_ps, n - 1)
                    eng.tensor_tensor(tok[:, t, 0:HALF].rearrange("p (h d) -> p h d", d=HEAD),
                                      bank.rearrange("p (h d) -> p h d", d=HEAD), wide(hs[:, 0, 1, 0:8], HEAD),
                                      ALU.mult).then_inc(proj_used, 1)
                    n_qk[0] += 1

            for c in range(6):
                feed(2 * c)
                if c:
                    take_projection(c - 1)
                if c == 2:
                    for h in range(N_BIAS):
                        eng.wait_ge(bias_ps, h + 1)
                        eng.tensor_copy(bias_stage[:, h, :], PS[:, 6 + h % 2, 0:DIST_COLS]).then_inc(bias_copied, 1)
                feed(2 * c + 1, BEFORE_MOE)
                if c == 3:
                    eng.wait_ge(lam_exp, 1)
                    link(eng.tensor_tensor(lam[:, 4:5], lam[:, 2:3], lam[:, 3:4], ALU.subtract))
                    link(eng.tensor_scalar(lam[:, 5:6], lam[:, 4:5], LAMBDA_INIT, -1.0, ALU.add, ALU.mult))
                    eng.wait_ge(small_hi, 2)
                    for raw_small, (hi, lo) in ((router, router_parts), (w_if, w_if_parts)):
                        eng.tensor_tensor(lo[:, :, :], raw_small[:, :, :], hi[:, :, :], ALU.subtract).then_inc(small_lo, 1)
                    link(eng.tensor_copy(sink[:, :].rearrange("p (g i m) -> p g m i", g=2, i=4),
                                         sink_nat[:, :].rearrange("p (g m i) -> p g m i", g=2, m=2)))
            take_projection(5)
            feed(12, BEFORE_MOE)

            eng.wait_ge(bias_loaded, 16)

            def masked_logits(t):
                n = P * (t + 1)
                for g in range(8):
                    eng.wait_ge(score, 8 * t + g + 1)
                    b = 2 * (g % 2)
                    if g < 4:
                        add = bias[:, g:g + 1, SEQ - n:].broadcast_to([P, 2, n])
                    else:
                        add = bias[:, DIFF_HEADS + 2 * (g - 4):DIFF_HEADS + 2 * (g - 4) + 2, SEQ - n:]
                    eng.tensor_tensor(L[t][:, 2 * g:2 * g + 2, 0:n], PS[:, b:b + 2, 0:n], add, ALU.add).then_inc(score_used, 1)
                eng.wait_ge(score_used, 8 * (t + 1))
                link(eng.tensor_reduce(hs[:, t, 0, :], L[t][:, :, 0:n], AX_X, ALU.max))
                eng.tensor_scalar(hs[:, t, 1, :], hs[:, t, 0, :], -1.0, None, ALU.mult).then_inc(maxed, 1)

            def differential_weights(t):
                n = P * (t + 1)
                eng.wait_ge(expd, MAPS * (t + 1))
                link(eng.reciprocal(hs[:, t, 5, :], hs[:, t, 2, :]))
                link(eng.tensor_scalar(hs[:, t, 6, 0:4], hs[:, t, 5, 1:8:2], lam[:, 5:6], None, ALU.mult))
                for j in range(DIFF_HEADS):
                    ins = eng.tensor_scalar(L[t][:, 2 * j, 0:n], L[t][:, 2 * j, 0:n], hs[:, t, 5, 2 * j:2 * j + 1], None, ALU.mult)
                link(ins)
                for j in range(DIFF_HEADS):
                    eng.scalar_tensor_tensor(L[t][:, 2 * j, 0:n], L[t][:, 2 * j + 1, 0:n], hs[:, t, 6, j:j + 1], L[t][:, 2 * j, 0:n],
                                             ALU.mult, ALU.add).then_inc(weighted, 1)

            def normed_heads(t):
                eng.wait_ge(pv_sq, t + 1)
                link(eng.tensor_reduce(hs[:, t, 7, 0:4], flat(L[t])[:, 0:HALF].rearrange("p (h c) -> p h c", h=4), AX_X, ALU.add))
                rsqrt(hs[:, t, 7, 4:8], hs[:, t, 7, 0:4], 2 * HEAD)
                eng.tensor_tensor(tok[:, t, 0:HALF].rearrange("p (h c) -> p h c", h=4),
                                  PS[:, 2 * t, :].rearrange("p (h c) -> p h c", h=4), wide(hs[:, t, 7, 4:8], P),
                                  ALU.mult).then_inc(mixed, 1)
                eng.wait_ge(pv, 2 * t + 2)
                eng.tensor_tensor(tok[:, t, HALF:].rearrange("p (h c) -> p h c", h=8),
                                  PS[:, 2 * t + 1, :].rearrange("p (h c) -> p h c", h=8), wide(hs[:, t, 5, 8:16], HEAD),
                                  ALU.mult).then_inc(mixed, 1)

            for t in range(TILES):
                masked_logits(t)
            differential_weights(0)
            pT_copy((0, 0))
            differential_weights(1)
            normed_heads(0)
            pT_copy((0, 1))
            normed_heads(1)
            t8_split(T_Y, yT, vec[:, V_SUB:V_SUB + 1])
            feed(13, BEFORE_MOE)
            for h in range(HALVES):
                add_to_residual("w_out", h)

            norm(N2)
            t8_split(T_N2, hT)
            for t in range(TILES):
                eng.wait_ge(tok_hi, t + 1)
                eng.tensor_tensor(tok_parts[1][:, t], tok[:, t, :].rearrange("p (d k) -> p k d", k=KT), tok_parts[0][:, t],
                                  ALU.subtract).then_inc(tok_lo, 1)
            eng.wait_ge(route, TILES)
            ONE = lambda c: rt[:, :, c:c + 1]
            each = range(TILES)
            link(eng.tensor_copy(rt8[:, :, 0, 0:GROUPS], PS[:, 0:TILES, 0:GROUPS]))
            link([eng.max(rt8[:, t, 1, :], rt8[:, t, 0, :]) for t in each][-1])
            eng.tensor_scalar(ONE(84), rt8[:, :, 1, 0:1], -1.0, None, ALU.mult)
            link([eng.max_index(rt8u[:, t, 0, :], rt8[:, t, 1, :], rt8[:, t, 0, :]) for t in each][-1])
            link(eng.tensor_copy(ONE(88), rt8u[:, :, 0, 0:1]))
            eng.tensor_scalar(ONE(91), ONE(88), float(PER_GROUP), None, ALU.mult)
            link(eng.tensor_tensor(rt[:, :, 40:44], iota[:, 0:GROUPS].unsqueeze(1).broadcast_to([P, TILES, GROUPS]),
                                   rt[:, :, 88:89].broadcast_to([P, TILES, GROUPS]), ALU.is_equal))
            link(eng.tensor_tensor(rt[:, :, 8:40].rearrange("p t (g e) -> p t g e", g=GROUPS),
                                   PS[:, 0:TILES, GROUPS:ROUTES].rearrange("p t (g e) -> p t g e", g=GROUPS),
                                   wide(rt[:, :, 40:44], PER_GROUP), ALU.mult))
            link(eng.tensor_reduce(rt[:, :, 0:8], rt[:, :, 8:40].rearrange("p t (g e) -> p t e g", g=GROUPS), AX_X, ALU.add))
            link([eng.max(rt8[:, t, 2, :], rt[:, t, 0:8]) for t in each][-1])
            eng.tensor_tensor(ONE(87), rt8[:, :, 2, 1:2], rt8[:, :, 2, 0:1], ALU.subtract).then_inc(route_exp_in, 1)
            link([eng.max_index(rt8u[:, t, 1, :], rt8[:, t, 2, :], rt[:, t, 0:8]) for t in each][-1])
            link(eng.tensor_copy(rt[:, :, 89:91], rt8u[:, :, 1, 0:2]))
            link(eng.tensor_tensor(rt[:, :, 89:91], rt[:, :, 89:91], rt[:, :, 91:92].broadcast_to([P, TILES, 2]), ALU.add))
            link(eng.tensor_tensor(assign[:, :, 0:2, :], iota[:, 0:EXPERTS].unsqueeze(1).unsqueeze(1).broadcast_to([P, TILES, 2, EXPERTS]),
                                   wide(rt[:, :, 89:91], EXPERTS), ALU.is_equal))
            eng.tensor_tensor(assign[:, :, 2, :], assign[:, :, 0, :], assign[:, :, 1, :], ALU.add).then_inc(assigned, 1)
            eng.wait_ge(pos_ps, 1)
            eng.wait_ge(assigned, 1)
            link(eng.scalar_tensor_tensor(posn[:, :, 1, :], PS[:, 2, 0:TILES * EXPERTS].rearrange("p (t e) -> p t e", t=TILES),
                                          1.0, assign[:, :, 2, :], ALU.add, ALU.mult))
            link(eng.tensor_scalar(posn[:, :, 1, :], posn[:, :, 1, :], -1.0, None, ALU.add))

            def select(it):
                eng.tensor_tensor(sel[:, :, :].rearrange("p t (e c) -> p t e c", e=RING),
                                  iota[:, :].unsqueeze(1).unsqueeze(1).broadcast_to([P, TILES, RING, SLOTS]),
                                  wide(posn[:, :, 1, bass.ds(it * RING, RING)], SLOTS), ALU.is_equal).then_inc(sel_ready, 1)

            def select_weighted(i, done, count):
                cut = selw.rearrange("p t (e c) -> p t e c", e=2)
                eng.tensor_tensor(cut, iota[:, :].unsqueeze(1).unsqueeze(1).broadcast_to([P, TILES, 2, SLOTS]),
                                  wide(posn[:, :, 1, bass.ds(i * 2, 2)], SLOTS), ALU.is_equal).then_inc(done, 1)
                eng.wait_ge(done, count)
                return eng.tensor_tensor(cut, cut, wide(wtok[:, :, bass.ds(i * 2, 2)], SLOTS), ALU.mult)

            def slot_weights(u, done):
                src = PS[:, 7, SEQ:]
                eng.tensor_scalar(selT[:, u, :], src, 0.0, None, ALU.is_gt)
                eng.tensor_reduce(wslot[:, :], src, AX_X, ALU.add).then_inc(done, 1)

            def rest_of_rows(h, done):
                cut = slice(h * HALF, (h + 1) * HALF)
                eng.scalar_tensor_tensor(exo[1][:, cut], PS[:, 7 - h, :], wslot[:, 0:1], exo[0][:, cut],
                                         ALU.mult, ALU.subtract).then_inc(done, 1)

            def expert_pair(it, u, more, first_one=False):
                j = it * 2 + u
                if not (first_one and u == 0):
                    eng.wait_ge(ex_hT, j)
                select_weighted(j, selw_ready, j * 2 + 1).then_inc(selw_ready, 1)
                eng.wait_ge(ex_act, j + 1)
                eng.tensor_tensor(hid_e, act_e, PS[:, 6, HIDDEN:], ALU.mult).then_inc(ex_hid, 1)
                eng.wait_ge(ex_hT, j + 1)
                eng.tensor_copy(flat(hidT_e), PS[:, 7, 0:HIDDEN]).then_inc(ex_hTc, 1)
                slot_weights(u, ex_selTc)
                if more and u == 1:
                    eng.wait_ge(ex_gath, it * 2 + 4)
                    select(it + 2)
                for x, h in enumerate((1, 0)):
                    eng.wait_ge(ex_hi, j * 2 + (x + 1))
                    rest_of_rows(h, ex_lo)

            select(0)
            eng.wait_ge(route_exp, 1)
            eng.tensor_scalar(ONE(94), ONE(86), 1.0, None, ALU.add)
            link(eng.reciprocal(ONE(91), ONE(85)))
            link(eng.reciprocal(ONE(95), ONE(94)))
            link(eng.tensor_tensor(ONE(92), ONE(91), ONE(95), ALU.mult))
            link(eng.tensor_tensor(ONE(93), ONE(92), ONE(86), ALU.mult))
            link(eng.tensor_tensor(assign[:, :, 0:2, :], assign[:, :, 0:2, :], wide(rt[:, :, 92:94], EXPERTS), ALU.mult))
            link(eng.tensor_tensor(wtok[:, :, :], assign[:, :, 0, :], assign[:, :, 1, :], ALU.add))
            eng.wait_ge(pos_ps, 2)
            link(eng.tensor_reduce(most_f[:, :], PS[:, 3, 0:EXPERTS], AX_X, ALU.max))
            eng.tensor_copy(most[:, :], most_f[:, :]).then_inc(counted, 1)
            eng.wait_ge(ex_gath, 2)
            select(1)
            for u in range(2):
                expert_pair(0, u, True, True)
            with eng.Fori(1, PAIRS // 2 - 2) as it:
                for u in range(2):
                    expert_pair(it, u, True)
            for it in range(PAIRS // 2 - 2, PAIRS // 2):
                for u in range(2):
                    expert_pair(it, u, False)

            def add_rows(done):
                for t in range(TILES):
                    for h in range(HALVES):
                        x = res[:, t, h * HALF:(h + 1) * HALF]
                        ins = eng.tensor_tensor(x, x, PS[:, 2 * t + h, :], ALU.add)
                ins.then_inc(done, 1)

            eng.wait_ge(ex_sum, PAIRS)
            add_rows(ov_added)
            with overflow(eng):
                with eng.Fori(0, ROUNDS - 1) as r:
                    eng.tensor_scalar(posn[:, :, 1, :], posn[:, :, 1, :], -float(SLOTS), None, ALU.add).then_inc(ov_step, 1)
                    with eng.Fori(0, PAIRS) as i:
                        j = r * PAIRS + i
                        eng.wait_ge(ov_step, r * (PAIRS + 1) + i + 1)
                        eng.tensor_tensor(sel[:, :, 0:P].rearrange("p t (e c) -> p t e c", e=2),
                                          iota[:, :].unsqueeze(1).unsqueeze(1).broadcast_to([P, TILES, 2, SLOTS]),
                                          wide(posn[:, :, 1, bass.ds(i * 2, 2)], SLOTS), ALU.is_equal)
                        select_weighted(i, ov_step, r * (PAIRS + 1) + i + 2).then_inc(ov_sel, 1)
                        eng.wait_ge(ov_act, j + 1)
                        eng.tensor_tensor(hid_e, act_e, PS[:, 6, HIDDEN:], ALU.mult).then_inc(ov_hid, 1)
                        eng.wait_ge(ov_hT, j + 1)
                        eng.tensor_copy(flat(hidT_e), PS[:, 7, 0:HIDDEN]).then_inc(ov_hTc, 1)
                        slot_weights(0, ov_selTc)
                        for x, h in enumerate((1, 0)):
                            eng.wait_ge(ov_hi, j * 2 + (x + 1))
                            rest_of_rows(h, ov_lo)
                        eng.wait_ge(ov_sum, j + 1)
                        eng.wait_ge(ov_added, j + 1)
                        add_rows(ov_added)
            eng.tensor_copy(most_f[:, :], ones[:, 0:1]).then_inc(moe_added, 1)

            def ffn(f):
                base, g0 = first[("ffn1", "ffn2")[f]], f * CHUNKS

                def hidden_units(c):
                    eng.wait_ge(piece_used, c * 3 + (base + 2))
                    eng.wait_ge(ff_act, c + (g0 + 1))
                    eng.tensor_tensor(flat(hid_f), flat(act_f), PS[:, 5, :], ALU.mult).then_inc(ff_hid, 1)

                def hidden_T(c):
                    eng.wait_ge(ff_hTh, c + (g0 + 1))
                    eng.tensor_tensor(flat(hidT_f[1][:, :, :]), PS[:, 6, :], flat(hidT_f[0][:, :, :]), ALU.subtract).then_inc(ff_hTl, 1)

                def chunk(c, parts):
                    hidden_units(c - 1)
                    parts(2)
                    hidden_T(c - 1)
                    parts(3)
                    parts(4)

                def part_of(n):
                    return lambda j: feed(n + j - 2)

                def part_in_loop(c):
                    return lambda j: split_at(c * 3 + (base - 1 + j), (base - 1 + j) % STEPS)

                feed(base)
                feed(base + 1)
                chunk(1, part_of(base + 2))
                with eng.Fori(2, CHUNKS - 1) as c:
                    chunk(c, part_in_loop(c))
                last = base + 3 * (CHUNKS - 1) - 1
                done[0] = last + 2
                chunk(CHUNKS - 1, part_of(last))
                hidden_units(CHUNKS - 1)
                hidden_T(CHUNKS - 1)
                feed(last + 3)
                eng.wait_ge(piece_used, last + 4)
                for t in range(TILES):
                    for h in range(HALVES):
                        x = res[:, t, h * HALF:(h + 1) * HALF]
                        eng.scalar_tensor_tensor(x, PS[:, 2 * t + h, :], 0.5, x, ALU.mult, ALU.add).then_inc(ff_added, 1)

            feed(BEFORE_MOE, BEFORE_MOE + 2)
            norm(NF1)
            feed(BEFORE_MOE)
            t8_split(T_F1, hT)
            ffn(0)

            norm(NMIX)
            t8_split(T_MIX, hT)
            eng.wait_ge(bb_loaded, 32)
            eng.memset(raw[:, :, 0:CONV - 1], 0.0).then_inc(pad_zeroed, 1)

            def take(g):
                if g < 9:
                    eng.wait_ge(piece_used, first["w_in_2"] + 2 * g + 2)
                for n in units_of[g]:
                    kind, _, i = Z[n]
                    if kind == "m":
                        eng.wait_ge(z_act, sum(by_act[:n + 1]))
                        if i == 0:
                            eng.wait_ge(pad_zeroed, 1)
                        if i >= 2:
                            eng.wait_ge(conv_silu, i - 1)
                        acc = conv[:, i % 2, :]
                        tap = lambda j: vec[:, V_CONV + 8 * j + i:V_CONV + 8 * j + i + 1]
                        link(eng.tensor_scalar(acc, raw[:, i % 2, 0:SEQ], tap(0), None, ALU.mult))
                        for j in range(1, CONV):
                            ins = eng.scalar_tensor_tensor(acc, raw[:, i % 2, j:j + SEQ], tap(j), acc, ALU.mult, ALU.add)
                            if j < CONV - 1:
                                link(ins)
                        ins.then_inc(conv_done, 1)
                    if by_act[n]:
                        continue
                    bank = z_bank(n)
                    if kind == "av":
                        dst, src, add = sv[:, i, :], bank[:, 0:256], bias_av
                    elif kind == "if":
                        eng.wait_ge(z_unit, i + 1)
                        dst, src, add = ga[:, i, 0, :], bank[:, 0:16], b_if[:, :]
                    else:
                        lo = (g - 5) % 2 * HALF
                        dst, src = (mv if kind == "mv" else mo)[:, i, lo:lo + HALF], bank
                        add = bias_mvo[:, (g - 5) * HALF:(g - 4) * HALF]
                    eng.tensor_tensor(dst, src, add, ALU.add).then_inc(z_dve, 1)

            for g in range(9):
                feed(first["w_in_2"] + 2 * g)
                if g:
                    take(g - 1)
                feed(first["w_in_2"] + 2 * g + 1)
            take(8)
            take(9)
            feed(first["w_in_2"] + 18)
            for t in range(TILES):
                G = ga[:, t]
                e = G[:, 2, 8:16]
                eng.wait_ge(gates_exp, 2 * t + 1)
                eng.tensor_scalar(G[:, 3, 0:8], e, 1.0, None, ALU.add).then_inc(gates_u, 1)
                eng.wait_ge(gates_u, t + 1)
                link(eng.tensor_scalar(G[:, 4, 0:8], G[:, 3, 0:8], -1.0, None, ALU.add))
                link(eng.tensor_scalar(G[:, 4, 8:16], G[:, 4, 0:8], 0.0, None, ALU.is_equal))
                link(eng.tensor_tensor(G[:, 5, 0:8], G[:, 4, 0:8], G[:, 4, 8:16], ALU.add))
                link(eng.reciprocal(G[:, 5, 8:16], G[:, 5, 0:8]))
                eng.wait_ge(gates_exp, 2 * t + 2)
                link(eng.tensor_tensor(G[:, 5, 8:16], G[:, 5, 8:16], G[:, 3, 8:16], ALU.mult))
                link(eng.tensor_tensor(G[:, 5, 8:16], G[:, 5, 8:16], G[:, 4, 8:16], ALU.add))
                link(eng.tensor_scalar(G[:, 6, 0:8], G[:, 1, 0:8], SOFTCAP, None, ALU.mult))
                eng.scalar_tensor_tensor(G[:, 6, 8:16], G[:, 5, 8:16], -1.0, e, ALU.mult, ALU.mult).then_inc(gates_ready, 1)
            for t in range(TILES):
                G = ga[:, t]
                eng.wait_ge(cum_ps, t + 1)
                link(eng.tensor_copy(G[:, 7, 0:8], PS[:, t, 0:8]))
                eng.tensor_tensor(G[:, 7, 8:16], G[:, 6, 0:8], G[:, 7, 0:8], ALU.subtract).then_inc(a_ready, 1)
            eng.wait_ge(a_ps, 1)
            eng.tensor_copy(aT[:, :], PS[0:8, 2, 0:SEQ]).then_inc(a_copied, 1)

            eng.wait_ge(conv_silu, 8)
            for t in range(TILES):
                n = P * (t + 1)
                mask = prev_causal[:, SEQ - n:].unsqueeze(1).broadcast_to([P, 2, n])
                for g in range(8):
                    eng.wait_ge(score, 16 + 8 * t + g + 1)
                    b = 2 * (g % 2)
                    eng.tensor_tensor(L[t][:, 2 * g:2 * g + 2, 0:n], PS[:, b:b + 2, 0:n], mask, ALU.add).then_inc(score_used, 1)
                eng.wait_ge(score_used, 16 + 8 * (t + 1))
                link(eng.tensor_reduce(hs[:, t, 0, :], L[t][:, :, 0:n], AX_X, ALU.max))
                link(eng.tensor_tensor(hs[:, t, 0, :], hs[:, t, 0, :], sink[:, :], ALU.max))
                link(eng.tensor_scalar(hs[:, t, 1, :], hs[:, t, 0, :], -1.0, None, ALU.mult))
                eng.tensor_tensor(hs[:, t, 3, :], sink[:, :], hs[:, t, 0, :], ALU.subtract).then_inc(maxed, 1)
            for t in range(TILES):
                pT_copy((1, t))
                eng.wait_ge(sink_exp, t + 1)
                link(eng.tensor_tensor(hs[:, t, 5, :], hs[:, t, 2, :], hs[:, t, 4, :], ALU.add))
                link(eng.reciprocal(hs[:, t, 6, :], hs[:, t, 5, :]))
                for g in range(2):
                    eng.wait_ge(pv, 4 + 2 * t + g + 1)
                    inv = hs[:, t, 6, 8 * g:8 * g + 8].rearrange("p (i m) -> p m i", m=2)
                    eng.tensor_tensor(tok[:, t, g * HALF:(g + 1) * HALF].rearrange("p (m i c) -> p m i c", m=2, i=4),
                                      PS[:, 2 * t + g, :].rearrange("p (m i c) -> p m i c", m=2, i=4), wide(inv, HEAD),
                                      ALU.mult).then_inc(mixed, 1)
            t8_split(T_SY, yT)

            for t in range(TILES):
                n = P * (t + 1)
                mask = zero_causal[:, SEQ - n:].unsqueeze(1).broadcast_to([P, 2, n])
                for j in range(4):
                    eng.wait_ge(ml_a, 4 * t + j + 1)
                    eng.tensor_tensor(ML[t][:, 2 * j:2 * j + 2, 0:n], PS[:, j, :].rearrange("p (m k) -> p m k", m=2)[:, :, 0:n],
                                      mask, ALU.add).then_inc(ml_used, 1)
                eng.wait_ge(ml_used, 4 * (t + 1))
                link(eng.tensor_reduce(hs[:, t, 0, 0:8], ML[t][:, :, 0:n], AX_X, ALU.max))
                link(eng.tensor_scalar(hs[:, t, 0, 0:8], hs[:, t, 0, 0:8], 0.0, None, ALU.max))
                link(eng.tensor_scalar(hs[:, t, 1, 0:8], hs[:, t, 0, 0:8], -1.0, None, ALU.mult))
                eng.tensor_tensor(hs[:, t, 4, 0:8], ga[:, t, 7, 0:8], hs[:, t, 0, 0:8], ALU.add).then_inc(ml_max, 1)

            def weighted_scores(t):
                n = P * (t + 1)
                for a in range(MLSTM_HEADS):
                    eng.wait_ge(ml_exp, 9 * t + a + 1)
                    eng.wait_ge(ml_s, 4 * t + a // 2 + 1)
                    eng.scalar_tensor_tensor(ML[t][:, a, 0:n], PS[:, 2 * (a // 2 % 2) + a % 2, 0:n], SCALE, ML[t][:, a, 0:n],
                                             ALU.mult, ALU.mult, accum_out=hs[:, t, 2, a:a + 1]).then_inc(ml_sc, 1)

            def mlstm_rows(t):
                eng.wait_ge(ml_exp, 9 * t + 9)
                eng.wait_ge(ml_sc, 8 * (t + 1))
                link(eng.tensor_scalar(hs[:, t, 6, 0:8], hs[:, t, 2, 0:8], -1.0, None, ALU.mult))
                link(eng.tensor_tensor(hs[:, t, 6, 0:8], hs[:, t, 6, 0:8], hs[:, t, 2, 0:8], ALU.max))
                link(eng.tensor_tensor(hs[:, t, 6, 0:8], hs[:, t, 6, 0:8], hs[:, t, 5, 0:8], ALU.max))
                link(eng.reciprocal(hs[:, t, 7, 0:8], hs[:, t, 6, 0:8]))
                for b in range(2):
                    eng.wait_ge(pv, 8 + 2 * t + b + 1)
                    ins = eng.tensor_tensor(tok[:, t, b * HALF:(b + 1) * HALF].rearrange("p (h v) -> p h v", h=4),
                                            PS[:, 2 * t + b, :].rearrange("p (h v) -> p h v", h=4),
                                            wide(hs[:, t, 7, 4 * b:4 * b + 4], P), ALU.mult)
                ins.then_inc(ml_h, 1)
                eng.wait_ge(ml_hsq, t + 1)
                link(eng.tensor_reduce(hs[:, t, 3, 0:8], head_squares.rearrange("p (h v) -> p h v", h=8), AX_X, ALU.add))
                rsqrt(hs[:, t, 3, 8:16], hs[:, t, 3, 0:8], V_DIM)
                rows = tok[:, t, :].rearrange("p (h v) -> p h v", h=8)
                link(eng.tensor_tensor(rows, rows, wide(hs[:, t, 3, 8:16], P), ALU.mult))
                eng.wait_ge(sig_done, t + 1)
                link(eng.tensor_tensor(tok[:, t, :], tok[:, t, :], mo[:, t, :], ALU.mult))
                eng.wait_ge(gain_loaded, 16 * GB["hm"])
                eng.tensor_tensor(tok[:, t, :], tok[:, t, :], gain[:, :], ALU.mult).then_inc(mixed, 1)

            weighted_scores(0)
            pT_copy((2, 0))
            weighted_scores(1)
            mlstm_rows(0)
            pT_copy((2, 1))
            mlstm_rows(1)

            def add_bias(j):
                if j == 0:
                    eng.wait_ge(bb_loaded, 48)
                lo = j * HALF
                eng.wait_ge(piece_used, first["w_in_2"] + 18 + 2 * j + 2)
                for t in range(TILES):
                    eng.tensor_tensor(gates[:, t, lo:lo + HALF], PS[:, 2 * (j % 2) + t, :], bias_g[:, lo:lo + HALF],
                                      ALU.add).then_inc(g_sig, 1)

            def merge(v, h):
                eng.wait_ge(sig_done, TILES + len(ZG))
                eng.wait_ge(piece_used, first[("w_proj_attn", "w_proj_mlstm")[v]] + 2 * h + 2)
                for t in range(TILES):
                    x = tok[:, t, h * HALF:(h + 1) * HALF]
                    lo = v * D + h * HALF
                    g = gates[:, t, lo:lo + HALF]
                    if v == 0:
                        link(eng.tensor_tensor(x, PS[:, 2 * h + t, :], g, ALU.mult))
                    else:
                        link(eng.tensor_tensor(g, PS[:, 4 + 2 * h + t, :], g, ALU.mult))
                        eng.tensor_tensor(x, x, g, ALU.add).then_inc(merged, 1)

            for j in range(4):
                feed(first["w_in_2"] + 18 + 2 * j)
                if j:
                    add_bias(j - 1)
                feed(first["w_in_2"] + 18 + 2 * j + 1)
            p = first["w_proj_attn"]
            feed(p)
            add_bias(3)
            t8_split(T_HM, hT)
            for n in range(1, 9):
                feed(p + n)
                if n % 2 == 0:
                    merge((n - 2) // 4, (n - 2) // 2 % 2)
            t8_split(T_MG, yT)
            p = first["w_out_2"]
            feed(p + 1)
            feed(p + 2)
            add_to_residual("w_out_2", 0)
            feed(p + 3)
            add_to_residual("w_out_2", 1)
            norm(NF2)
            t8_split(T_F2, hT)
            ffn(1)
            norm(NFIN)


_OUT = ((1, SEQ, D), "float32")


def kernel(**inputs):
    import concourse.bacc as _bacc
    from concourse.bass_utils import run_bass_kernel_spmd as _run

    nc = _bacc.Bacc("TRN2", target_bir_lowering=False, num_devices=1, dynamic_dma_scratch_size=8192)
    arrays, args = {}, {}
    for name, a in inputs.items():
        a = np.ascontiguousarray(a)
        arrays[f"in_{name}"] = a
        args[name] = nc.dram_tensor(f"in_{name}", a.shape, mybir.dt.from_np(a.dtype), kind="ExternalInput").ap()
    b = distance_buckets()
    arrays["in_buckets"] = b
    buckets = nc.dram_tensor("in_buckets", b.shape, F32, kind="ExternalInput").ap()
    out = nc.dram_tensor("out_0", _OUT[0], F32, kind="ExternalOutput").ap()
    two_blocks(nc, args, buckets, out)
    r = _run(nc, [arrays], core_ids=[0])
    return r.results[0]["out_0"]
```

```python
from contextlib import ExitStack

import numpy as np

import concourse.bass as bass
from concourse import mybir

F32 = mybir.dt.float32
F32R = mybir.dt.float32r
U32 = mybir.dt.uint32
I32 = mybir.dt.int32
ALU = mybir.AluOpType
ACT = mybir.ActivationFunctionType
AX_X = mybir.AxisListType.X

P = 128
SEQ = 256
TILES = SEQ // P
D = 1024
KT = D // P
HALF = 512
HALVES = D // HALF
HEAD = 64
EPS = 1e-6
MASKED = -1e30
SCALE = HEAD ** -0.5

DIFF_HEADS, MOBA_HEADS = 4, 8
MAPS = 2 * DIFF_HEADS + MOBA_HEADS
N_BIAS = DIFF_HEADS + MOBA_HEADS
BUCKETS, MAX_DISTANCE = 32, 2048
DIST_COLS = 384
LAMBDA_INIT = 0.8 - 0.6 * float(np.exp(-0.3 * 0))

GROUPS, PER_GROUP = 4, 8
EXPERTS = GROUPS * PER_GROUP
HIDDEN = 256
FT = HIDDEN // P
SLOTS = 64
ROUNDS = SEQ // SLOTS
PAIRS = EXPERTS // 2
ROUTES = GROUPS + EXPERTS

D_FF = ((8 * D // 3 + 127) // 128) * 128
CHUNKS = D_FF // HIDDEN
KV_HEADS, Q_HEADS = 4, 16
MLSTM_HEADS, V_DIM = 8, 128
SOFTCAP = 15.0
C_K, C_AV, C_MQ, C_MV, C_MO, C_IF, C_G, C_END = 1024, 1280, 1536, 2560, 3584, 4608, 4624, 6672

CONV = 4
V_BQ, V_BK, V_BM, V_CONV, V_QK, V_SUB, V_ROWS = 0, 8, 10, 18, 50, 54, 55
N_VEC = 4 + 1 + 1 + CONV + 8 + 1

RING = 4
EXTRA = RING
PIECE = KT * HIDDEN
STEPS = 3
KH = KT // 2


def weight_pieces():
    def feed_forward(f):
        out = [(f, "gate", 0), (f, "up", 0)]
        for c in range(1, CHUNKS):
            out += [(f, "gate", c), (f, "down", c - 1), (f, "up", c)]
        return out + [(f, "down", CHUNKS - 1)]

    def cols(src, n):
        return [(src, c, kh) for c in range(n) for kh in range(2)]

    p = cols("w_in", 6) + cols("w_out", 2) + feed_forward("ffn1") + cols("w_in_2", 13)
    for w in ("w_proj_attn", "w_proj_mlstm", "w_out_2"):
        p += cols(w, 2)
    return p + feed_forward("ffn2")


def distance_buckets():
    out = np.zeros((BUCKETS + 1, DIST_COLS), np.float32)
    exact = BUCKETS // 2
    for m in range(DIST_COLS):
        n = SEQ - 1 - m
        if n < 0:
            out[BUCKETS, m] = 1
        elif n < exact:
            out[n, m] = 1
        else:
            large = np.log(np.float32(n) / np.float32(exact)) / np.log(MAX_DISTANCE / exact) * (BUCKETS - exact)
            out[min(exact + int(large), BUCKETS - 1), m] = 1
    return out


def two_blocks(nc, A, buckets, out):
    PIECES = weight_pieces()
    first = {}
    for n, (src, _, _) in enumerate(PIECES):
        first.setdefault(src, n)
    BEFORE_MOE = first["ffn1"]

    with ExitStack() as ctx:
        def sb(name, shape, dt=F32):
            return ctx.enter_context(nc.sbuf_tensor(name, shape, dt))

        def sem(name):
            return ctx.enter_context(nc.semaphore(name))

        PS = ctx.enter_context(nc.psum_tensor("banks", [P, 8, HALF], F32))

        bias_rows = nc.dram_tensor("bias_rows", [N_BIAS, P, DIST_COLS], F32, kind="Internal").ap()

        raw_w = sb("raw_weights", [P, STEPS * PIECE])
        with ExitStack() as room:
            w_hi = room.enter_context(nc.sbuf_tensor("weights_hi", [P, STEPS, PIECE], F32R))
            w_lo = room.enter_context(nc.sbuf_tensor("weights_lo", [P, STEPS, PIECE], F32R))
        expert_room = sb("expert_weights", [P, 2 * STEPS * PIECE])
        res = sb("residual", [P, TILES, D])
        tok = sb("token_major", [P, TILES, D])
        with ExitStack() as room:
            hT = [room.enter_context(nc.sbuf_tensor(f"normed_T_{part}", [P, KT, SEQ], F32R)) for part in ("hi", "lo")]
        extra_gate_up = sb("extra_gate_up", [P, 2 * PIECE])
        with ExitStack() as room:
            yT = [room.enter_context(nc.sbuf_tensor(f"mixed_T_{part}", [P, KT, SEQ], F32R)) for part in ("hi", "lo")]
        conv_room = sb("conv_room", [P, 2 * KT * SEQ])
        tok_parts = [y[:, :, :].rearrange("p k q -> p (k q)").rearrange("p (t k d) -> p t k d", t=TILES, k=KT) for y in yT]
        with ExitStack() as room:
            def part(name, shape, dt=F32R):
                return room.enter_context(nc.sbuf_tensor(name, shape, dt))

            part("room_of_activations", [P, 2048], F32)
            hidT_f = [part(f"ffn_hidden_T_{x}", [P, FT, SEQ]) for x in ("hi", "lo")]
            part("room_of_expert", [P, 3 * PIECE - 2048 - 2 * FT * SEQ], F32)
            sel = part("select", [P, TILES, RING * SLOTS])
            selT = part("select_T", [P, 2, SEQ])
            exo = [part(f"expert_out_{x}", [P, D]) for x in ("hi", "lo")]
            routed_T = [part(f"routed_T_{x}", [P, KT, SEQ]) for x in ("hi", "lo")]
        STAGE = sb("stage", [P, 9216 + 2 * 16 * SEQ])
        AR = STAGE[:, 0:9216]
        LP = STAGE[:, 9216:]
        def blocks(where, lo, n, width):
            return where[:, lo:lo + n * width].rearrange("p (a k) -> p a k", a=n)

        L = [blocks(conv_room, 0, 16, P), blocks(LP, 0, 16, SEQ)]
        PT = [blocks(conv_room, 16 * P, 16, P), blocks(LP, 16 * SEQ, 32, P)]
        ML = [blocks(LP, 0, 8, P), blocks(LP, 8 * P, 8, SEQ)]
        MPT = [blocks(LP, 16 * SEQ, 8, P), blocks(LP, 16 * SEQ + 8 * P, 16, P)]
        head_squares = LP[:, 3 * D:4 * D]
        ring = [raw_w[:, :], expert_room[:, 0:3 * PIECE], expert_room[:, 3 * PIECE:], AR[:, 0:3 * PIECE]]

        def view(lo, *dims):
            n = int(np.prod(dims))
            names = " ".join("abc"[:len(dims)])
            return AR[:, lo:lo + n].rearrange(f"p ({names}) -> p {names}", **dict(zip("abc", dims)))

        qkT = [view(1024 * n, 4, SEQ) for n in range(4)]
        vals = view(4096, TILES, D)
        bias = view(6144, N_BIAS, SEQ)
        bias_stage = LP[:, 0:N_BIAS * DIST_COLS].rearrange("p (h m) -> p h m", h=N_BIAS)
        BS = N_BIAS * DIST_COLS
        relb = LP[0:BUCKETS + 1, BS:BS + N_BIAS * P].rearrange("p (h q) -> p h q", h=N_BIAS)
        onehot = LP[0:BUCKETS + 1, BS + N_BIAS * P:BS + N_BIAS * P + DIST_COLS]
        lam_rows = LP[:, BS + N_BIAS * P + DIST_COLS:BS + N_BIAS * P + DIST_COLS + 4 * HEAD].rearrange("p (n d) -> p n d", n=4)
        xgT = LP[:, 0:KT * RING * SLOTS].rearrange("p (k s) -> p k s", k=KT)
        selw = LP[:, 4096:4096 + TILES * P].rearrange("p (t s) -> p t s", t=TILES)
        act_e = LP[:, 4608:4608 + HIDDEN]
        hid_e = LP[:, 5120:5120 + HIDDEN]
        hidT_e = LP[:, 5632:5632 + HIDDEN].rearrange("p (k s) -> p k s", k=FT)
        act_f, hid_f = view(0, TILES, HIDDEN), view(1024, TILES, HIDDEN)
        sqT, skT = view(0, 8, SEQ), view(2048, 2, SEQ)
        sv = view(2560, TILES, 256)
        mv, mo = view(3072, TILES, D), view(5120, TILES, D)
        mqk = view(7168, 8, SEQ)
        conv = conv_room[:, 0:2 * SEQ].rearrange("p (a b) -> p a b", a=2)
        raw = conv_room[:, 2 * SEQ:2 * SEQ + 2 * (SEQ + CONV)].rearrange("p (a b) -> p a b", a=2)[:, :, 1:]
        gates = LP[:, 0:4096].rearrange("p (t g) -> p t g", t=TILES)
        bias_av, bias_mvo = LP[:, 0:256], LP[:, 256:2304]
        bias_g = LP[:, 4096:6144]

        gain = sb("gain_rows", [P, D])
        ident = sb("ident", [P, P])
        ones = sb("ones", [P, P])
        upto = sb("upto", [P, P])
        before = sb("before", [P, P])
        masks = sb("masks", [P, 4 * P])
        zero_causal, prev_causal = masks[:, 0:256], masks[:, 256:512]
        vec_rows = sb("vec_rows", [V_ROWS, P])
        vec = sb("vec", [P, V_ROWS])
        relx = sb("rel_bias", [BUCKETS + 1, N_BIAS])
        lam = sb("lambda_parts", [P, 6])
        router = sb("router", [P, KT, ROUTES])
        router_parts = sb("router_hi_lo", [P, KT, 2 * ROUTES], F32R)
        w_if_parts = [sb(f"w_if_{x}", [P, KT, 16], F32R) for x in ("hi", "lo")]
        w_if, b_if = sb("w_if", [P, KT, 16]), sb("b_if", [P, 16])
        sink_nat, sink = sb("sink_natural", [P, Q_HEADS]), sb("sink", [P, Q_HEADS])
        iota_i, iota = sb("iota_int", [P, SLOTS], I32), sb("iota", [P, SLOTS])
        minus_half = sb("minus_half", [P, 8])
        ss = sb("square_sums", [P, 16])
        rstd = sb("rstd", [P, 16])
        hs = sb("head_stats", [P, TILES, 8, 16])
        rt = sb("route_stats", [P, TILES, 96])
        rt8 = sb("route_top", [P, TILES, 4, 8])
        rt8u = sb("route_top_index", [P, TILES, 2, 8], U32)
        assign = sb("assign", [P, TILES, 3, EXPERTS])
        posn = sb("position", [P, TILES, 3, EXPERTS])
        wtok = sb("token_weights", [P, TILES, EXPERTS])
        wslot = sb("slot_weights", [P, 1])
        most_f, most = sb("most_tokens_f", [P, 1]), sb("most_tokens", [P, 1], U32)
        ga = sb("gate_stats", [P, TILES, 8, 16])
        aT = sb("a_rows", [MLSTM_HEADS, SEQ])

        piece_loaded = [sem(f"piece_loaded{s}") for s in range(STEPS)]
        split_hi, split_lo, piece_used = sem("split_hi"), sem("split_lo"), sem("piece_used")
        gate_up_loaded = [sem(f"gate_up_loaded{s}") for s in range(RING)]
        down_loaded = [sem(f"down_loaded{s}") for s in range(RING)]
        extra_loaded = sem("extra_loaded")
        x_loaded = [sem(f"x_loaded{t}") for t in range(TILES)]
        vec_loaded, lam_loaded = sem("vec_loaded"), sem("lam_loaded")
        rel_loaded, router_loaded, if_loaded = sem("rel_loaded"), sem("router_loaded"), sem("if_loaded")
        gain_loaded, bias_loaded, bb_loaded = sem("gain_loaded"), sem("bias_loaded"), sem("bb_loaded")
        bias_stored = sem("bias_stored")
        out_stored = sem("out_stored")
        pool_seq, dve_seq, act_seq = sem("pool_seq"), sem("dve_seq"), sem("act_seq")
        consts, root_in, root_out = sem("consts"), sem("root_in"), sem("root_out")
        vec_T, vec_ready, rel_wide = sem("vec_T"), sem("vec_ready"), sem("rel_wide")
        bias_ps, bias_copied = sem("bias_ps"), sem("bias_copied")
        squared, normed = sem("squared"), sem("normed")
        t8, t8_hi, t8_lo = sem("t8"), sem("t8_hi"), sem("t8_lo")
        small_hi, small_lo = sem("small_hi"), sem("small_lo")
        proj_sq, proj_used = sem("proj_sq"), sem("proj_used")
        proj_sq_read = sem("proj_sq_read")
        qk_ps, qk_done = sem("qk_ps"), sem("qk_done")
        score, score_used, maxed, expd = sem("score"), sem("score_used"), sem("maxed"), sem("expd")
        lam_sum, lam_exp = sem("lam_sum"), sem("lam_exp")
        weighted = sem("weighted")
        pT_ps, pT_a, pT_d = sem("pT_ps"), sem("pT_a"), sem("pT_d")
        pv, pv_sq, mixed = sem("pv"), sem("pv_sq"), sem("mixed")
        gemm_used = sem("gemm_used")
        route, route_exp_in, route_exp, assigned = sem("route"), sem("route_exp_in"), sem("route_exp"), sem("assigned")
        pos_ps, tok_hi, tok_lo = sem("pos_ps"), sem("tok_hi"), sem("tok_lo")
        sel_ready, ex_gath, ex_xT = sem("sel_ready"), sem("ex_gath"), sem("ex_xT")
        ex_gu, ex_act, ex_hid, ex_hT, ex_hTc = sem("ex_gu"), sem("ex_act"), sem("ex_hid"), sem("ex_hT"), sem("ex_hTc")
        selw_ready, ex_selTc = sem("selw_ready"), sem("ex_selTc")
        ex_down, ex_hi, ex_lo, ex_sum = sem("ex_down"), sem("ex_hi"), sem("ex_lo"), sem("ex_sum")
        moe_added, counted = sem("moe_added"), sem("counted")
        ov_step, ov_sel, ov_gath, ov_xT, ov_loaded = (
            sem("ov_step"), sem("ov_sel"), sem("ov_gath"), sem("ov_xT"), sem("ov_loaded"))
        ov_gu, ov_act, ov_hid, ov_hT, ov_hTc = (
            sem("ov_gu"), sem("ov_act"), sem("ov_hid"), sem("ov_hT"), sem("ov_hTc"))
        ov_selTc, ov_down, ov_hi, ov_lo, ov_tile, ov_added, first_rows = (
            sem("ov_selTc"), sem("ov_down"), sem("ov_hi"), sem("ov_lo"), sem("ov_tile"), sem("ov_added"), sem("first_rows"))
        ff_gate, ff_up, ff_act, ff_hid, ff_hT, ff_hTh, ff_hTl, ff_added = (
            sem("ff_gate"), sem("ff_up"), sem("ff_act"), sem("ff_hid"), sem("ff_hT"), sem("ff_hTh"), sem("ff_hTl"),
            sem("ff_added"))
        z_unit, z_act, z_dve = sem("z_unit"), sem("z_act"), sem("z_dve")
        conv_done, conv_silu, pad_zeroed = sem("conv_done"), sem("conv_silu"), sem("pad_zeroed")
        gates_exp, gates_u, gates_ready = sem("gates_exp"), sem("gates_u"), sem("gates_ready")
        cum_ps, a_ready, a_ps, a_copied = sem("cum_ps"), sem("a_ready"), sem("a_ps"), sem("a_copied")
        sink_exp, sig_done = sem("sink_exp"), sem("sig_done")
        weighed, gated_gain = sem("weighed"), sem("gated_gain")
        sy_hi, sy_lo, first_tile = sem("sy_hi"), sem("sy_lo"), sem("first_tile")
        ml_a, ml_used, ml_max, ml_exp, ml_s, ml_sc = (
            sem("ml_a"), sem("ml_used"), sem("ml_max"), sem("ml_exp"), sem("ml_s"), sem("ml_sc"))
        ml_h, ml_hsq = sem("ml_h"), sem("ml_hsq")
        g_sig, merged = sem("g_sig"), sem("merged")

        N1, N2, NF1, NMIX, NF2, NFIN = range(6)
        T_N1, T_Y, T_N2, T_F1, T_MIX, T_HM, T_MG, T_F2 = range(8)
        G_OUT, G_PA, G_PM, G_OUT2 = range(4)
        GB = {N1: 1, N2: 2, NF1: 3, NMIX: 4, "hm": 5, NF2: 6, NFIN: 7}

        def raw_piece(n):
            return raw_w[:, n % STEPS * PIECE:(n % STEPS + 1) * PIECE]

        def cols(w, n):
            return w[:, n % STEPS, :].rearrange("p (k f) -> p k f", k=KH)

        def hidden(w, n):
            return w[:, n % STEPS, :].rearrange("p (k f) -> p k f", k=KT)

        def down_piece(w, n):
            return w[:, n % STEPS, :].rearrange("p (k n) -> p k n", k=FT)

        def by_pairs(ap):
            return ap.rearrange("p (k m i d) -> p k m i d", k=KH, m=2, i=4)

        def by_pairs_split(ap):
            return ap.rearrange("p (k i m d) -> p k i m d", k=KH, m=2, i=4)

        def gate_up(s):
            return (extra_gate_up[:, :] if s == EXTRA else ring[s][:, 0:2 * PIECE]).rearrange("p (g k f) -> p k g f", g=2, k=KT)

        def down(s):
            return (LP[:, 6144:] if s == EXTRA else ring[s][:, 2 * PIECE:]).rearrange("p (k n) -> p k n", k=FT)

        def flat(ap):
            return ap.rearrange("p a b -> p (a b)")

        def overflow(eng):
            eng.wait_ge(counted, 1)
            return eng.If(eng.value_load(most[0:1, 0:1], min_val=0, max_val=SEQ) > SLOTS)

        Z = [("q", gp, i) for gp in range(2) for i in range(4)] + [("k", 2, b) for b in range(2)]
        Z += [("av", 2, t) for t in range(TILES)]
        Z += [("m", 3 + b // 4, b) for b in range(8)]
        Z += [("mv", g, t) for g in (5, 6) for t in range(TILES)]
        Z += [("if", None, t) for t in range(TILES)]
        Z += [("mo", g, t) for g in (7, 8) for t in range(TILES)]
        ZG = [("g", g, t) for g in range(9, 13) for t in range(TILES)]
        by_act = [u[0] in ("q", "k", "m") for u in Z]
        units_of = [[n for n, u in enumerate(Z) if u[1] == g] for g in range(9)]
        units_of.append([n for n, u in enumerate(Z) if u[1] is None])

        def splits_between(n):
            return Z[n][0] == "m" and Z[n][2] % 4 == 3

        def z_bank(n):
            g = next(g for g, us in enumerate(units_of) if n in us)
            if g == 9:
                return PS[:, 6 + units_of[g].index(n), :]
            return PS[:, 4 * (g % 2) + units_of[g].index(n), :]

        PT_BANKS = {(0, 0): 3, (0, 1): 6, (1, 0): 4, (1, 1): 8, (2, 0): 2, (2, 1): 4}
        PT_BASE, PT_A, PT_D, n_ps, n_a, n_d = {}, {}, {}, 0, 0, 0
        for key, banks in PT_BANKS.items():
            PT_BASE[key], PT_A[key], PT_D[key] = n_ps, n_a, n_d
            n_ps, n_a, n_d = n_ps + banks, n_a + banks // 2, n_d + (banks + 1) // 2

        block = ctx.enter_context(nc.Block())

        @block.sync
        def _(eng):
            by_row, by_tile = "(p k) f -> p k f", "(k p) f -> p k f"

            def load(n, moe_over=False):
                src, c, kh = PIECES[n]
                if n >= STEPS:
                    eng.wait_ge(split_lo, n - STEPS + 1)
                if moe_over and n < BEFORE_MOE + STEPS:
                    eng.wait_ge(ex_down, 2 * PAIRS - 2)
                if src in ("ffn1", "ffn2"):
                    part, c = c, kh
                    w = A[f"{src}_w_{part}_2"][0]
                    if part == "down":
                        cut = w[c * HIDDEN:(c + 1) * HIDDEN, :].rearrange("(p k) n -> p (k n)", k=FT)
                        eng.dma_start(raw_piece(n), cut).then_inc(piece_loaded[n % STEPS], 16)
                        return
                    cut = w[:, c * HIDDEN:(c + 1) * HIDDEN].rearrange(by_row, k=KT)
                else:
                    lo = c * HALF if src != "w_in_2" or c < 9 else C_G + (c - 9) * HALF
                    w = A[src if src in ("w_in", "w_out", "w_in_2", "w_out_2") else src + "_2"][0]
                    order = by_row if src in ("w_in", "w_in_2") else by_tile
                    cut = w.rearrange(order, k=KT)[:, kh * KH:(kh + 1) * KH, lo:lo + HALF]
                eng.dma_start(raw_piece(n).rearrange("p (k f) -> p k f", k=cut.shape[1]), cut
                              ).then_inc(piece_loaded[n % STEPS], 16)

            def load_gate_up(s, e, done):
                for j, w in enumerate(("w_gate", "w_up")):
                    eng.dma_start((extra_gate_up if s == EXTRA else ring[s])[:, j * PIECE:(j + 1) * PIECE],
                                  A[w][0, bass.ds(e, 1)].rearrange("a (p k) f -> p (a k f)", k=KT)).then_inc(done, 16)

            def load_down(s, e, done):
                eng.dma_start(LP[:, 6144:] if s == EXTRA else ring[s][:, 2 * PIECE:], A["w_down"][0, bass.ds(e, 1)].rearrange(
                    "a (p k) n -> p (a k n)", k=FT)).then_inc(done, 16)

            for t in range(TILES):
                eng.dma_start(res[:, t, :], A["x"][0, t * P:(t + 1) * P, :]).then_inc(x_loaded[t], 16)
            for n in range(STEPS):
                load(n)
            b_in = A["b_in_2"][0]
            n_vec = [0]

            def load_vec(dst, src):
                eng.dma_start(dst, src).then_inc(vec_loaded, 16)
                n_vec[0] += 1

            bq = b_in[0:C_K].rearrange("(g m i d) -> m g i d", g=2, m=2, i=4)
            for m in range(2):
                for g in range(2):
                    load_vec(vec_rows[V_BQ + 4 * g:V_BQ + 4 * g + 4, HEAD * m:HEAD * m + HEAD], bq[m, g])
            load_vec(vec_rows[V_BK:V_BM, :], b_in[C_K:C_AV].rearrange("(r p) -> r p", p=P))
            load_vec(vec_rows[V_BM:V_CONV, :], b_in[C_MQ:C_MV].rearrange("(r p) -> r p", p=P))
            for j in range(CONV):
                load_vec(vec_rows[V_CONV + 8 * j:V_CONV + 8 * j + 8, :],
                         A["mlstm_conv_2"][0, j].rearrange("(r p) -> r p", p=P))
            for n, name in enumerate(("diff_q_g", "diff_k_g", "moba_q_g", "moba_k_g")):
                for m in range(2):
                    load_vec(vec_rows[V_QK + n:V_QK + n + 1, HEAD * m:HEAD * m + HEAD], A[name][0:1, :])
            load_vec(vec_rows[V_SUB:V_SUB + 1, :], A["diff_sub_g"][0:1, :])
            assert n_vec[0] == N_VEC
            eng.dma_start(relx[0:BUCKETS, :], A["rel_bias"]).then_inc(rel_loaded, 16)
            eng.dma_start(onehot[:, :], buckets).then_inc(rel_loaded, 16)
            for n, name in enumerate(("lambda_q1", "lambda_k1", "lambda_q2", "lambda_k2")):
                eng.dma_start(lam_rows[:, n, :], A[name][0].partition_broadcast(P)).then_inc(lam_loaded, 16)
            eng.dma_start(router[:, :, 0:GROUPS], A["router_group"][0].rearrange("(p k) g -> p k g", k=KT)).then_inc(router_loaded, 16)
            for g in range(GROUPS):
                eng.dma_start(router[:, :, GROUPS + PER_GROUP * g:GROUPS + PER_GROUP * (g + 1)],
                              A["router_expert"][0, g].rearrange("(p k) e -> p k e", k=KT)).then_inc(router_loaded, 16)
            eng.dma_start(w_if[:, :, :], A["w_in_2"][0, :, C_IF:C_G].rearrange("(p k) f -> p k f", k=KT)).then_inc(if_loaded, 16)
            eng.dma_start(b_if[:, :], b_in[C_IF:C_G].partition_broadcast(P)).then_inc(if_loaded, 16)
            eng.dma_start(sink_nat[:, :], A["attn_sinks_2"][0].partition_broadcast(P)).then_inc(if_loaded, 16)
            for n in range(STEPS, BEFORE_MOE):
                load(n)
            eng.wait_ge(piece_used, first["w_out"])
            load_gate_up(EXTRA, RING, extra_loaded)
            eng.wait_ge(split_lo, BEFORE_MOE)
            load_gate_up(0, 0, gate_up_loaded[0])
            load_down(0, 0, down_loaded[0])
            eng.wait_ge(piece_used, BEFORE_MOE)
            for s in range(1, RING):
                load_gate_up(s, s, gate_up_loaded[s])
                load_down(s, s, down_loaded[s])
            load_down(EXTRA, RING, extra_loaded)

            def next_experts(it, u, slots, later=()):
                turns = [(s, it) for s in slots] + [(s, it + 1) for s in later]
                eng.wait_ge(ex_gu, it * 2 + (u - 1))
                for s, turn in turns:
                    load_gate_up(s, turn * RING + s, gate_up_loaded[s])
                eng.wait_ge(ex_down, it * 4 + (2 * u - 2))
                for s, turn in turns:
                    load_down(s, turn * RING + s, down_loaded[s])

            next_experts(1, 0, (1,), later=(0,))
            next_experts(1, 1, (2, 3))
            next_experts(2, 0, (1,))
            next_experts(2, 1, (2, 3))
            with eng.Fori(3, EXPERTS // RING) as it:
                for u in range(2):
                    next_experts(it, u, (2 * u, 2 * u + 1))
            with overflow(eng):
                eng.wait_ge(ex_down, 2 * PAIRS)
                with eng.Fori(0, ROUNDS - 1) as r:
                    with eng.Fori(0, PAIRS) as i:
                        eng.wait_ge(ov_step, r * (PAIRS + 1) + i + 2)
                        for m in range(2):
                            load_gate_up(m, 2 * i + m, ov_loaded)
                            load_down(m, 2 * i + m, ov_loaded)
                eng.wait_ge(ov_down, 2 * (ROUNDS - 1) * PAIRS)
            for n in range(BEFORE_MOE, len(PIECES)):
                load(n, True)
            for t in range(TILES):
                eng.wait_ge(normed, TILES * NFIN + t + 1)
                eng.dma_start(out[0, t * P:(t + 1) * P, :], tok[:, t, :]).then_inc(out_stored, 16)
            eng.wait_ge(out_stored, 16 * TILES)

        @block.gpsimd
        def _(eng):
            seq = [0]

            def link(ins):
                seq[0] += 1
                ins.then_inc(pool_seq, 1)
                eng.wait_ge(pool_seq, seq[0])

            def load_gain(name):
                eng.dma_start(gain[:, :], A[name].rearrange("a d -> (a d)").partition_broadcast(P)
                              if name != "final_norm_2" else A[name].partition_broadcast(P)).then_inc(gain_loaded, 16)

            roots = [0]

            def root(dst):
                roots[0] += 1
                eng.wait_ge(root_in, roots[0])
                eng.tensor_tensor(dst, dst, minus_half[:, 0:dst.shape[1]], ALU.pow).then_inc(root_out, 1)
                eng.wait_ge(root_out, roots[0])

            def norm_root(k):
                for t in range(TILES):
                    root(rstd[:, TILES * k + t:TILES * k + t + 1])

            load_gain("norm1_g")
            link(eng.memset(minus_half[:, :], -0.5))
            link(eng.memset(ones[:, :], 1.0))
            link(eng.memset(ident[:, :], 0.0))
            link(eng.affine_select(out=ident[:, :], in_=ident[:, :], compare_op=ALU.not_equal, fill=1.0,
                                   base=0, pattern=[[-1, P]], channel_multiplier=1))
            for m, base in ((upto, 0), (before, -1)):
                link(eng.affine_select(out=m[:, :], in_=ones[:, :], compare_op=ALU.is_ge, fill=0.0,
                                       base=base, pattern=[[1, P]], channel_multiplier=-1))
            link(eng.memset(masks[:, :], 0.0))
            for lo in (P, 3 * P):
                link(eng.affine_select(out=masks[:, lo:lo + P], in_=masks[:, lo:lo + P], compare_op=ALU.is_ge,
                                       fill=MASKED, base=0, pattern=[[-1, P]], channel_multiplier=1))
            link(eng.affine_select(out=masks[:, 2 * P:3 * P], in_=masks[:, 2 * P:3 * P], compare_op=ALU.is_gt,
                                   fill=MASKED, base=0, pattern=[[1, P]], channel_multiplier=-1))
            link(eng.iota(iota_i[:, :], pattern=[[1, SLOTS]], base=0, channel_multiplier=0))
            link(eng.tensor_copy(iota[:, :], iota_i[:, :]))
            eng.memset(relx[BUCKETS:BUCKETS + 1, :], MASKED).then_inc(consts, 1)
            eng.wait_ge(consts, 1)
            norm_root(N1)

            for _ in range(2 * TILES):
                root(hs[:, 0, 1, 0:8])
            eng.wait_ge(bias_copied, N_BIAS)
            eng.dma_start(bias_rows.rearrange("h p m -> p h m"), bias_stage).then_inc(bias_stored, 16)
            eng.wait_ge(bias_stored, 16)
            skewed = bass.AP(tensor=bias_rows.tensor, offset=P - 1,
                             ap=[[DIST_COLS - 1, P], [P * DIST_COLS, N_BIAS], [1, SEQ]])
            eng.dma_start(bias, skewed).then_inc(bias_loaded, 16)
            eng.wait_ge(normed, TILES * (N1 + 1))
            load_gain("norm2_g")
            for _ in range(2 * TILES):
                root(hs[:, 0, 1, 0:8])
            for t in range(TILES):
                root(hs[:, t, 7, 4:8])
            norm_root(N2)
            eng.wait_ge(normed, TILES * (N2 + 1))
            load_gain("ffn1_norm_2")
            eng.wait_ge(moe_added, TILES)
            norm_root(NF1)
            b_in = A["b_in_2"][0]
            eng.dma_start(bias_av, b_in[C_AV:C_MQ].partition_broadcast(P)).then_inc(bb_loaded, 16)
            eng.dma_start(bias_mvo, b_in[C_MV:C_IF].partition_broadcast(P)).then_inc(bb_loaded, 16)
            eng.wait_ge(normed, TILES * (NF1 + 1))
            load_gain("mix_norm_2")
            norm_root(NMIX)
            eng.wait_ge(normed, TILES * (NMIX + 1))
            eng.dma_start(gain[:, :], A["mlstm_head_norm_2"].rearrange("a h v -> (a h v)").partition_broadcast(P)
                          ).then_inc(gain_loaded, 16)
            for t in range(TILES):
                eng.wait_ge(sig_done, t + 1)
                eng.wait_ge(gain_loaded, 16 * GB["hm"])
                eng.tensor_tensor(mo[:, t, :], mo[:, t, :], gain[:, :], ALU.mult).then_inc(gated_gain, 1)
                eng.wait_ge(gated_gain, t + 1)
            for t in range(TILES):
                root(hs[:, t, 3, 8:16])
            eng.wait_ge(mixed, 3 * TILES)
            eng.dma_start(bias_g, b_in[C_G:C_END].partition_broadcast(P)).then_inc(bb_loaded, 16)
            load_gain("ffn2_norm_2")
            norm_root(NF2)
            eng.wait_ge(normed, TILES * (NF2 + 1))
            load_gain("final_norm_2")
            norm_root(NFIN)

        @block.scalar
        def _(eng):
            seq = [0]

            def link(ins):
                seq[0] += 1
                ins.then_inc(act_seq, 1)
                eng.wait_ge(act_seq, seq[0])

            def square(k, ready):
                for t in range(TILES):
                    eng.wait_ge(*ready(t))
                    eng.activation(tok[:, t, :], res[:, t, :], ACT.Square,
                                   accum_out=ss[:, TILES * k + t:TILES * k + t + 1]).then_inc(squared, 1)

            done = [0]

            def split_at(n, slot, turn, permute=False):
                eng.wait_ge(piece_loaded[slot], turn * 16 + 16)
                if not isinstance(n, int) or n >= STEPS:
                    eng.wait_ge(piece_used, n - (STEPS - 1))
                raw = raw_w[:, slot * PIECE:(slot + 1) * PIECE]
                if permute:
                    for m in range(2):
                        ins = eng.activation(by_pairs_split(w_hi[:, slot, :])[:, :, :, m], by_pairs(raw)[:, :, m], ACT.Copy)
                else:
                    ins = eng.activation(w_hi[:, slot, :], raw, ACT.Copy)
                ins.then_inc(split_hi, 1)

            def split(n):
                if BEFORE_MOE <= n < BEFORE_MOE + STEPS:
                    eng.wait_ge(ex_down, 2 * PAIRS)
                split_at(n, n % STEPS, n // STEPS, PIECES[n][0] == "w_in_2" and PIECES[n][1] < 2)

            def feed(q, limit=len(PIECES)):
                while done[0] < min(q + STEPS, limit):
                    split(done[0])
                    done[0] += 1

            def t8_split(u, dst, scale=None):
                for t in range(TILES):
                    eng.wait_ge(t8, TILES * u + t + 1)
                    src = PS[:, 4 + 2 * t:6 + 2 * t, :].rearrange("p b (k q) -> p (b k) q", q=P)
                    to = dst[0][:, :, t * P:(t + 1) * P]
                    if scale is None:
                        eng.activation(to, src, ACT.Copy).then_inc(t8_hi, 1)
                    else:
                        eng.activation(to[:, 0:4], src[:, 0:4], ACT.Copy, scale=scale)
                        eng.activation(to[:, 4:8], src[:, 4:8], ACT.Copy).then_inc(t8_hi, 1)

            def pT_copy(key):
                for b in range(1, PT_BANKS[key], 2):
                    eng.wait_ge(pT_ps, PT_BASE[key] + b + 1)
                    to = (MPT if key[0] == 2 else PT)[key[1]]
                    eng.activation(flat(to[:, 4 * b:4 * b + 4, :]), PS[:, 4 + b % 4, :], ACT.Copy).then_inc(pT_a, 1)

            square(N1, lambda t: (x_loaded[t], 16))
            feed(0, 1)
            t8_split(T_N1, hT)
            feed(0)

            units = [(c, t) for c in (0, 1, 3, 4) for t in range(TILES)]
            def qk_copies(c):
                for n, (uc, t) in enumerate(units):
                    if uc != c:
                        continue
                    w = n // TILES
                    if n == 0:
                        eng.wait_ge(vec_ready, 1)
                    eng.wait_ge(qk_ps, n + 1)
                    eng.activation(qkT[w][:, :, t * P:(t + 1) * P], PS[:, 4 + n % 2, :].rearrange("p (j q) -> p j q", j=4),
                                   ACT.Copy, scale=vec[:, V_QK + w:V_QK + w + 1]).then_inc(qk_done, 1)

            for c in range(6):
                for n, (uc, t) in enumerate(units):
                    if uc != c - 1:
                        continue
                    eng.wait_ge(piece_used, 2 * c)
                    if n >= 2:
                        eng.wait_ge(proj_sq_read, n - 1)
                    eng.activation(tok[:, t, HALF:], PS[:, (TILES * (c - 1) + t) % 4, :], ACT.Square).then_inc(proj_sq, 1)
                feed(2 * c)
                qk_copies(c - 2)
                feed(2 * c + 1, BEFORE_MOE)
                if c == 3:
                    eng.wait_ge(lam_sum, 1)
                    eng.activation(lam[:, 2:4], lam[:, 0:2], ACT.Exp).then_inc(lam_exp, 1)
                    eng.wait_ge(router_loaded, 16 * (1 + GROUPS))
                    eng.activation(router_parts[:, :, 0:ROUTES], router[:, :, :], ACT.Copy).then_inc(small_hi, 1)
                    eng.wait_ge(if_loaded, 48)
                    eng.activation(w_if_parts[0][:, :, :], w_if[:, :, :], ACT.Copy).then_inc(small_hi, 1)
            qk_copies(4)
            feed(12, BEFORE_MOE)

            def exps(t, half, row):
                n = P * (t + 1)
                for a in range(8 * half, 8 * half + 8):
                    eng.activation(L[t][:, a, 0:n], L[t][:, a, 0:n], ACT.Exp, bias=hs[:, t, row, a:a + 1],
                                   accum_out=hs[:, t, row + 1, a:a + 1]).then_inc(expd, 1)

            for t in range(TILES):
                for half in range(2):
                    eng.wait_ge(maxed, 2 * t + half + 1)
                    exps(t, half, 1)
            for t in range(TILES):
                pT_copy((0, t))
                eng.wait_ge(pv, 2 * t + 1)
                eng.activation(flat(L[t])[:, 0:HALF], PS[:, 2 * t, :], ACT.Square).then_inc(pv_sq, 1)
            t8_split(T_Y, yT, vec[:, V_SUB:V_SUB + 1])
            feed(13, BEFORE_MOE)

            square(N2, lambda t: (gemm_used, 3 + t))
            t8_split(T_N2, routed_T)
            for t in range(TILES):
                eng.activation(tok_parts[0][:, t], tok[:, t, :].rearrange("p (d k) -> p k d", k=KT), ACT.Copy).then_inc(tok_hi, 1)
            eng.wait_ge(route_exp_in, 1)
            for t in range(TILES):
                eng.activation(rt[:, t, 80:84], rt8[:, t, 0, 0:4], ACT.Exp, bias=rt[:, t, 84:85],
                               accum_out=rt[:, t, 85:86])
            eng.activation(rt[:, :, 86:87], rt[:, :, 87:88], ACT.Exp).then_inc(route_exp, 1)

            def gathered(it, kh):
                eng.wait_ge(ex_gath, 2 * it + (kh + 1))
                eng.activation(flat(xgT[:, kh * KH:(kh + 1) * KH, :]), flat(PS[:, 4:6, :]), ACT.Copy).then_inc(ex_xT, 1)

            def expert_pair(it, u, more):
                j = it * 2 + u
                eng.wait_ge(ex_gu, j + 1)
                eng.activation(act_e, PS[:, 6, 0:HIDDEN], ACT.Silu).then_inc(ex_act, 1)
                if u and more:
                    for kh in range(2):
                        gathered(it + 1, kh)
                eng.wait_ge(ex_selTc, j + 1)
                for x, h in enumerate((1, 0)):
                    eng.wait_ge(ex_down, j * 2 + (x + 1))
                    eng.activation(exo[0][:, h * HALF:(h + 1) * HALF], PS[:, 7 - h, :], ACT.Copy,
                                   scale=wslot[:, 0:1]).then_inc(ex_hi, 1)

            for kh in range(2):
                gathered(0, kh)
            for u in range(2):
                expert_pair(0, u, True)
            with eng.Fori(1, PAIRS // 2 - 1) as it:
                for u in range(2):
                    expert_pair(it, u, True)
            for u in range(2):
                expert_pair(PAIRS // 2 - 1, u, False)
            with overflow(eng):
                with eng.Fori(0, ROUNDS - 1) as r:
                    with eng.Fori(0, PAIRS) as i:
                        j = r * PAIRS + i
                        eng.wait_ge(ov_gath, j + 1)
                        eng.activation(xgT[:, :, 0:P], PS[:, 4:6, :].rearrange("p b (k s) -> p (b k) s", s=P),
                                       ACT.Copy).then_inc(ov_xT, 1)
                        eng.wait_ge(ov_gu, j + 1)
                        eng.activation(act_e, PS[:, 6, 0:HIDDEN], ACT.Silu).then_inc(ov_act, 1)
                        eng.wait_ge(ov_selTc, j + 1)
                        for x, h in enumerate((1, 0)):
                            eng.wait_ge(ov_down, j * 2 + (x + 1))
                            eng.activation(exo[0][:, h * HALF:(h + 1) * HALF], PS[:, 7 - h, :], ACT.Copy,
                                           scale=wslot[:, 0:1]).then_inc(ov_hi, 1)

            def ffn(f):
                base, g0 = first[("ffn1", "ffn2")[f]], f * CHUNKS

                def silu(c, n):
                    eng.wait_ge(piece_used, n + 1)
                    eng.activation(flat(act_f), PS[:, 4, :], ACT.Silu).then_inc(ff_act, 1)

                def hidden_T(c):
                    eng.wait_ge(ff_hT, c + (g0 + 1))
                    eng.activation(flat(hidT_f[0][:, :, :]), PS[:, 6, :], ACT.Copy).then_inc(ff_hTh, 1)

                def chunk(c, n, parts):
                    parts(2)
                    hidden_T(c - 1)
                    parts(3)
                    silu(c, n)
                    parts(4)

                def part_of(n):
                    return lambda j: feed(n + j - 2)

                def part_in_loop(c):
                    return lambda j: split_at(c * 3 + (base - 1 + j), (base - 1 + j) % STEPS, c + (base - 1 + j) // STEPS)

                feed(base)
                silu(0, base)
                feed(base + 1)
                chunk(1, base + 2, part_of(base + 2))
                with eng.Fori(2, CHUNKS - 1) as c:
                    chunk(c, c * 3 + (base - 1), part_in_loop(c))
                last = base + 3 * (CHUNKS - 1) - 1
                done[0] = last + 2
                chunk(CHUNKS - 1, last, part_of(last))
                hidden_T(CHUNKS - 1)
                feed(last + 3)

            feed(BEFORE_MOE, BEFORE_MOE + 1)
            square(NF1, lambda t: (moe_added, t + 1))
            feed(BEFORE_MOE, BEFORE_MOE + 2)
            t8_split(T_F1, hT)
            feed(BEFORE_MOE)
            ffn(0)

            square(NMIX, lambda t: (ff_added, 2 * t + 2))
            t8_split(T_MIX, hT)
            n_silu = [0]

            def silu_conv():
                b = n_silu[0]
                eng.wait_ge(conv_done, b + 1)
                eng.activation(mqk[:, b, :], conv[:, b % 2, :], ACT.Silu).then_inc(conv_silu, 1)
                n_silu[0] += 1

            def take(g):
                for n in units_of[g]:
                    kind, _, i = Z[n]
                    if splits_between(n):
                        feed(first["w_in_2"] + 2 * g + 3)
                    if not by_act[n]:
                        continue
                    eng.wait_ge(piece_used, first["w_in_2"] + 2 * g + 2)
                    src = z_bank(n)[:, 0:SEQ]
                    if kind == "q":
                        eng.activation(sqT[:, 4 * g + i, :], src, ACT.Identity, scale=SCALE,
                                       bias=vec[:, V_BQ + 4 * g + i:V_BQ + 4 * g + i + 1]).then_inc(z_act, 1)
                    elif kind == "k":
                        eng.activation(skT[:, i, :], src, ACT.Identity, bias=vec[:, V_BK + i:V_BK + i + 1]).then_inc(z_act, 1)
                    else:
                        if i >= 2:
                            eng.wait_ge(conv_done, i - 1)
                        eng.activation(raw[:, i % 2, CONV - 1:], src, ACT.Identity,
                                       bias=vec[:, V_BM + i:V_BM + i + 1]).then_inc(z_act, 1)
                        if i >= 1:
                            silu_conv()
                        if i == 7:
                            silu_conv()

            for g in range(9):
                feed(first["w_in_2"] + 2 * g)
                if g:
                    take(g - 1)
                feed(first["w_in_2"] + 2 * g + 1)
                if g == 7:
                    eng.wait_ge(z_dve, sum(not a for a in by_act[:units_of[9][-1] + 1]))
                    link(eng.activation(ga[:, :, 1, :], ga[:, :, 0, :], ACT.Tanh, scale=1.0 / SOFTCAP))
                    eng.activation(ga[:, :, 2, 8:16], ga[:, :, 1, 8:16], ACT.Exp, scale=-SOFTCAP).then_inc(gates_exp, 1)
            eng.wait_ge(gates_u, 1)
            eng.activation(ga[:, :, 3, 8:16], ga[:, :, 3, 0:8], ACT.Ln).then_inc(gates_exp, 1)
            feed(first["w_in_2"] + 18)
            eng.wait_ge(z_dve, sum(not a for a in by_act))
            for t in range(TILES):
                eng.activation(mo[:, t, :], mo[:, t, :], ACT.Sigmoid).then_inc(sig_done, 1)
            for t in range(TILES):
                for half in range(2):
                    mine = slice(8 * half, 8 * half + 8)
                    eng.wait_ge(maxed, 2 * TILES + 2 * t + half + 1)
                    exps(t, half, 1)
                    eng.activation(hs[:, t, 4, mine], hs[:, t, 3, mine], ACT.Exp).then_inc(sink_exp, 1)
            def attention_rows(t):
                for g in range(2):
                    eng.wait_ge(pv, 4 + 2 * t + g + 1)
                    eng.activation(yT[0][:, 4 * g:4 * g + 4, t * P:(t + 1) * P],
                                   PS[:, 2 * t + g, :].rearrange("p (k q) -> p k q", q=P), ACT.Copy).then_inc(sy_hi, 1)

            pT_copy((1, 0))
            attention_rows(0)
            pT_copy((1, 1))
            for t in range(TILES):
                if t == 1:
                    attention_rows(1)
                eng.wait_ge(ml_max, t + 1)
                n = P * (t + 1)
                for a in range(MLSTM_HEADS):
                    eng.activation(ML[t][:, a, 0:n], ML[t][:, a, 0:n], ACT.Exp, bias=hs[:, t, 1, a:a + 1]).then_inc(ml_exp, 1)
                eng.activation(hs[:, t, 5, 0:8], hs[:, t, 4, 0:8], ACT.Exp, scale=-1.0).then_inc(ml_exp, 1)
            for t in range(TILES):
                pT_copy((2, t))
                eng.wait_ge(ml_h, t + 1)
                eng.activation(head_squares, tok[:, t, :], ACT.Square).then_inc(ml_hsq, 1)
            def sigmoids(j):
                for t in range(TILES):
                    eng.wait_ge(g_sig, TILES * j + t + 1)
                    x = gates[:, t, j * HALF:(j + 1) * HALF]
                    eng.activation(x, x, ACT.Sigmoid).then_inc(sig_done, 1)

            for j in range(4):
                feed(first["w_in_2"] + 18 + 2 * j)
                if j:
                    sigmoids(j - 1)
                feed(first["w_in_2"] + 18 + 2 * j + 1)
            feed(first["w_proj_attn"])
            sigmoids(3)
            t8_split(T_HM, hT)
            for n in range(first["w_proj_attn"], first["w_out_2"] + 1):
                feed(n)
            t8_split(T_MG, yT)
            for n in range(first["w_out_2"] + 1, first["ffn2"]):
                feed(n)
            square(NF2, lambda t: (gemm_used, 4 + 3 + t))
            t8_split(T_F2, hT)
            ffn(1)
            square(NFIN, lambda t: (ff_added, 4 + 2 * t + 2))

        @block.tensor
        def _(eng):
            def product(dst, x, w, first_one, last_one):
                eng.matmul(dst, x[0], w[0], start=first_one, stop=False)
                eng.matmul(dst, x[0], w[1], start=False, stop=False)
                return eng.matmul(dst, x[1], w[0], start=False, stop=last_one)

            def stay_warm(n, bank):
                for _ in range(n):
                    eng.matmul(PS[:, bank, 0:P], ident[:, :], ident[:, :], start=True, stop=True)

            def both(parts, cut):
                return [cut(x) for x in parts]

            def transpose8(u, src, ready, strided, idle=(0, 0)):
                for t in range(TILES):
                    stay_warm(idle[t], 6)
                    eng.wait_ge(*ready(t))
                    for k in range(KT):
                        cut = src[:, t, k:D:KT] if strided else src[:, t, k * P:(k + 1) * P]
                        mm = eng.transpose(PS[:, 4 + 2 * t + k // 4, (k % 4) * P:(k % 4 + 1) * P], cut, ident[:, :])
                    mm.then_inc(t8, 1)

            def copied8(u):
                eng.wait_ge(t8_lo, TILES * (u + 1))

            def half_gemm(n, dst, src, kh, u=None, last=False):
                eng.wait_ge(split_lo, n + 1)
                for t in range(TILES):
                    if u is not None and kh == 0:
                        eng.wait_ge(t8_lo, TILES * u + t + 1)
                    for k in range(KH):
                        mm = product(dst(t), both(src, lambda x: x[:, kh * KH + k, t * P:(t + 1) * P]),
                                     both((w_hi, w_lo), lambda w: cols(w, n)[:, k, :]),
                                     kh == 0 and k == 0, kh == 1 and k == KH - 1)
                    if last and t == 0:
                        mm.then_inc(first_tile, 1)
                mm.then_inc(piece_used, 1)

            eng.wait_ge(consts, 1)
            transpose8(T_N1, tok, lambda t: (normed, TILES * N1 + t + 1), True, (12, 4))
            eng.wait_ge(vec_loaded, 16 * N_VEC)
            eng.transpose(PS[:, 3, 0:V_ROWS], vec_rows[:, :], ident[0:V_ROWS, 0:V_ROWS]).then_inc(vec_T, 1)
            stay_warm(14, 2)

            qk_groups = (0, 1, 3, 4)

            def qk_transposes(c):
                for t in range(TILES):
                    n = TILES * qk_groups.index(c) + t
                    eng.wait_ge(proj_used, TILES * c + t + 1)
                    if n >= 2:
                        eng.wait_ge(qk_done, n - 1)
                    for b in range(4):
                        mm = eng.transpose(PS[:, 4 + n % 2, b * P:(b + 1) * P], tok[:, t, b * P:(b + 1) * P], ident[:, :])
                    mm.then_inc(qk_ps, 1)

            for c in range(6):
                if c == 1:
                    eng.wait_ge(vec_ready, 1)
                if c >= 2:
                    eng.wait_ge(proj_used, TILES * (c - 1))
                for kh in range(2):
                    half_gemm(2 * c + kh, lambda t: PS[:, (TILES * c + t) % 4, :], hT, kh, T_N1)
                    if kh == 1 and c - 1 in qk_groups:
                        qk_transposes(c - 1)
                    if kh == 0 and c == 3:
                        eng.wait_ge(rel_wide, 1)
                        for h in range(N_BIAS):
                            if h >= 2:
                                eng.wait_ge(bias_copied, h - 1)
                            eng.matmul(PS[:, 6 + h % 2, 0:DIST_COLS], relb[:, h, :], onehot[:, :], start=True, stop=True
                                       ).then_inc(bias_ps, 1)

            def scores(base, t, q, k, pairs):
                n = P * (t + 1)
                for g in range(pairs):
                    if t > 0 or g >= 2:
                        eng.wait_ge(score_used, base + g - 1)
                    for m in range(2):
                        a, b = HEAD * m, HEAD * (m + 1)
                        mm = eng.matmul(PS[:, 2 * (g % 2) + m, 0:n], q(g)[a:b, t * P:(t + 1) * P], k(g)[a:b, 0:n],
                                        start=True, stop=True)
                    mm.then_inc(score, 1)

            def weight_transposes(key, blocks, ready):
                assert (len(blocks) + 3) // 4 == PT_BANKS[key]
                for x, (a, kb) in enumerate(blocks):
                    j = x // 4
                    if x % 4 == 0 and j >= 4:
                        done, base = (pT_a, PT_A[key]) if j % 2 else (pT_d, PT_D[key])
                        eng.wait_ge(done, base + (j - 4) // 2 + 1)
                    if kb == 0:
                        eng.wait_ge(*ready(a))
                    src = (ML if key[0] == 2 else L)[key[1]]
                    mm = eng.transpose(PS[:, 4 + j % 4, (x % 4) * P:(x % 4 + 1) * P],
                                       src[:, a, kb * P:(kb + 1) * P], ident[:, :])
                    if x % 4 == 3 or x == len(blocks) - 1:
                        mm.then_inc(pT_ps, 1)
                banks = PT_BANKS[key]
                eng.wait_ge(pT_a, PT_A[key] + banks // 2)
                eng.wait_ge(pT_d, PT_D[key] + (banks + 1) // 2)

            eng.wait_ge(qk_done, 8)
            eng.wait_ge(proj_used, 6 * TILES)
            eng.wait_ge(bias_copied, N_BIAS)
            for t in range(TILES):
                scores(8 * t, t, lambda g: qkT[2 * (g // 4)][:, g % 4, :], lambda g: qkT[2 * (g // 4) + 1][:, g % 4, :], 8)
            for t in range(TILES):
                maps = [2 * j for j in range(4)] + list(range(8, MAPS))
                blocks = [(a, kb) for a in maps for kb in range(t + 1)]

                if t == 0:
                    stay_warm(20, 7)
                weight_transposes((0, t), blocks, lambda a: (weighted, 4 * t + a // 2 + 1) if a < 8
                                  else (expd, MAPS * t + a + 1))
                eng.wait_ge(score_used, 8 * TILES)
                for u in range(12):
                    for kb in range(t + 1):
                        lhs = PT[t][:, u * (t + 1) + kb, :]
                        if u < 4:
                            dst, v = PS[:, 2 * t, u * P:(u + 1) * P], vals[:, kb, u * P:(u + 1) * P]
                        else:
                            h = u - 4
                            dst, v = PS[:, 2 * t + 1, h * HEAD:(h + 1) * HEAD], vals[:, kb, HALF + h * HEAD:HALF + (h + 1) * HEAD]
                        mm = eng.matmul(dst, lhs, v, start=(kb == 0), stop=(kb == t))
                    if u == 3 or u == 11:
                        mm.then_inc(pv, 1)
            transpose8(T_Y, tok, lambda t: (mixed, 2 * t + 2), False)

            def gemm_1024(v, src, u, name):
                if u is None:
                    eng.wait_ge(sy_lo, 2 * TILES)
                bank = 4 if v == G_PM else 0
                for h in range(HALVES):
                    if v == G_PA and h == 1:
                        eng.wait_ge(g_sig, len(ZG))
                    for kh in range(2):
                        half_gemm(first[name] + 2 * h + kh, lambda t: PS[:, bank + 2 * h + t, :], src, kh, u,
                                  v != G_PA and h == 1 and kh == 1)

            eng.wait_ge(mixed, 2 * TILES)
            gemm_1024(G_OUT, yT, T_Y, "w_out")

            eng.wait_ge(gemm_used, 3)
            stay_warm(10, 0)
            transpose8(T_N2, tok, lambda t: (normed, TILES * N2 + t + 1), True)
            stay_warm(8, 2)
            copied8(T_N2)
            eng.wait_ge(small_lo, 1)
            for t in range(TILES):
                for k in range(KT):
                    for x in range(2):
                        mm = eng.matmul(PS[:, t, 0:2 * ROUTES], routed_T[x][:, k, t * P:(t + 1) * P], router_parts[:, k, :],
                                        start=(k == 0 and x == 0), stop=(k == KT - 1 and x == 1))
                mm.then_inc(route, 1)
            stay_warm(12, 3)
            eng.wait_ge(assigned, 1)
            eng.matmul(PS[:, 2, 0:EXPERTS], before[:, :], assign[:, 0, 2, :], start=True, stop=True)
            eng.matmul(PS[:, 2, EXPERTS:2 * EXPERTS], ones[:, :], assign[:, 0, 2, :], start=True, stop=False)
            eng.matmul(PS[:, 2, EXPERTS:2 * EXPERTS], before[:, :], assign[:, 1, 2, :], start=False, stop=True).then_inc(pos_ps, 1)
            for t in range(TILES):
                mm = eng.matmul(PS[:, 3, 0:EXPERTS], ones[:, :], assign[:, t, 2, :], start=(t == 0), stop=(t == TILES - 1))
            mm.then_inc(pos_ps, 1)

            def gather(it, kh):
                if kh == 0:
                    eng.wait_ge(sel_ready, it + 1)
                for k in range(KH):
                    dst = PS[:, 4 + k // 2, (k % 2) * SEQ:(k % 2 + 1) * SEQ]
                    for t in range(TILES):
                        for x in range(2):
                            mm = eng.matmul(dst, tok_parts[x][:, t, kh * KH + k, :], sel[:, t, :],
                                            start=(t == 0 and x == 0), stop=(t == 1 and x == 1))
                mm.then_inc(ex_gath, 1)

            def combine(u, first_one, last_one, done, tile_done=None):
                for t in range(TILES):
                    for h in range(HALVES):
                        for x in range(2):
                            mm = eng.matmul(PS[:, 2 * t + h, :], selT[:, u, t * P:(t + 1) * P],
                                            exo[x][:, h * HALF:(h + 1) * HALF], start=(first_one and x == 0),
                                            stop=(last_one and x == 1))
                    if tile_done is not None and t == 0:
                        mm.then_inc(tile_done, 1)
                mm.then_inc(done, 1)

            def gate_and_up_pair(slots, at, done):
                for k in range(KT):
                    for m, s in enumerate(slots):
                        mm = eng.matmul(PS[SLOTS * m:SLOTS * (m + 1), 6, :], xgT[:, k, at + SLOTS * m:at + SLOTS * (m + 1)],
                                        gate_up(s)[:, k], start=(k == 0), stop=(k == KT - 1))
                mm.then_inc(done, 1)

            def transposed_pair(done):
                for t in range(TILES):
                    eng.transpose(PS[:, 7, SEQ + t * P:SEQ + (t + 1) * P], selw[:, t, :], ident[:, :])
                for k in range(FT):
                    mm = eng.transpose(PS[:, 7, k * P:(k + 1) * P], hid_e[:, k:HIDDEN:FT], ident[:, :])
                mm.then_inc(done, 1)

            def down_pair(slots, h, done):
                for k in range(FT):
                    for m, s in enumerate(slots):
                        mm = eng.matmul(PS[SLOTS * m:SLOTS * (m + 1), 7 - h, :], hidT_e[:, k, SLOTS * m:SLOTS * (m + 1)],
                                        down(s)[:, k, h * HALF:(h + 1) * HALF], start=(k == 0), stop=(k == FT - 1))
                mm.then_inc(done, 1)

            def expert_pair(it, u, more, first_one=False, extra=False):
                j, slots = it * 2 + u, [2 * u, 2 * u + 1]
                turns = [it, it]
                if u == 0 and not first_one:
                    turns[0] = it - 1
                if extra:
                    slots[0] = EXTRA
                if u == 0:
                    eng.wait_ge(ex_xT, it * 2 + 2)
                for s, turn in zip(slots, turns):
                    if s == EXTRA:
                        eng.wait_ge(extra_loaded, 48)
                    else:
                        eng.wait_ge(gate_up_loaded[s], turn * 32 + 32)
                if not (first_one and u == 0):
                    eng.wait_ge(ex_lo, j * 2 - 1)
                gate_and_up_pair(slots, P * u, ex_gu)
                if not (first_one and u == 0):
                    eng.wait_ge(ex_lo, j * 2)
                    combine(1 - u, first_one and u == 1, False, ex_sum)
                if more and u == 0:
                    gather(it + 1, 0)
                eng.wait_ge(selw_ready, j * 2 + 2)
                eng.wait_ge(ex_hid, j + 1)
                transposed_pair(ex_hT)
                if more and u == 1:
                    eng.wait_ge(ex_xT, it * 2 + 3)
                    gather(it + 1, 1)
                for s, turn in zip(slots, turns):
                    if s != EXTRA:
                        eng.wait_ge(down_loaded[s], turn * 16 + 16)
                eng.wait_ge(ex_hTc, j + 1)
                down_pair(slots, 1, ex_down)
                eng.wait_ge(ex_selTc, j + 1)
                down_pair(slots, 0, ex_down)

            for t in range(TILES):
                eng.wait_ge(tok_lo, t + 1)
            stay_warm(4, 6)
            gather(0, 0)
            stay_warm(4, 6)
            eng.wait_ge(ex_xT, 1)
            gather(0, 1)
            stay_warm(4, 6)
            for u in range(2):
                expert_pair(0, u, True, True)
            for u in range(2):
                expert_pair(1, u, True, extra=(u == 0))
            with eng.Fori(2, PAIRS // 2 - 1) as it:
                for u in range(2):
                    expert_pair(it, u, True)
            for u in range(2):
                expert_pair(PAIRS // 2 - 1, u, False)
            eng.wait_ge(ex_lo, 2 * PAIRS)
            combine(1, False, True, ex_sum, first_rows)

            with overflow(eng):
                with eng.Fori(0, ROUNDS - 1) as r:
                    with eng.Fori(0, PAIRS) as i:
                        j = r * PAIRS + i
                        eng.wait_ge(ov_sel, j + 1)
                        for k in range(KT):
                            for t in range(TILES):
                                for x in range(2):
                                    mm = eng.matmul(PS[:, 4 + k // 4, (k % 4) * P:(k % 4 + 1) * P], tok_parts[x][:, t, k, :],
                                                    sel[:, t, 0:P], start=(t == 0 and x == 0), stop=(t == 1 and x == 1))
                        mm.then_inc(ov_gath, 1)
                        eng.wait_ge(ov_xT, j + 1)
                        eng.wait_ge(ov_loaded, 96 * j + 96)
                        gate_and_up_pair((0, 1), 0, ov_gu)
                        eng.wait_ge(ov_hid, j + 1)
                        transposed_pair(ov_hT)
                        eng.wait_ge(ov_hTc, j + 1)
                        down_pair((0, 1), 1, ov_down)
                        eng.wait_ge(ov_selTc, j + 1)
                        down_pair((0, 1), 0, ov_down)
                        eng.wait_ge(ov_lo, j * 2 + 2)
                        eng.wait_ge(ov_added, j + 1)
                        combine(0, True, True, ex_sum)

            def ffn(f, u):
                base, g0 = first[("ffn1", "ffn2")[f]], f * CHUNKS

                def hidden_columns(x, slot, side, t):
                    for k in range(KT):
                        mm = product(PS[:, 4 + side, t * HIDDEN:(t + 1) * HIDDEN],
                                     both(hT, lambda h: h[:, k, t * P:(t + 1) * P]),
                                     both((w_hi, w_lo), lambda w: hidden(w, slot)[:, k, :]), k == 0, k == KT - 1)
                    return mm

                def transposes(c):
                    eng.wait_ge(ff_hid, c + (g0 + 1))
                    for t in range(TILES):
                        for k in range(FT):
                            mm = eng.transpose(PS[:, 6, k * SEQ + t * P:k * SEQ + (t + 1) * P],
                                               hid_f[:, t, k:HIDDEN:FT], ident[:, :])
                    mm.then_inc(ff_hT, 1)

                def down_chunk(c, slot, first_one, last_one):
                    eng.wait_ge(ff_hTl, c + (g0 + 1))
                    for t in range(TILES):
                        for h in range(HALVES):
                            for k in range(FT):
                                mm = product(PS[:, 2 * t + h, :], both(hidT_f, lambda x: x[:, k, t * P:(t + 1) * P]),
                                             both((w_hi, w_lo), lambda w: down_piece(w, slot)[:, k, h * HALF:(h + 1) * HALF]),
                                             first_one and k == 0, last_one and k == FT - 1)
                        if last_one and t == 0:
                            mm.then_inc(first_tile, 1)
                    mm.then_inc(piece_used, 1)

                def chunk(c, n, slot, first_one=False):
                    eng.wait_ge(split_lo, n + 1)
                    eng.wait_ge(ff_act, c + g0)
                    hidden_columns(hT, slot, 0, 0)
                    transposes(c - 1)
                    hidden_columns(hT, slot, 0, 1).then_inc(piece_used, 1)
                    eng.wait_ge(split_lo, n + 2)
                    down_chunk(c - 1, slot + 1, first_one, False)
                    eng.wait_ge(split_lo, n + 3)
                    for t in range(TILES):
                        mm = hidden_columns(hT, slot + 2, 1, t)
                    mm.then_inc(piece_used, 1)

                for side in range(2):
                    eng.wait_ge(split_lo, base + side + 1)
                    for t in range(TILES):
                        if side == 0:
                            eng.wait_ge(t8_lo, TILES * u + t + 1)
                        mm = hidden_columns(hT, base + side, side, t)
                    mm.then_inc(piece_used, 1)
                chunk(1, base + 2, base + 2, True)
                with eng.Fori(2, CHUNKS - 1) as c:
                    chunk(c, c * 3 + (base - 1), base + 2)
                last = base + 3 * (CHUNKS - 1) - 1
                chunk(CHUNKS - 1, last, last)
                transposes(CHUNKS - 1)
                eng.wait_ge(split_lo, last + 4)
                down_chunk(CHUNKS - 1, last + 3, False, True)

            transpose8(T_F1, tok, lambda t: (normed, TILES * NF1 + t + 1), True, (22, 4))
            stay_warm(9, 0)
            ffn(0, T_F1)

            transpose8(T_MIX, tok, lambda t: (normed, TILES * NMIX + t + 1), True, (13, 4))
            stay_warm(11, 0)
            copied8(T_MIX)

            def all_taken(us):
                last = us[-1] + 1
                if sum(by_act[:last]):
                    eng.wait_ge(z_act, sum(by_act[:last]))
                if last - sum(by_act[:last]):
                    eng.wait_ge(z_dve, last - sum(by_act[:last]))

            for g in range(9):
                if g >= 2:
                    all_taken(units_of[g - 2])
                for kh in range(2):
                    p = first["w_in_2"] + 2 * g + kh
                    eng.wait_ge(split_lo, p + 1)
                    for n in units_of[g]:
                        kind, _, i = Z[n]
                        for k in range(KH):
                            x = both(hT, lambda h: h[:, kh * KH + k, :])
                            w = both((w_hi, w_lo), lambda w: cols(w, p)[:, k, :])
                            flags = (kh == 0 and k == 0, kh == 1 and k == KH - 1)
                            if kind in ("q", "k", "m"):
                                mm = product(z_bank(n)[:, 0:SEQ], both(w, lambda a: a[:, i % 4 * P:(i % 4 + 1) * P]), x, *flags)
                            else:
                                lo = 256 if kind == "av" else 0
                                mm = product(z_bank(n)[:, 0:HALF - lo], both(x, lambda a: a[:, i * P:(i + 1) * P]),
                                             both(w, lambda a: a[:, lo:]), *flags)
                    mm.then_inc(piece_used, 1)
                if g == 6:
                    eng.wait_ge(small_lo, 2)
                    for n in units_of[9]:
                        i = Z[n][2]
                        for k in range(KT):
                            mm = product(z_bank(n)[:, 0:16], both(hT, lambda h: h[:, k, i * P:(i + 1) * P]),
                                         both(w_if_parts, lambda w: w[:, k, :]), k == 0, k == KT - 1)
                        mm.then_inc(z_unit, 1)
            eng.wait_ge(z_dve, sum(not x for x in by_act))
            eng.wait_ge(z_act, sum(by_act))
            for t in range(TILES):
                scores(16 + 8 * t, t, lambda g: sqT[:, g, :], lambda g: skT[:, g // 4, :], 8)
            eng.wait_ge(gates_ready, 1)
            eng.matmul(PS[:, 6, 0:8], upto[:, :], ga[:, 0, 6, 8:16], start=True, stop=True).then_inc(cum_ps, 1)
            eng.matmul(PS[:, 7, 0:8], ones[:, :], ga[:, 0, 6, 8:16], start=True, stop=False)
            eng.matmul(PS[:, 7, 0:8], upto[:, :], ga[:, 1, 6, 8:16], start=False, stop=True).then_inc(cum_ps, 1)
            for t in range(TILES):
                eng.wait_ge(a_ready, t + 1)
                mm = eng.transpose(PS[0:8, 5, t * P:(t + 1) * P], ga[:, t, 7, 8:16], ident[:, :])
            mm.then_inc(a_ps, 1)
            eng.wait_ge(a_copied, 1)
            stay_warm(13, 5)

            def gate_rows(t):
                n = P * (t + 1)
                for j in range(4):
                    if t > 0:
                        eng.wait_ge(ml_used, 4 * (t - 1) + j + 1)
                    for m in range(2):
                        mm = eng.matmul(PS[:, 4 + j, m * SEQ:m * SEQ + n], ident[0:8, 2 * j + m:2 * j + m + 1].broadcast_to([8, P]),
                                        aT[:, 0:n], start=True, stop=True)
                    mm.then_inc(ml_a, 1)

            for t in range(TILES):
                place = lambda h: 8 * (h // 8) + 2 * (h % 4) + h % 8 // 4
                weight_transposes((1, t), [(place(4 * kv + 2 * i + m), kb) for kv in range(KV_HEADS) for m in range(2)
                                           for kb in range(t + 1) for i in range(2)],
                                  lambda a: (weighed, 2 * t + a // 8 + 1))
                if t == TILES - 1:
                    gate_rows(0)
                eng.wait_ge(score_used, 8 * TILES * 2)
                for kv in range(KV_HEADS):
                    for kb in range(t + 1):
                        for m in range(2):
                            b = 2 * ((2 * kv + m) * (t + 1) + kb)
                            mm = eng.matmul(PS[HEAD * m:HEAD * (m + 1), 2 * t + kv // 2, kv % 2 * SEQ:(kv % 2 + 1) * SEQ],
                                            sv[:, kb, kv * HEAD:(kv + 1) * HEAD], flat(PT[t][:, b:b + 2, :]),
                                            start=(kb == 0), stop=(kb == t))
                    if kv % 2:
                        mm.then_inc(pv, 1)
            gate_rows(1)
            eng.wait_ge(conv_silu, 8)
            eng.wait_ge(sy_lo, 2 * TILES)
            for t in range(TILES):
                n = P * (t + 1)
                for j in range(4):
                    if t > 0 or j >= 2:
                        eng.wait_ge(ml_sc, 8 * t + 2 * (j - 1))
                    for m in range(2):
                        a, b = HEAD * m, HEAD * (m + 1)
                        mm = eng.matmul(PS[:, 2 * (j % 2) + m, 0:n], mqk[a:b, j, t * P:(t + 1) * P], mqk[a:b, 4 + j, 0:n],
                                        start=True, stop=True)
                    mm.then_inc(ml_s, 1)
            eng.wait_ge(ml_used, 4 * TILES)
            for t in range(TILES):
                weight_transposes((2, t), [(a, kb) for a in range(MLSTM_HEADS) for kb in range(t + 1)],
                                  lambda a: (ml_sc, 8 * t + a + 1))
                eng.wait_ge(ml_sc, 8 * TILES)
                for a in range(MLSTM_HEADS):
                    for kb in range(t + 1):
                        mm = eng.matmul(PS[:, 2 * t + a // 4, (a % 4) * P:(a % 4 + 1) * P], MPT[t][:, a * (t + 1) + kb, :],
                                        mv[:, kb, a * P:(a + 1) * P], start=(kb == 0), stop=(kb == t))
                    if a % 4 == 3:
                        mm.then_inc(pv, 1)
            for j in range(4):
                if j < 2:
                    eng.wait_ge(ml_h, j + 1)
                else:
                    eng.wait_ge(g_sig, TILES * (j - 1))
                for kh in range(2):
                    half_gemm(first["w_in_2"] + 18 + 2 * j + kh, lambda t: PS[:, 2 * (j % 2) + t, :], hT, kh)
            transpose8(T_HM, tok, lambda t: (mixed, 4 + t + 1), False)
            eng.wait_ge(g_sig, 3 * TILES)
            gemm_1024(G_PA, yT, None, "w_proj_attn")
            gemm_1024(G_PM, hT, T_HM, "w_proj_mlstm")
            transpose8(T_MG, tok, lambda t: (merged, 3 + t), False)
            stay_warm(12, 0)
            gemm_1024(G_OUT2, yT, T_MG, "w_out_2")
            transpose8(T_F2, tok, lambda t: (normed, TILES * NF2 + t + 1), True, (13, 4))
            ffn(1, T_F2)

        @block.vector
        def _(eng):
            seq, roots = [0], [0]

            def link(ins):
                seq[0] += 1
                ins.then_inc(dve_seq, 1)
                eng.wait_ge(dve_seq, seq[0])

            def wide(ap, n):
                return ap.unsqueeze(len(ap.shape)).broadcast_to([*ap.shape, n])

            def rsqrt(dst, sums, n):
                roots[0] += 1
                eng.tensor_scalar(dst, sums, 1.0 / n, EPS, ALU.mult, ALU.add).then_inc(root_in, 1)
                eng.wait_ge(root_out, roots[0])

            def mean_root(c):
                eng.wait_ge(squared, c + 1)
                roots[0] += 1
                eng.tensor_scalar(rstd[:, c:c + 1], ss[:, c:c + 1], 1.0 / D, EPS, ALU.mult, ALU.add).then_inc(root_in, 1)
                return roots[0]

            def norm(k, add=lambda t: None):
                def scaled(t, root):
                    eng.wait_ge(root_out, root)
                    eng.wait_ge(gain_loaded, 16 * GB[k])
                    eng.scalar_tensor_tensor(tok[:, t, :], res[:, t, :], rstd[:, TILES * k + t:TILES * k + t + 1], gain[:, :],
                                             ALU.mult, ALU.mult).then_inc(normed, 1)

                add(0)
                root = mean_root(TILES * k)
                add(1)
                scaled(0, root)
                scaled(1, mean_root(TILES * k + 1))

            done = [0]

            def split_at(n, slot, permute=False):
                eng.wait_ge(split_hi, n + 1)
                raw = raw_w[:, slot * PIECE:(slot + 1) * PIECE]
                if permute:
                    for m in range(2):
                        ins = eng.tensor_tensor(by_pairs_split(w_lo[:, slot, :])[:, :, :, m], by_pairs(raw)[:, :, m],
                                                by_pairs_split(w_hi[:, slot, :])[:, :, :, m], ALU.subtract)
                else:
                    ins = eng.tensor_tensor(w_lo[:, slot, :], raw, w_hi[:, slot, :], ALU.subtract)
                ins.then_inc(split_lo, 1)

            def feed(q, limit=len(PIECES)):
                while done[0] < min(q + STEPS, limit):
                    n = done[0]
                    split_at(n, n % STEPS, PIECES[n][0] == "w_in_2" and PIECES[n][1] < 2)
                    done[0] += 1

            def t8_split(u, dst, scale=None):
                for t in range(TILES):
                    eng.wait_ge(t8_hi, TILES * u + t + 1)
                    src = PS[:, 4 + 2 * t:6 + 2 * t, :].rearrange("p b (k q) -> p (b k) q", q=P)
                    hi, lo = [x[:, :, t * P:(t + 1) * P] for x in dst]
                    if scale is None:
                        eng.tensor_tensor(lo, src, hi, ALU.subtract).then_inc(t8_lo, 1)
                    else:
                        eng.scalar_tensor_tensor(lo[:, 0:4], src[:, 0:4], scale, hi[:, 0:4], ALU.mult, ALU.subtract)
                        eng.tensor_tensor(lo[:, 4:8], src[:, 4:8], hi[:, 4:8], ALU.subtract).then_inc(t8_lo, 1)

            def pT_copy(key):
                for b in range(0, PT_BANKS[key], 2):
                    eng.wait_ge(pT_ps, PT_BASE[key] + b + 1)
                    to, n = (MPT if key[0] == 2 else PT)[key[1]], min(4, 4 * PT_BANKS[key] - 4 * b)
                    eng.tensor_copy(flat(to[:, 4 * b:4 * b + n, :]), PS[:, 4 + b % 4, 0:n * P]).then_inc(pT_d, 1)

            def add_to_residual(name, h, t, tile=None):
                if tile is not None and t == 0:
                    eng.wait_ge(first_tile, tile)
                else:
                    eng.wait_ge(piece_used, first[name] + 2 * h + 2)
                x = res[:, t, h * HALF:(h + 1) * HALF]
                eng.tensor_tensor(x, x, PS[:, 2 * h + t, :], ALU.add).then_inc(gemm_used, 1)

            link(eng.memset(rt8[:, :, 0, :], -3e38))
            norm(N1)
            feed(0, 1)
            t8_split(T_N1, hT)
            eng.wait_ge(vec_T, 1)
            link(eng.tensor_copy(vec[:, :], PS[:, 3, 0:V_ROWS]))
            for c, n, f in ((V_BQ, 8, SCALE), (V_QK, 1, SCALE), (V_QK + 2, 1, SCALE)):
                link(eng.tensor_scalar(vec[:, c:c + n], vec[:, c:c + n], f, None, ALU.mult))
            eng.tensor_scalar(vec[:, V_SUB:V_SUB + 1], vec[:, V_SUB:V_SUB + 1], 1.0 - LAMBDA_INIT, None,
                              ALU.mult).then_inc(vec_ready, 1)
            feed(0)
            eng.wait_ge(rel_loaded, 32)
            eng.tensor_copy(relb[:, :, :], wide(relx[:, :], P)).then_inc(rel_wide, 1)
            eng.wait_ge(lam_loaded, 64)
            for n in range(2):
                ins = eng.tensor_tensor_reduce(lam_rows[:, 2 * n, :], lam_rows[:, 2 * n, :], lam_rows[:, 2 * n + 1, :], 1.0, 0.0,
                                               ALU.mult, ALU.add, lam[:, n:n + 1])
            ins.then_inc(lam_sum, 1)

            n_qk = [0]

            def take_projection(c):
                eng.wait_ge(piece_used, 2 * c + 2)
                for t in range(TILES):
                    bank, n = PS[:, (TILES * c + t) % 4, :], n_qk[0]
                    if c in (2, 5):
                        lo = 0 if c == 2 else HALF
                        eng.tensor_copy(vals[:, t, lo:lo + HALF], bank).then_inc(proj_used, 1)
                        continue
                    eng.wait_ge(proj_sq, n + 1)
                    eng.tensor_reduce(hs[:, 0, 0, 0:8], tok[:, t, HALF:].rearrange("p (h d) -> p h d", d=HEAD),
                                      AX_X, ALU.add).then_inc(proj_sq_read, 1)
                    eng.wait_ge(proj_sq_read, n + 1)
                    rsqrt(hs[:, 0, 1, 0:8], hs[:, 0, 0, 0:8], HEAD)
                    if n >= 2:
                        eng.wait_ge(qk_ps, n - 1)
                    eng.tensor_tensor(tok[:, t, 0:HALF].rearrange("p (h d) -> p h d", d=HEAD),
                                      bank.rearrange("p (h d) -> p h d", d=HEAD), wide(hs[:, 0, 1, 0:8], HEAD),
                                      ALU.mult).then_inc(proj_used, 1)
                    n_qk[0] += 1

            for c in range(6):
                feed(2 * c)
                if c:
                    take_projection(c - 1)
                if c == 3:
                    for h in range(N_BIAS):
                        eng.wait_ge(bias_ps, h + 1)
                        eng.tensor_copy(bias_stage[:, h, :], PS[:, 6 + h % 2, 0:DIST_COLS]).then_inc(bias_copied, 1)
                feed(2 * c + 1, BEFORE_MOE)
                if c == 4:
                    eng.wait_ge(lam_exp, 1)
                    link(eng.tensor_tensor(lam[:, 4:5], lam[:, 2:3], lam[:, 3:4], ALU.subtract))
                    link(eng.tensor_scalar(lam[:, 5:6], lam[:, 4:5], LAMBDA_INIT, -1.0, ALU.add, ALU.mult))
                    eng.wait_ge(small_hi, 2)
                    eng.tensor_tensor(router_parts[:, :, ROUTES:], router[:, :, :], router_parts[:, :, 0:ROUTES],
                                      ALU.subtract).then_inc(small_lo, 1)
                    eng.tensor_tensor(w_if_parts[1][:, :, :], w_if[:, :, :], w_if_parts[0][:, :, :], ALU.subtract).then_inc(small_lo, 1)
                    link(eng.tensor_copy(sink[:, :].rearrange("p (g i m) -> p g m i", g=2, i=4),
                                         sink_nat[:, :].rearrange("p (g m i) -> p g m i", g=2, m=2)))
            take_projection(5)
            feed(12, BEFORE_MOE)

            eng.wait_ge(bias_loaded, 16)

            def masked_logits(t):
                n = P * (t + 1)
                for g in range(8):
                    eng.wait_ge(score, 8 * t + g + 1)
                    b = 2 * (g % 2)
                    if g < 4:
                        add = bias[:, g:g + 1, SEQ - n:].broadcast_to([P, 2, n])
                    else:
                        add = bias[:, DIFF_HEADS + 2 * (g - 4):DIFF_HEADS + 2 * (g - 4) + 2, SEQ - n:]
                    eng.tensor_tensor(L[t][:, 2 * g:2 * g + 2, 0:n], PS[:, b:b + 2, 0:n], add, ALU.add).then_inc(score_used, 1)
                    if g % 4 == 3:
                        mine = slice(2 * g - 6, 2 * g + 2)
                        eng.wait_ge(score_used, 8 * t + g + 1)
                        link(eng.tensor_reduce(hs[:, t, 0, mine], L[t][:, mine, 0:n], AX_X, ALU.max))
                        eng.tensor_scalar(hs[:, t, 1, mine], hs[:, t, 0, mine], -1.0, None, ALU.mult).then_inc(maxed, 1)

            def differential_weights(t):
                n = P * (t + 1)
                eng.wait_ge(expd, MAPS * t + 2 * DIFF_HEADS)
                link(eng.reciprocal(hs[:, t, 5, 0:8], hs[:, t, 2, 0:8]))
                link(eng.tensor_scalar(hs[:, t, 6, 0:4], hs[:, t, 5, 1:8:2], lam[:, 5:6], None, ALU.mult))
                for j in range(DIFF_HEADS):
                    ins = eng.tensor_scalar(L[t][:, 2 * j, 0:n], L[t][:, 2 * j, 0:n], hs[:, t, 5, 2 * j:2 * j + 1], None, ALU.mult)
                link(ins)
                for j in range(DIFF_HEADS):
                    eng.scalar_tensor_tensor(L[t][:, 2 * j, 0:n], L[t][:, 2 * j + 1, 0:n], hs[:, t, 6, j:j + 1], L[t][:, 2 * j, 0:n],
                                             ALU.mult, ALU.add).then_inc(weighted, 1)

            def normed_heads(t):
                eng.wait_ge(expd, MAPS * (t + 1))
                eng.reciprocal(hs[:, t, 5, 8:16], hs[:, t, 2, 8:16])
                eng.wait_ge(pv_sq, t + 1)
                link(eng.tensor_reduce(hs[:, t, 7, 0:4], flat(L[t])[:, 0:HALF].rearrange("p (h c) -> p h c", h=4), AX_X, ALU.add))
                rsqrt(hs[:, t, 7, 4:8], hs[:, t, 7, 0:4], 2 * HEAD)
                eng.tensor_tensor(tok[:, t, 0:HALF].rearrange("p (h c) -> p h c", h=4),
                                  PS[:, 2 * t, :].rearrange("p (h c) -> p h c", h=4), wide(hs[:, t, 7, 4:8], P),
                                  ALU.mult).then_inc(mixed, 1)
                eng.wait_ge(pv, 2 * t + 2)
                eng.tensor_tensor(tok[:, t, HALF:].rearrange("p (h c) -> p h c", h=8),
                                  PS[:, 2 * t + 1, :].rearrange("p (h c) -> p h c", h=8), wide(hs[:, t, 5, 8:16], HEAD),
                                  ALU.mult).then_inc(mixed, 1)

            for t in range(TILES):
                masked_logits(t)
            differential_weights(0)
            pT_copy((0, 0))
            differential_weights(1)
            pT_copy((0, 1))
            normed_heads(0)
            normed_heads(1)
            t8_split(T_Y, yT, vec[:, V_SUB:V_SUB + 1])
            feed(13, BEFORE_MOE)
            for t in range(TILES):
                add_to_residual("w_out", 0, t)

            norm(N2, lambda t: add_to_residual("w_out", 1, t, 1))
            t8_split(T_N2, routed_T)
            for t in range(TILES):
                eng.wait_ge(tok_hi, t + 1)
                eng.tensor_tensor(tok_parts[1][:, t], tok[:, t, :].rearrange("p (d k) -> p k d", k=KT), tok_parts[0][:, t],
                                  ALU.subtract).then_inc(tok_lo, 1)
            eng.wait_ge(route, TILES)
            ONE = lambda c: rt[:, :, c:c + 1]
            each = range(TILES)
            link(eng.tensor_copy(rt[:, :, 4:40], PS[:, 0:TILES, 0:ROUTES]))
            link(eng.tensor_tensor(rt[:, :, 4:40], rt[:, :, 4:40], PS[:, 0:TILES, ROUTES:2 * ROUTES], ALU.add))
            link(eng.tensor_copy(rt8[:, :, 0, 0:GROUPS], rt[:, :, 4:4 + GROUPS]))
            link([eng.max(rt8[:, t, 1, :], rt8[:, t, 0, :]) for t in each][-1])
            eng.tensor_scalar(ONE(84), rt8[:, :, 1, 0:1], -1.0, None, ALU.mult)
            link([eng.max_index(rt8u[:, t, 0, :], rt8[:, t, 1, :], rt8[:, t, 0, :]) for t in each][-1])
            link(eng.tensor_copy(ONE(88), rt8u[:, :, 0, 0:1]))
            eng.tensor_scalar(ONE(91), ONE(88), float(PER_GROUP), None, ALU.mult)
            link(eng.tensor_tensor(rt[:, :, 40:44], iota[:, 0:GROUPS].unsqueeze(1).broadcast_to([P, TILES, GROUPS]),
                                   rt[:, :, 88:89].broadcast_to([P, TILES, GROUPS]), ALU.is_equal))
            link(eng.tensor_tensor(rt[:, :, 8:40].rearrange("p t (g e) -> p t g e", g=GROUPS),
                                   rt[:, :, 8:40].rearrange("p t (g e) -> p t g e", g=GROUPS),
                                   wide(rt[:, :, 40:44], PER_GROUP), ALU.mult))
            link(eng.tensor_reduce(rt[:, :, 0:8], rt[:, :, 8:40].rearrange("p t (g e) -> p t e g", g=GROUPS), AX_X, ALU.add))
            link([eng.max(rt8[:, t, 2, :], rt[:, t, 0:8]) for t in each][-1])
            eng.tensor_tensor(ONE(87), rt8[:, :, 2, 1:2], rt8[:, :, 2, 0:1], ALU.subtract).then_inc(route_exp_in, 1)
            link([eng.max_index(rt8u[:, t, 1, :], rt8[:, t, 2, :], rt[:, t, 0:8]) for t in each][-1])
            link(eng.tensor_copy(rt[:, :, 89:91], rt8u[:, :, 1, 0:2]))
            link(eng.tensor_tensor(rt[:, :, 89:91], rt[:, :, 89:91], rt[:, :, 91:92].broadcast_to([P, TILES, 2]), ALU.add))
            link(eng.tensor_tensor(assign[:, :, 0:2, :], iota[:, 0:EXPERTS].unsqueeze(1).unsqueeze(1).broadcast_to([P, TILES, 2, EXPERTS]),
                                   wide(rt[:, :, 89:91], EXPERTS), ALU.is_equal))
            eng.tensor_tensor(assign[:, :, 2, :], assign[:, :, 0, :], assign[:, :, 1, :], ALU.add).then_inc(assigned, 1)
            eng.wait_ge(pos_ps, 1)
            eng.wait_ge(assigned, 1)
            link(eng.scalar_tensor_tensor(posn[:, :, 1, :], PS[:, 2, 0:TILES * EXPERTS].rearrange("p (t e) -> p t e", t=TILES),
                                          1.0, assign[:, :, 2, :], ALU.add, ALU.mult))
            link(eng.tensor_scalar(posn[:, :, 1, :], posn[:, :, 1, :], -1.0, None, ALU.add))

            def select(it):
                eng.tensor_tensor(sel[:, :, :].rearrange("p t (e c) -> p t e c", e=RING),
                                  iota[:, :].unsqueeze(1).unsqueeze(1).broadcast_to([P, TILES, RING, SLOTS]),
                                  wide(posn[:, :, 1, bass.ds(it * RING, RING)], SLOTS), ALU.is_equal).then_inc(sel_ready, 1)

            def select_weighted(i, done, count):
                cut = selw.rearrange("p t (e c) -> p t e c", e=2)
                eng.tensor_tensor(cut, iota[:, :].unsqueeze(1).unsqueeze(1).broadcast_to([P, TILES, 2, SLOTS]),
                                  wide(posn[:, :, 1, bass.ds(i * 2, 2)], SLOTS), ALU.is_equal).then_inc(done, 1)
                eng.wait_ge(done, count)
                return eng.tensor_tensor(cut, cut, wide(wtok[:, :, bass.ds(i * 2, 2)], SLOTS), ALU.mult)

            def slot_weights(u, done):
                src = PS[:, 7, SEQ:]
                eng.tensor_scalar(selT[:, u, :], src, 0.0, None, ALU.is_gt)
                eng.tensor_reduce(wslot[:, :], src, AX_X, ALU.add).then_inc(done, 1)

            def rest_of_rows(h, done):
                cut = slice(h * HALF, (h + 1) * HALF)
                eng.scalar_tensor_tensor(exo[1][:, cut], PS[:, 7 - h, :], wslot[:, 0:1], exo[0][:, cut],
                                         ALU.mult, ALU.subtract).then_inc(done, 1)

            def expert_pair(it, u, more, first_one=False):
                j = it * 2 + u
                if not (first_one and u == 0):
                    eng.wait_ge(ex_hT, j)
                select_weighted(j, selw_ready, j * 2 + 1).then_inc(selw_ready, 1)
                eng.wait_ge(ex_act, j + 1)
                eng.tensor_tensor(hid_e, act_e, PS[:, 6, HIDDEN:], ALU.mult).then_inc(ex_hid, 1)
                eng.wait_ge(ex_hT, j + 1)
                eng.tensor_copy(flat(hidT_e), PS[:, 7, 0:HIDDEN]).then_inc(ex_hTc, 1)
                slot_weights(u, ex_selTc)
                if more and u == 1:
                    eng.wait_ge(ex_gath, it * 2 + 4)
                    select(it + 2)
                for x, h in enumerate((1, 0)):
                    eng.wait_ge(ex_hi, j * 2 + (x + 1))
                    rest_of_rows(h, ex_lo)

            select(0)
            eng.wait_ge(route_exp, 1)
            eng.tensor_scalar(ONE(94), ONE(86), 1.0, None, ALU.add)
            link(eng.reciprocal(ONE(91), ONE(85)))
            link(eng.reciprocal(ONE(95), ONE(94)))
            link(eng.tensor_tensor(ONE(92), ONE(91), ONE(95), ALU.mult))
            link(eng.tensor_tensor(ONE(93), ONE(92), ONE(86), ALU.mult))
            link(eng.tensor_tensor(assign[:, :, 0:2, :], assign[:, :, 0:2, :], wide(rt[:, :, 92:94], EXPERTS), ALU.mult))
            link(eng.tensor_tensor(wtok[:, :, :], assign[:, :, 0, :], assign[:, :, 1, :], ALU.add))
            eng.wait_ge(pos_ps, 2)
            link(eng.tensor_reduce(most_f[:, :], PS[:, 3, 0:EXPERTS], AX_X, ALU.max))
            eng.tensor_copy(most[:, :], most_f[:, :]).then_inc(counted, 1)
            eng.wait_ge(ex_gath, 2)
            select(1)
            for u in range(2):
                expert_pair(0, u, True, True)
            with eng.Fori(1, PAIRS // 2 - 2) as it:
                for u in range(2):
                    expert_pair(it, u, True)
            for it in range(PAIRS // 2 - 2, PAIRS // 2):
                for u in range(2):
                    expert_pair(it, u, False)

            def add_rows(t, done):
                for h in range(HALVES):
                    x = res[:, t, h * HALF:(h + 1) * HALF]
                    ins = eng.tensor_tensor(x, x, PS[:, 2 * t + h, :], ALU.add)
                ins.then_inc(done, 1)

            with overflow(eng):
                with eng.Fori(0, ROUNDS - 1) as r:
                    eng.tensor_scalar(posn[:, :, 1, :], posn[:, :, 1, :], -float(SLOTS), None, ALU.add).then_inc(ov_step, 1)
                    with eng.Fori(0, PAIRS) as i:
                        j = r * PAIRS + i
                        eng.wait_ge(ov_step, r * (PAIRS + 1) + i + 1)
                        eng.tensor_tensor(sel[:, :, 0:P].rearrange("p t (e c) -> p t e c", e=2),
                                          iota[:, :].unsqueeze(1).unsqueeze(1).broadcast_to([P, TILES, 2, SLOTS]),
                                          wide(posn[:, :, 1, bass.ds(i * 2, 2)], SLOTS), ALU.is_equal)
                        select_weighted(i, ov_step, r * (PAIRS + 1) + i + 2).then_inc(ov_sel, 1)
                        eng.wait_ge(ov_act, j + 1)
                        eng.tensor_tensor(hid_e, act_e, PS[:, 6, HIDDEN:], ALU.mult).then_inc(ov_hid, 1)
                        eng.wait_ge(ov_hT, j + 1)
                        eng.tensor_copy(flat(hidT_e), PS[:, 7, 0:HIDDEN]).then_inc(ov_hTc, 1)
                        slot_weights(0, ov_selTc)
                        for x, h in enumerate((1, 0)):
                            eng.wait_ge(ov_hi, j * 2 + (x + 1))
                            rest_of_rows(h, ov_lo)
                        eng.wait_ge(ex_sum, j + PAIRS)
                        for t in range(TILES):
                            add_rows(t, ov_tile)
                            eng.wait_ge(ov_tile, j * 2 + t + 1)
                        eng.tensor_copy(most_f[:, :], ones[:, 0:1]).then_inc(ov_added, 1)
                eng.wait_ge(ex_sum, ROUNDS * PAIRS)

            def ffn(f):
                base, g0 = first[("ffn1", "ffn2")[f]], f * CHUNKS

                def hidden_units(c):
                    eng.wait_ge(piece_used, c * 3 + (base + 2))
                    eng.wait_ge(ff_act, c + (g0 + 1))
                    eng.tensor_tensor(flat(hid_f), flat(act_f), PS[:, 5, :], ALU.mult).then_inc(ff_hid, 1)

                def hidden_T(c):
                    eng.wait_ge(ff_hTh, c + (g0 + 1))
                    eng.tensor_tensor(flat(hidT_f[1][:, :, :]), PS[:, 6, :], flat(hidT_f[0][:, :, :]), ALU.subtract).then_inc(ff_hTl, 1)

                def chunk(c, parts):
                    hidden_units(c - 1)
                    parts(2)
                    hidden_T(c - 1)
                    parts(3)
                    parts(4)

                def part_of(n):
                    return lambda j: feed(n + j - 2)

                def part_in_loop(c):
                    return lambda j: split_at(c * 3 + (base - 1 + j), (base - 1 + j) % STEPS)

                feed(base)
                feed(base + 1)
                chunk(1, part_of(base + 2))
                with eng.Fori(2, CHUNKS - 1) as c:
                    chunk(c, part_in_loop(c))
                last = base + 3 * (CHUNKS - 1) - 1
                done[0] = last + 2
                chunk(CHUNKS - 1, part_of(last))
                hidden_units(CHUNKS - 1)
                hidden_T(CHUNKS - 1)
                feed(last + 3)

                def add(t):
                    if t == 0:
                        eng.wait_ge(first_tile, 3 * f + 2)
                    else:
                        eng.wait_ge(piece_used, last + 4)
                    for h in range(HALVES):
                        x = res[:, t, h * HALF:(h + 1) * HALF]
                        eng.scalar_tensor_tensor(x, PS[:, 2 * t + h, :], 0.5, x, ALU.mult, ALU.add).then_inc(ff_added, 1)

                return add

            def add_experts(t):
                if t == 0:
                    eng.wait_ge(first_rows, 1)
                else:
                    eng.wait_ge(ex_sum, PAIRS)
                add_rows(t, moe_added)

            norm(NF1, add_experts)
            feed(BEFORE_MOE, BEFORE_MOE + 1)
            t8_split(T_F1, hT)
            feed(BEFORE_MOE)
            add = ffn(0)

            norm(NMIX, add)
            t8_split(T_MIX, hT)
            eng.wait_ge(bb_loaded, 32)
            eng.memset(raw[:, :, 0:CONV - 1], 0.0).then_inc(pad_zeroed, 1)

            def take(g):
                if g < 9:
                    eng.wait_ge(piece_used, first["w_in_2"] + 2 * g + 2)
                for n in units_of[g]:
                    kind, _, i = Z[n]
                    if splits_between(n):
                        feed(first["w_in_2"] + 2 * g + 3)
                    if kind == "m":
                        eng.wait_ge(z_act, sum(by_act[:n + 1]))
                        if i == 0:
                            eng.wait_ge(pad_zeroed, 1)
                        if i >= 2:
                            eng.wait_ge(conv_silu, i - 1)
                        acc = conv[:, i % 2, :]
                        tap = lambda j: vec[:, V_CONV + 8 * j + i:V_CONV + 8 * j + i + 1]
                        link(eng.tensor_scalar(acc, raw[:, i % 2, 0:SEQ], tap(0), None, ALU.mult))
                        for j in range(1, CONV):
                            ins = eng.scalar_tensor_tensor(acc, raw[:, i % 2, j:j + SEQ], tap(j), acc, ALU.mult, ALU.add)
                            if j < CONV - 1:
                                link(ins)
                        ins.then_inc(conv_done, 1)
                    if by_act[n]:
                        continue
                    bank = z_bank(n)
                    if kind == "av":
                        dst, src, add = sv[:, i, :], bank[:, 0:256], bias_av
                    elif kind == "if":
                        eng.wait_ge(z_unit, i + 1)
                        dst, src, add = ga[:, i, 0, :], bank[:, 0:16], b_if[:, :]
                    else:
                        lo = (g - 5) % 2 * HALF
                        dst, src = (mv if kind == "mv" else mo)[:, i, lo:lo + HALF], bank
                        add = bias_mvo[:, (g - 5) * HALF:(g - 4) * HALF]
                    eng.tensor_tensor(dst, src, add, ALU.add).then_inc(z_dve, 1)

            for g in range(9):
                feed(first["w_in_2"] + 2 * g)
                if g:
                    take(g - 1)
                if g == 7:
                    take(9)
                feed(first["w_in_2"] + 2 * g + 1)
                if g == 7:
                    G = lambda row, lo: ga[:, :, row, lo:lo + 8]
                    eng.wait_ge(gates_exp, 1)
                    eng.tensor_scalar(G(3, 0), G(2, 8), 1.0, None, ALU.add).then_inc(gates_u, 1)
            take(8)
            eng.wait_ge(gates_u, 1)
            link(eng.tensor_scalar(G(4, 0), G(3, 0), -1.0, None, ALU.add))
            link(eng.tensor_scalar(G(4, 8), G(4, 0), 0.0, None, ALU.is_equal))
            link(eng.tensor_tensor(G(5, 0), G(4, 0), G(4, 8), ALU.add))
            link(eng.reciprocal(G(5, 8), G(5, 0)))
            eng.wait_ge(gates_exp, 2)
            link(eng.tensor_tensor(G(5, 8), G(5, 8), G(3, 8), ALU.mult))
            link(eng.tensor_tensor(G(5, 8), G(5, 8), G(4, 8), ALU.add))
            eng.tensor_scalar(G(6, 0), G(1, 0), SOFTCAP, None, ALU.mult)
            eng.scalar_tensor_tensor(G(6, 8), G(5, 8), -1.0, G(2, 8), ALU.mult, ALU.mult).then_inc(gates_ready, 1)
            eng.wait_ge(conv_silu, 8)
            for t in range(TILES):
                n = P * (t + 1)
                mask = prev_causal[:, SEQ - n:].unsqueeze(1).broadcast_to([P, 2, n])
                for g in range(8):
                    eng.wait_ge(score, 16 + 8 * t + g + 1)
                    b = 2 * (g % 2)
                    eng.tensor_tensor(L[t][:, 2 * g:2 * g + 2, 0:n], PS[:, b:b + 2, 0:n], mask, ALU.add).then_inc(score_used, 1)
                    if g % 4 == 3:
                        mine = slice(2 * g - 6, 2 * g + 2)
                        eng.wait_ge(score_used, 16 + 8 * t + g + 1)
                        link(eng.tensor_reduce(hs[:, t, 0, mine], L[t][:, mine, 0:n], AX_X, ALU.max))
                        link(eng.tensor_tensor(hs[:, t, 0, mine], hs[:, t, 0, mine], sink[:, mine], ALU.max))
                        eng.tensor_scalar(hs[:, t, 1, mine], hs[:, t, 0, mine], -1.0, None, ALU.mult)
                        eng.tensor_tensor(hs[:, t, 3, mine], sink[:, mine], hs[:, t, 0, mine], ALU.subtract).then_inc(maxed, 1)
            for t in range(TILES):
                G = ga[:, t]
                eng.wait_ge(cum_ps, t + 1)
                link(eng.tensor_copy(G[:, 7, 0:8], PS[:, 6 + t, 0:8]))
                eng.tensor_tensor(G[:, 7, 8:16], G[:, 6, 0:8], G[:, 7, 0:8], ALU.subtract).then_inc(a_ready, 1)
            eng.wait_ge(a_ps, 1)
            eng.tensor_copy(aT[:, :], PS[0:8, 5, 0:SEQ]).then_inc(a_copied, 1)


            def attention_weights(t):
                n = P * (t + 1)
                for g in range(2):
                    mine = slice(8 * g, 8 * g + 8)
                    eng.wait_ge(sink_exp, 2 * t + g + 1)
                    link(eng.tensor_tensor(hs[:, t, 5, mine], hs[:, t, 2, mine], hs[:, t, 4, mine], ALU.add))
                    link(eng.reciprocal(hs[:, t, 6, mine], hs[:, t, 5, mine]))
                    x = L[t][:, 8 * g:8 * g + 8, 0:n]
                    eng.tensor_tensor(x, x, wide(hs[:, t, 6, 8 * g:8 * g + 8], n), ALU.mult).then_inc(weighed, 1)

            def attention_rows(t):
                for g in range(2):
                    to = slice(4 * g, 4 * g + 4), slice(t * P, (t + 1) * P)
                    eng.wait_ge(sy_hi, 2 * t + g + 1)
                    eng.tensor_tensor(yT[1][:, to[0], to[1]], PS[:, 2 * t + g, :].rearrange("p (k q) -> p k q", q=P),
                                      yT[0][:, to[0], to[1]], ALU.subtract).then_inc(sy_lo, 1)

            def masked_gates(t):
                n = P * (t + 1)
                mask = zero_causal[:, SEQ - n:].unsqueeze(1).broadcast_to([P, 2, n])
                for j in range(4):
                    eng.wait_ge(ml_a, 4 * t + j + 1)
                    eng.tensor_tensor(ML[t][:, 2 * j:2 * j + 2, 0:n], PS[:, 4 + j, :].rearrange("p (m k) -> p m k", m=2)[:, :, 0:n],
                                      mask, ALU.add).then_inc(ml_used, 1)

            def gate_maxima(t):
                n = P * (t + 1)
                eng.wait_ge(ml_used, 4 * (t + 1))
                link(eng.tensor_reduce(hs[:, t, 0, 0:8], ML[t][:, :, 0:n], AX_X, ALU.max))
                link(eng.tensor_scalar(hs[:, t, 0, 0:8], hs[:, t, 0, 0:8], 0.0, None, ALU.max))
                link(eng.tensor_scalar(hs[:, t, 1, 0:8], hs[:, t, 0, 0:8], -1.0, None, ALU.mult))
                eng.tensor_tensor(hs[:, t, 4, 0:8], ga[:, t, 7, 0:8], hs[:, t, 0, 0:8], ALU.add).then_inc(ml_max, 1)

            attention_weights(0)
            feed(first["w_in_2"] + 18)
            pT_copy((1, 0))
            attention_weights(1)
            pT_copy((1, 1))
            attention_rows(0)
            masked_gates(0)
            gate_maxima(0)
            attention_rows(1)
            masked_gates(1)

            def weighted_scores(t, heads):
                n = P * (t + 1)
                for a in heads:
                    eng.wait_ge(ml_exp, 9 * t + a + 1)
                    eng.wait_ge(ml_s, 4 * t + a // 2 + 1)
                    eng.scalar_tensor_tensor(ML[t][:, a, 0:n], PS[:, 2 * (a // 2 % 2) + a % 2, 0:n], SCALE, ML[t][:, a, 0:n],
                                             ALU.mult, ALU.mult, accum_out=hs[:, t, 2, a:a + 1]).then_inc(ml_sc, 1)

            def mlstm_rows(t):
                eng.wait_ge(ml_exp, 9 * t + 9)
                eng.wait_ge(ml_sc, 8 * (t + 1))
                link(eng.tensor_scalar(hs[:, t, 6, 0:8], hs[:, t, 2, 0:8], -1.0, None, ALU.mult))
                link(eng.tensor_tensor(hs[:, t, 6, 0:8], hs[:, t, 6, 0:8], hs[:, t, 2, 0:8], ALU.max))
                link(eng.tensor_tensor(hs[:, t, 6, 0:8], hs[:, t, 6, 0:8], hs[:, t, 5, 0:8], ALU.max))
                link(eng.reciprocal(hs[:, t, 7, 0:8], hs[:, t, 6, 0:8]))
                for b in range(2):
                    eng.wait_ge(pv, 8 + 2 * t + b + 1)
                    ins = eng.tensor_tensor(tok[:, t, b * HALF:(b + 1) * HALF].rearrange("p (h v) -> p h v", h=4),
                                            PS[:, 2 * t + b, :].rearrange("p (h v) -> p h v", h=4),
                                            wide(hs[:, t, 7, 4 * b:4 * b + 4], P), ALU.mult)
                ins.then_inc(ml_h, 1)

            def normed_rows(t):
                eng.wait_ge(ml_hsq, t + 1)
                link(eng.tensor_reduce(hs[:, t, 3, 0:8], head_squares.rearrange("p (h v) -> p h v", h=8), AX_X, ALU.add))
                rsqrt(hs[:, t, 3, 8:16], hs[:, t, 3, 0:8], V_DIM)
                rows = tok[:, t, :].rearrange("p (h v) -> p h v", h=8)
                link(eng.tensor_tensor(rows, rows, wide(hs[:, t, 3, 8:16], P), ALU.mult))
                eng.wait_ge(gated_gain, t + 1)
                eng.tensor_tensor(tok[:, t, :], tok[:, t, :], mo[:, t, :], ALU.mult).then_inc(mixed, 1)

            weighted_scores(0, range(4))
            gate_maxima(1)
            weighted_scores(0, range(4, MLSTM_HEADS))
            weighted_scores(1, range(MLSTM_HEADS))
            pT_copy((2, 0))
            mlstm_rows(0)
            pT_copy((2, 1))
            normed_rows(0)
            mlstm_rows(1)
            normed_rows(1)

            def add_bias(j):
                if j == 0:
                    eng.wait_ge(bb_loaded, 48)
                lo = j * HALF
                eng.wait_ge(piece_used, first["w_in_2"] + 18 + 2 * j + 2)
                for t in range(TILES):
                    eng.tensor_tensor(gates[:, t, lo:lo + HALF], PS[:, 2 * (j % 2) + t, :], bias_g[:, lo:lo + HALF],
                                      ALU.add).then_inc(g_sig, 1)

            def merge(v, h):
                eng.wait_ge(sig_done, TILES + len(ZG))
                for t in range(TILES):
                    if v == 1 and h == 1 and t == 0:
                        eng.wait_ge(first_tile, 3)
                    else:
                        eng.wait_ge(piece_used, first[("w_proj_attn", "w_proj_mlstm")[v]] + 2 * h + 2)
                    x = tok[:, t, h * HALF:(h + 1) * HALF]
                    lo = v * D + h * HALF
                    g = gates[:, t, lo:lo + HALF]
                    if v == 0:
                        link(eng.tensor_tensor(x, PS[:, 2 * h + t, :], g, ALU.mult))
                    else:
                        link(eng.tensor_tensor(g, PS[:, 4 + 2 * h + t, :], g, ALU.mult))
                        eng.tensor_tensor(x, x, g, ALU.add).then_inc(merged, 1)

            for j in range(4):
                feed(first["w_in_2"] + 18 + 2 * j)
                if j:
                    add_bias(j - 1)
                feed(first["w_in_2"] + 18 + 2 * j + 1)
            p = first["w_proj_attn"]
            feed(p)
            add_bias(3)
            t8_split(T_HM, hT)
            for n in range(1, 9):
                if n == 8:
                    merge(1, 1)
                feed(p + n)
                if n % 2 == 0 and n < 8:
                    merge((n - 2) // 4, (n - 2) // 2 % 2)
            t8_split(T_MG, yT)
            p = first["w_out_2"]
            feed(p + 1)
            feed(p + 2)
            for t in range(TILES):
                add_to_residual("w_out_2", 0, t)
            feed(p + 3)
            norm(NF2, lambda t: add_to_residual("w_out_2", 1, t, 4))
            t8_split(T_F2, hT)
            norm(NFIN, ffn(1))


_OUT = ((1, SEQ, D), "float32")


def kernel(**inputs):
    import concourse.bacc as _bacc
    from concourse.bass_utils import run_bass_kernel_spmd as _run

    nc = _bacc.Bacc("TRN2", target_bir_lowering=False, num_devices=1, dynamic_dma_scratch_size=8192)
    arrays, args = {}, {}
    for name, a in inputs.items():
        a = np.ascontiguousarray(a)
        arrays[f"in_{name}"] = a
        args[name] = nc.dram_tensor(f"in_{name}", a.shape, mybir.dt.from_np(a.dtype), kind="ExternalInput").ap()
    b = distance_buckets()
    arrays["in_buckets"] = b
    buckets = nc.dram_tensor("in_buckets", b.shape, F32, kind="ExternalInput").ap()
    out = nc.dram_tensor("out_0", _OUT[0], F32, kind="ExternalOutput").ap()
    two_blocks(nc, args, buckets, out)
    r = _run(nc, [arrays], core_ids=[0])
    return r.results[0]["out_0"]
```
